# Optimizing a Trainium2 kernel written in Bass

```python
import math
import jax, jax.numpy as jnp
from jax import lax
import numpy as np

D_MODEL = 1024
BATCH = 1
SEQ = 256
DEPTH = 2

GRID_W = 64
CTX_LEN = 256
CONV_WIDTH = 3
D_CONV = 512
N_DIFF_HEADS = 4
DIFF_QK_DIM = 64
DIFF_V_DIM = 128
D_ATTN = N_DIFF_HEADS * DIFF_V_DIM
N_FOURIER_GROUPS = 8
FOURIER_GROUP = D_MODEL // N_FOURIER_GROUPS
D_FF = 4 * D_MODEL
Q_BLOCK = 128
ROPE_BASE = 10000.0
LN_EPS = 1e-6
SUBLN_EPS = 1e-5
DEEPNORM_ALPHA = (2.0 * DEPTH) ** 0.25
DEEPNORM_BETA = (8.0 * DEPTH) ** -0.25
N_EVEN = (DEPTH + 1) // 2
N_ODD = DEPTH // 2
COL_CONV = 3 * D_CONV
COL_Q = N_DIFF_HEADS * 2 * DIFF_QK_DIM
COL_K = N_DIFF_HEADS * 2 * DIFF_QK_DIM
COL_V = D_ATTN
Q0 = COL_CONV
K0 = Q0 + COL_Q
V0 = K0 + COL_K
D_IN = V0 + COL_V


def layer_norm(x):
    xf = x.astype(jnp.float32)
    mu = jnp.mean(xf, axis=-1, keepdims=True)
    var = jnp.mean(jnp.square(xf - mu), axis=-1, keepdims=True)
    return ((xf - mu) * lax.rsqrt(var + LN_EPS)).astype(x.dtype)

def layer_norm_affine(x, g, b):
    xf = x.astype(jnp.float32)
    mu = jnp.mean(xf, axis=-1, keepdims=True)
    var = jnp.mean(jnp.square(xf - mu), axis=-1, keepdims=True)
    y = (xf - mu) * lax.rsqrt(var + LN_EPS) * g.astype(jnp.float32) + b.astype(jnp.float32)
    return y.astype(x.dtype)

def modulation(cond, w, b):
    return jnp.split(jax.nn.silu(cond) @ w + b, 6, axis=-1)

def modulate(h, shift, scale):
    return layer_norm(h) * (1.0 + scale) + shift

def post_norm_residual(h, y, gate, g, b):
    return layer_norm_affine(DEEPNORM_ALPHA * h + gate * y, g, b)

def rope_1d(x, pos):
    half = x.shape[-1] // 2
    inv = ROPE_BASE ** (-jnp.arange(half, dtype=jnp.float32) / half)
    ang = pos.astype(jnp.float32)[:, None] * inv[None, :]
    cos = jnp.cos(ang)[:, None, None, :].astype(x.dtype)
    sin = jnp.sin(ang)[:, None, None, :].astype(x.dtype)
    x1, x2 = x[..., :half], x[..., half:]
    return jnp.concatenate([x1 * cos - x2 * sin, x1 * sin + x2 * cos], axis=-1)

def rope_2d(x, row, col):
    d = x.shape[-1] // 2
    return jnp.concatenate([rope_1d(x[..., :d], row), rope_1d(x[..., d:], col)], axis=-1)

def short_conv(u, w):
    n = u.shape[1]
    pad = CONV_WIDTH // 2
    up = jnp.pad(u, ((0, 0), (pad, pad), (0, 0)))
    return sum(up[:, t:t + n] * w[t] for t in range(CONV_WIDTH))

def conv_mixer(p, w):
    gb, gc, v = jnp.split(p, 3, axis=-1)
    return gb * short_conv(gc * v, w)

def heads_qk(p):
    return p.reshape(p.shape[0], p.shape[1], N_DIFF_HEADS, 2, DIFF_QK_DIM)

def heads_v(p):
    return p.reshape(p.shape[0], p.shape[1], N_DIFF_HEADS, DIFF_V_DIM)

def diff_attend(q, k, v, lam):
    s = jnp.einsum('bqhcd,bkhcd->bhcqk', q, k).astype(jnp.float32) * (DIFF_QK_DIM ** -0.5)
    p = jax.nn.softmax(s, axis=-1)
    pd = (p[:, :, 0] - lam * p[:, :, 1]).astype(v.dtype)
    return jnp.einsum('bhqk,bkhd->bqhd', pd, v)

def diff_attention_blocks(q, k, v, lam):
    b, n = q.shape[0], q.shape[1]
    nb = n // Q_BLOCK
    qb = q.reshape(b, nb, Q_BLOCK, N_DIFF_HEADS, 2, DIFF_QK_DIM).transpose(1, 0, 2, 3, 4, 5)
    out = lax.map(lambda blk: diff_attend(blk, k, v, lam), qb)
    return out.transpose(1, 0, 2, 3, 4).reshape(b, n, N_DIFF_HEADS, DIFF_V_DIM)

def sub_ln(o, g, lam_init):
    of = o.astype(jnp.float32)
    y = of * lax.rsqrt(jnp.mean(of * of, axis=-1, keepdims=True) + SUBLN_EPS)
    y = y * g.astype(jnp.float32) * (1.0 - lam_init)
    return y.reshape(o.shape[0], o.shape[1], D_ATTN).astype(o.dtype)

def fourier_mix(u):
    b, n, _ = u.shape
    ug = u.astype(jnp.float32).reshape(b, n, N_FOURIER_GROUPS, FOURIER_GROUP)
    f = jnp.fft.fft2(ug, axes=(1, 3), norm='ortho').real
    return f.reshape(b, n, D_MODEL).astype(u.dtype)

def sq_relu_mlp(u, w1, w2):
    return jnp.square(jax.nn.relu(u @ w1)) @ w2

def first_inputs(seed: int = 0) -> dict:
    key = jax.random.key(seed)
    ks = jax.random.split(key, 16)
    f32 = jnp.float32

    def nrm(k, shape, s):
        return s * jax.random.normal(k, shape, f32)

    return {
        'x': nrm(ks[0], (BATCH, SEQ, D_MODEL), 1.0),
        'c': nrm(ks[1], (BATCH, D_MODEL), 1.0),
        'ctx': nrm(ks[2], (BATCH, CTX_LEN, D_MODEL), 1.0),
        'c_ctx': nrm(ks[3], (D_MODEL,), 1.0),
        'ada_w': nrm(ks[4], (DEPTH, D_MODEL, 6 * D_MODEL), 0.5 * D_MODEL ** -0.5),
        'ada_b': nrm(ks[5], (DEPTH, 6 * D_MODEL), 0.01),
        'ln_g': 1.0 + nrm(ks[6], (DEPTH, 2, D_MODEL), 0.05),
        'ln_b': nrm(ks[7], (DEPTH, 2, D_MODEL), 0.02),
        'mlp_w1': nrm(ks[8], (DEPTH, D_MODEL, D_FF), D_MODEL ** -0.5),
        'mlp_w2': nrm(ks[9], (DEPTH, D_FF, D_MODEL), DEEPNORM_BETA * D_FF ** -0.5),
        'w_in': nrm(ks[10], (N_EVEN, D_MODEL, D_IN), D_MODEL ** -0.5),
        'conv_w': nrm(ks[11], (N_EVEN, CONV_WIDTH, D_CONV), CONV_WIDTH ** -0.5),
        'lambda_qk': nrm(ks[12], (N_EVEN, 4, DIFF_QK_DIM), 0.1),
        'subln_g': 1.0 + nrm(ks[13], (N_EVEN, DIFF_V_DIM), 0.05),
        'w_out_mix': nrm(ks[14], (N_EVEN, D_CONV + D_ATTN, D_MODEL), DEEPNORM_BETA * (D_CONV + D_ATTN) ** -0.5),
        'w_out_fourier': nrm(ks[15], (N_ODD, D_MODEL, D_MODEL), DEEPNORM_BETA * D_MODEL ** -0.5),
    }

def first_block(x, c, ctx, c_ctx, ada_w, ada_b, ln_g, ln_b, mlp_w1, mlp_w2, w_in, conv_w, lambda_qk, subln_g, w_out_mix, w_out_fourier):
    n = x.shape[1]
    rows = n // GRID_W
    row = jnp.repeat(jnp.arange(rows, dtype=jnp.int32), GRID_W)
    col = jnp.tile(jnp.arange(GRID_W, dtype=jnp.int32), rows)
    last_attn = 2 * ((DEPTH - 1) // 2)
    cond_lat = c[:, None, :]
    cond_ctx = c_ctx[None, None, :]
    h, hc = x, ctx
    for i in range(DEPTH):
        j = i // 2
        update_ctx = i < last_attn
        sh1, sc1, g1, sh2, sc2, g2 = modulation(cond_lat, ada_w[i], ada_b[i])
        u = modulate(h, sh1, sc1)
        if update_ctx or i == last_attn:
            mc = modulation(cond_ctx, ada_w[i], ada_b[i])
            uc = modulate(hc, mc[0], mc[1])
        if i % 2 == 0:
            lam_init = 0.8 - 0.6 * math.exp(-0.3 * i)
            lq = lambda_qk[j].astype(jnp.float32)
            lam = jnp.exp(jnp.sum(lq[0] * lq[1])) - jnp.exp(jnp.sum(lq[2] * lq[3])) + lam_init
            p = u @ w_in[j]
            q = rope_2d(heads_qk(p[..., Q0:K0]), row, col)
            k = rope_2d(heads_qk(p[..., K0:V0]), row, col)
            v = heads_v(p[..., V0:])
            if update_ctx:
                pc = uc @ w_in[j]
                kvc = pc[..., K0:]
            else:
                kvc = uc @ w_in[j][:, K0:]
            kc = heads_qk(kvc[..., :COL_K])
            vc = heads_v(kvc[..., COL_K:])
            k_all = jnp.concatenate([k, kc], axis=1)
            v_all = jnp.concatenate([v, vc], axis=1)
            o = diff_attention_blocks(q, k_all, v_all, lam)
            y = jnp.concatenate([conv_mixer(p[..., :COL_CONV], conv_w[j]), sub_ln(o, subln_g[j], lam_init)], axis=-1) @ w_out_mix[j]
            if update_ctx:
                oc = diff_attend(heads_qk(pc[..., Q0:K0]), kc, vc, lam)
                yc = jnp.concatenate([conv_mixer(pc[..., :COL_CONV], conv_w[j]), sub_ln(oc, subln_g[j], lam_init)], axis=-1) @ w_out_mix[j]
        else:
            y = fourier_mix(u) @ w_out_fourier[j]
            if update_ctx:
                yc = fourier_mix(uc) @ w_out_fourier[j]
        h = post_norm_residual(h, y, g1, ln_g[i, 0], ln_b[i, 0])
        h = post_norm_residual(h, sq_relu_mlp(modulate(h, sh2, sc2), mlp_w1[i], mlp_w2[i]), g2, ln_g[i, 1], ln_b[i, 1])
        if update_ctx:
            hc = post_norm_residual(hc, yc, mc[2], ln_g[i, 0], ln_b[i, 0])
            hc = post_norm_residual(hc, sq_relu_mlp(modulate(hc, mc[3], mc[4]), mlp_w1[i], mlp_w2[i]), mc[5], ln_g[i, 1], ln_b[i, 1])
    return h


N_MIXERS = 2
N_LAYERS_A = (DEPTH + 1) // 2
N_LAYERS_B = DEPTH // 2
FOX_HEADS = 16
FOX_HEAD_DIM = D_MODEL // FOX_HEADS
FOX_IN = 4 * D_MODEL + FOX_HEADS
RET_HEADS = 4
RET_QK_DIM = D_MODEL // RET_HEADS
RET_V_DIM = 2 * D_MODEL // RET_HEADS
RET_CHUNK = 128
RET_IN = 2 * RET_HEADS * RET_QK_DIM + 2 * RET_HEADS * RET_V_DIM
N_GROUPS = 4
EXPERTS_PER_GROUP = 8
N_EXPERTS = N_GROUPS * EXPERTS_PER_GROUP
TOP_K = 2
EXPERT_FF = D_MODEL // 2
MOE_BLOCK = 128

EPS = 1e-6
NEG_INF = -1e30


F32 = jnp.float32

def rms_norm(x, g):
    xf = x.astype(F32)
    y = xf * lax.rsqrt(jnp.mean(xf * xf, axis=-1, keepdims=True) + EPS)
    return (y * g.astype(F32)).astype(x.dtype)

def forgetting_attention(h, w_in, b_f, w_out):
    B, S, _ = h.shape
    H, dh = FOX_HEADS, FOX_HEAD_DIM
    proj = h @ w_in
    q, k, v, gate = jnp.split(proj[..., :4 * D_MODEL], 4, axis=-1)
    f_logit = (proj[..., 4 * D_MODEL:] + b_f).astype(F32)
    cum = jnp.cumsum(jax.nn.log_sigmoid(f_logit), axis=1).transpose(0, 2, 1)
    heads = lambda t: t.reshape(B, S, H, dh).transpose(0, 2, 1, 3)
    q, k, v = heads(q), heads(k), heads(v)
    scale = dh ** -0.5
    k_pos = jnp.arange(S)

    def query_block(i):
        start = i * Q_BLOCK
        q_b = lax.dynamic_slice_in_dim(q, start, Q_BLOCK, axis=2)
        c_b = lax.dynamic_slice_in_dim(cum, start, Q_BLOCK, axis=2)
        s = jnp.einsum('bhqd,bhkd->bhqk', q_b, k).astype(F32) * scale
        s = s + c_b[..., :, None] - cum[..., None, :]
        q_pos = start + jnp.arange(Q_BLOCK)
        s = jnp.where(k_pos[None, :] <= q_pos[:, None], s, NEG_INF)
        p = jax.nn.softmax(s, axis=-1)
        return jnp.einsum('bhqk,bhkd->bhqd', p.astype(v.dtype), v)

    o = lax.map(query_block, jnp.arange(S // Q_BLOCK))
    o = o.transpose(1, 0, 3, 2, 4).reshape(B, S, D_MODEL)
    o = o * jax.nn.sigmoid(gate)
    return o @ w_out

def rotary(t, pos):
    d = t.shape[-1]
    inv = 1.0 / (ROPE_BASE ** jnp.linspace(0.0, 1.0, d // 2, dtype=F32))
    ang = pos.astype(F32)[:, None] * inv[None, :]
    cos, sin = jnp.cos(ang), jnp.sin(ang)
    t1, t2 = t[..., :d // 2].astype(F32), t[..., d // 2:].astype(F32)
    return jnp.concatenate([t1 * cos - t2 * sin, t1 * sin + t2 * cos], axis=-1)

def retention(h, w_in, gn_gain, w_out):
    B, S, _ = h.shape
    H, dk, dv, C = RET_HEADS, RET_QK_DIM, RET_V_DIM, RET_CHUNK
    proj = h @ w_in
    q, k, v, gate = jnp.split(proj, [H * dk, 2 * H * dk, 2 * H * dk + H * dv], axis=-1)
    heads = lambda t, d: t.reshape(B, S, H, d).transpose(0, 2, 1, 3)
    pos = jnp.arange(S)
    q = rotary(heads(q, dk), pos)
    k = rotary(heads(k, dk), pos) * (dk ** -0.5)
    v = heads(v, dv).astype(F32)

    log_g = jnp.log(1.0 - 2.0 ** (-5.0 - jnp.arange(H, dtype=F32)))
    idx = jnp.arange(C, dtype=F32)
    rel = idx[:, None] - idx[None, :]
    intra = jnp.where(rel >= 0, jnp.exp(log_g[:, None, None] * jnp.maximum(rel, 0.0)), 0.0)
    q_decay = jnp.exp(log_g[:, None] * (idx + 1.0))[None, :, :, None]
    k_decay = jnp.exp(log_g[:, None] * (C - 1.0 - idx))[None, :, :, None]
    chunk_decay = jnp.exp(log_g * C)[None, :, None, None]

    n_chunks = S // C
    to_chunks = lambda t: t.reshape(B, H, n_chunks, C, t.shape[-1]).transpose(2, 0, 1, 3, 4)

    def step(R, qkv):
        q_n, k_n, v_n = qkv
        s = jnp.einsum('bhid,bhjd->bhij', q_n, k_n) * intra
        o = jnp.einsum('bhij,bhje->bhie', s, v_n)
        o = o + jnp.einsum('bhid,bhde->bhie', q_n, R) * q_decay
        R = R * chunk_decay + jnp.einsum('bhjd,bhje->bhde', k_n * k_decay, v_n)
        return R, o

    R0 = jnp.zeros((B, H, dk, dv), F32)
    _, o = lax.scan(step, R0, (to_chunks(q), to_chunks(k), to_chunks(v)))
    o = o.transpose(1, 0, 3, 2, 4).reshape(B, S, H, dv)
    mu = jnp.mean(o, axis=-1, keepdims=True)
    var = jnp.mean(jnp.square(o - mu), axis=-1, keepdims=True)
    o = ((o - mu) * lax.rsqrt(var + EPS)).reshape(B, S, H * dv) * gn_gain.astype(F32)
    o = jax.nn.silu(gate.astype(F32)) * o
    return o.astype(h.dtype) @ w_out

def grouped_experts(xf, expert_id, gates, w_gu, w_down):
    T, D = xf.shape
    A = T * TOP_K
    flat_e = expert_id.reshape(A)
    order = jnp.argsort(flat_e)
    sorted_e = flat_e[order]
    counts = jnp.bincount(flat_e, length=N_EXPERTS)
    padded = (counts + MOE_BLOCK - 1) // MOE_BLOCK * MOE_BLOCK
    pad_end = jnp.cumsum(padded)
    pad_start = pad_end - padded
    start = jnp.cumsum(counts) - counts
    dest = pad_start[sorted_e] + jnp.arange(A) - start[sorted_e]
    n_blocks = (A + N_EXPERTS * (MOE_BLOCK - 1) + MOE_BLOCK - 1) // MOE_BLOCK
    n_rows = n_blocks * MOE_BLOCK
    tok_sorted = (order // TOP_K).astype(jnp.int32)
    row_tok = jnp.full((n_rows,), T, jnp.int32).at[dest].set(tok_sorted)
    x_pad = jnp.concatenate([xf, jnp.zeros((1, D), xf.dtype)], axis=0)
    x_rows = x_pad[row_tok].reshape(n_blocks, MOE_BLOCK, D)
    block_e = jnp.minimum(jnp.searchsorted(pad_end, jnp.arange(n_blocks) * MOE_BLOCK, side='right'),
                          N_EXPERTS - 1)

    def expert_block(args):
        xb, e = args
        a, b = jnp.split(xb @ w_gu[e], 2, axis=-1)
        return (jax.nn.silu(a) * b) @ w_down[e]

    y_rows = lax.map(expert_block, (x_rows, block_e)).reshape(n_rows, D)
    w_sorted = gates.reshape(A)[order].astype(y_rows.dtype)
    return jax.ops.segment_sum(y_rows[dest] * w_sorted[:, None], tok_sorted, num_segments=T)

def hier_moe(h, wr_g, br_g, wr_e, br_e, w_gu, w_down):
    B, S, D = h.shape
    T = B * S
    xf = h.reshape(T, D)
    p_group = jax.nn.softmax((xf @ wr_g).astype(F32) + br_g.astype(F32), axis=-1)
    pg, gi = lax.top_k(p_group, 1)
    e_logits = ((xf @ wr_e).astype(F32) + br_e.astype(F32)).reshape(T, N_GROUPS, EXPERTS_PER_GROUP)
    e_in = jnp.einsum('tge,tg->te', e_logits, jax.nn.one_hot(gi[:, 0], N_GROUPS, dtype=F32))
    pv, pi = lax.top_k(jax.nn.softmax(e_in, axis=-1), TOP_K)
    gates = pg * pv / jnp.sum(pv, axis=-1, keepdims=True)
    expert_id = gi * EXPERTS_PER_GROUP + pi
    return grouped_experts(xf, expert_id, gates, w_gu, w_down).reshape(B, S, D)

def second_inputs(seed: int = 0) -> dict:
    key = jax.random.key(seed)
    ks = jax.random.split(key, 17)
    nrm = lambda k, shape, fan_in: jax.random.normal(k, shape, F32) * (fan_in ** -0.5)
    out_scale = (2.0 * DEPTH) ** -0.5
    return {
        "x": jax.random.normal(ks[0], (BATCH, SEQ, D_MODEL), F32),
        "fox_w_in": nrm(ks[1], (N_LAYERS_A, D_MODEL, FOX_IN), D_MODEL),
        "fox_b_f": 3.0 + 0.5 * jax.random.normal(ks[2], (N_LAYERS_A, FOX_HEADS), F32),
        "fox_w_out": nrm(ks[3], (N_LAYERS_A, D_MODEL, D_MODEL), D_MODEL) * out_scale,
        "ret_w_in": nrm(ks[4], (N_LAYERS_B, D_MODEL, RET_IN), D_MODEL),
        "ret_gn_gain": 1.0 + 0.02 * jax.random.normal(ks[5], (N_LAYERS_B, RET_HEADS * RET_V_DIM), F32),
        "ret_w_out": nrm(ks[6], (N_LAYERS_B, RET_HEADS * RET_V_DIM, D_MODEL), RET_HEADS * RET_V_DIM) * out_scale,
        "norm_mix": 1.0 + 0.02 * jax.random.normal(ks[7], (DEPTH, D_MODEL), F32),
        "norm_ffn": 1.0 + 0.02 * jax.random.normal(ks[8], (DEPTH, D_MODEL), F32),
        "router_group_w": nrm(ks[9], (DEPTH, D_MODEL, N_GROUPS), D_MODEL),
        "router_group_b": 0.01 * jax.random.normal(ks[10], (DEPTH, N_GROUPS), F32),
        "router_expert_w": nrm(ks[11], (DEPTH, D_MODEL, N_EXPERTS), D_MODEL),
        "router_expert_b": 0.01 * jax.random.normal(ks[12], (DEPTH, N_EXPERTS), F32),
        "expert_w_gu": nrm(ks[13], (DEPTH, N_EXPERTS, D_MODEL, 2 * EXPERT_FF), D_MODEL),
        "expert_w_down": nrm(ks[14], (DEPTH, N_EXPERTS, EXPERT_FF, D_MODEL), EXPERT_FF) * out_scale,
        "norm_final": 1.0 + 0.02 * jax.random.normal(ks[15], (D_MODEL,), F32),
    }

def second_block(x, fox_w_in, fox_b_f, fox_w_out, ret_w_in, ret_gn_gain, ret_w_out,
              norm_mix, norm_ffn, router_group_w, router_group_b, router_expert_w,
              router_expert_b, expert_w_gu, expert_w_down, norm_final):
    h = x
    for i in range(DEPTH):
        hn = rms_norm(h, norm_mix[i])
        j = i // N_MIXERS
        if i % N_MIXERS == 0:
            h = h + forgetting_attention(hn, fox_w_in[j], fox_b_f[j], fox_w_out[j])
        else:
            h = h + retention(hn, ret_w_in[j], ret_gn_gain[j], ret_w_out[j])
        hn = rms_norm(h, norm_ffn[i])
        h = h + hier_moe(hn, router_group_w[i], router_group_b[i], router_expert_w[i],
                         router_expert_b[i], expert_w_gu[i], expert_w_down[i])
    return rms_norm(h, norm_final)


def setup_inputs(seed=0):
    out = dict(first_inputs(seed))
    for name, value in second_inputs(seed + 1).items():
        if name != "x":
            out[name + "_2"] = value
    return out


def reference(
    x, c, ctx, c_ctx, ada_w, ada_b, ln_g, ln_b, mlp_w1, mlp_w2, w_in, conv_w, lambda_qk,
    subln_g, w_out_mix, w_out_fourier, fox_w_in_2, fox_b_f_2, fox_w_out_2, ret_w_in_2,
    ret_gn_gain_2, ret_w_out_2, norm_mix_2, norm_ffn_2, router_group_w_2, router_group_b_2,
    router_expert_w_2, router_expert_b_2, expert_w_gu_2, expert_w_down_2, norm_final_2,
):
    x = first_block(
        x, c, ctx, c_ctx, ada_w, ada_b, ln_g, ln_b, mlp_w1, mlp_w2, w_in, conv_w, lambda_qk,
        subln_g, w_out_mix, w_out_fourier,
    )
    return second_block(
        x, fox_w_in_2, fox_b_f_2, fox_w_out_2, ret_w_in_2, ret_gn_gain_2, ret_w_out_2,
        norm_mix_2, norm_ffn_2, router_group_w_2, router_group_b_2, router_expert_w_2,
        router_expert_b_2, expert_w_gu_2, expert_w_down_2, norm_final_2,
    )


_drawn_inputs = setup_inputs


def setup_inputs(seed=0):
    import zlib

    import numpy as np

    out = dict(_drawn_inputs(seed))
    spreads = {}
    factors = {'ada_b': 3.352,
     'lambda_qk': 6.393,
     'subln_g': 8.0,
     'ret_gn_gain_2': 5.215,
     'norm_mix_2': 3.089,
     'router_group_b_2': 5.549,
     'router_expert_b_2': 7.617,
     'norm_final_2': 2.88}
    for name, (base, spread) in spreads.items():
        noise = np.random.default_rng([zlib.crc32(name.encode()), seed]).standard_normal(out[name].shape)
        drawn = base * np.exp(spread * noise) if base else spread * noise
        out[name] = __import__('jax').numpy.asarray(drawn.astype(out[name].dtype))
    for name, factor in factors.items():
        out[name] = (out[name] * factor).astype(out[name].dtype)
    return out
```

```python
import math
from contextlib import ExitStack

import numpy as np

import concourse.bass as bass
from concourse import mybir

P = 128
D = 1024
KT = D // P
SEQ = 256
TT = SEQ // P
GRID_W = 64
DEPTH = 2
D_CONV = 512
N_DIFF = 4
DIFF_QK = 64
FF = 4 * D
FOX_HEADS = 16
FOX_DIM = D // FOX_HEADS
RET_HEADS = 4
RET_V_TILES = 4
E = 32
GROUPS = 4
EPG = E // GROUPS
EXPERT_FF = 512
SLOTS = 64
PAIRS = E // 2
OVER = 7
ROWS = E * SLOTS + OVER * SLOTS
ALPHA = (2.0 * DEPTH) ** 0.25
LN_EPS, SUBLN_EPS = 1e-6, 1e-5
LAM_INIT = 0.8 - 0.6 * math.exp(-0.3 * 0)
CHUNK = 256
RING = 4
BANKS = 8
SH1, SC1, G1, SH2, SC2, G2 = (KT * i for i in range(6))

CONSTS = {}
_at = 0
for _name, _n in [("ident", P), ("ones", P), ("mean_d", P), ("mean_v", P), ("mean_gn", P), ("swap", P),
                  ("causal", P), ("before", P), ("iota", P), ("eps", 2), ("rope_cos", SEQ), ("rope_sin", SEQ),
                  ("ret_cos", SEQ), ("ret_sin", SEQ)]:
    CONSTS[_name] = (_at, _n)
    _at += _n
N_CONST = _at
N_DFT = 2 * P + 4 * SEQ
N_DECAY = RET_HEADS * (SEQ + P)

VEC1 = {"c": 0, "c_ctx": 8, "ada_b": 16, "gn": 112}
VEC2 = {"ln_g": 0, "ln_b": 32, "mix": 64, "ffn": 80, "final": 96, "subln": 104, "conv": 105}
N_VEC2 = 117
ROW_ROUTER = 256
N_ROW = 256 + DEPTH * (GROUPS + E)
NR = GROUPS + E

TILES = {}
_at = 0
for _name, _n in ([("vecs", 2), ("x", 4), ("ctx", 4), ("ada", 12), ("u", 2), ("uc", 2), ("w_in", 32), ("rope", 8),
                   ("attn", 32), ("mix", 8), ("post1_0", 2), ("mod2_0", 2), ("w1_0", 32), ("w2_0", 8),
                   ("post2_0", 2), ("mod1_1", 2), ("dft_in", 8), ("dft_out", 8), ("fourier", 8), ("post1_1", 2),
                   ("mod2_1", 2), ("w1_1", 32), ("w2_1", 8), ("post2_1", 2),
                   ("fox_norm", 1), ("forget", 1), ("fox_in", 32), ("fox_attn", 40), ("fox_out", 8),
                   ("moe_norm_0", 1), ("router_0", 2), ("hn_0", 4), ("combine_0", 4),
                   ("ret_norm", 1), ("ret_in", 48), ("ret_scores", 4), ("ret_pv", 8), ("gn_mean", 4), ("gn_var", 4),
                   ("ret_out", 8), ("moe_norm_1", 1), ("router_1", 2), ("hn_1", 4), ("combine_1", 4),
                   ("final_norm", 1), ("final", 4)]):
    TILES[_name] = _at
    _at += _n


def build(nc, A, out):
    f32, i32, u32 = mybir.dt.float32, mybir.dt.int32, mybir.dt.uint32
    ALU, ACT, AX = mybir.AluOpType, mybir.ActivationFunctionType, mybir.AxisListType
    ds = bass.ds
    expert_rows = nc.dram_tensor("expert_rows", (ROWS, D), f32, kind="Internal").ap()

    with ExitStack() as ctx:
        def sb(name, shape, dt=f32):
            return ctx.enter_context(nc.sbuf_tensor(name, shape, dt))[tuple(slice(None) for _ in shape)]

        sems = {}

        def S(name):
            if name not in sems:
                sems[name] = ctx.enter_context(nc.semaphore(name))
            return sems[name]

        dense_w = sb("dense_w", [P, RING, KT, CHUNK])
        expert_w = sb("expert_w", [P, 6, KT * 512])
        h = sb("h", [P, KT, SEQ])
        u = sb("u", [P, KT, SEQ])
        work = sb("work", [P, 11776])
        const = sb("const", [P, N_CONST])
        vec = sb("vec", [P, P + N_VEC2])
        mod = sb("mod", [P, DEPTH, 6 * KT, 2])
        cond = sb("cond", [P, KT, 2])
        rowbc = sb("rowbc", [P, N_ROW])
        rows_in = sb("rows_in", [1, N_ROW])
        router_w = sb("router_w", [P, DEPTH, KT, NR])
        forget_w = sb("forget_w", [P, KT, FOX_HEADS])
        forget_b = sb("forget_b", [FOX_HEADS, 1])
        small = sb("small", [P, 136])
        ps = [ctx.enter_context(nc.psum_tensor(f"bank{b}", [P, 512], f32)) for b in range(BANKS)]

        ew = expert_w[:, :, :].rearrange("p s n -> p (s n)")

        def K(name, n=None):
            at, w = CONSTS[name]
            return const[:, at:at + (n or w)]

        def part(t, at, *shape):
            n = int(np.prod(shape))
            v = t[:, at:at + n]
            if len(shape) == 2:
                return v.rearrange("p (a b) -> p a b", a=shape[0])
            if len(shape) == 3:
                return v.rearrange("p (a b c) -> p a b c", a=shape[0], b=shape[1])
            return v

        wk = work[:, :]
        resid = part(wk, 0, KT, SEQ)
        centered = part(wk, 2048, KT, SEQ)
        squares = part(wk, 4096, KT, SEQ)
        pd = part(wk, 6144, TT, 512)
        rstd = part(wk, 7168, SEQ)
        sq_o = part(wk, 7424, SEQ)
        rope_a = part(wk, 7680, SEQ)
        rope_b = part(wk, 7936, SEQ)
        dft = part(wk, 8192, N_DFT)
        vrow1 = part(wk, 9728, P)
        vrow2 = part(wk, 9856, P)
        x_tok = part(ew, 0, TT, D)
        ctx_tok = part(ew, 2048, TT, D)
        ctxT = part(ew, 4096, KT, SEQ)
        uc = part(ew, 6144, KT, SEQ)
        proj = part(ew, 8192, 16, SEQ)
        kraw = part(ew, 12288, 4, SEQ)
        qrot = part(ew, 13312, 4, SEQ)
        kall = part(ew, 14336, 4, 512)
        v_all = part(ew, 16384, 4, 512)
        cat = part(ew, 18432, KT, SEQ)
        pdT = part(ew, 20480, 2, 4, SEQ)
        expd = part(ew, 22528, 2, 2, 512)
        hidden = part(ew, 16384, 32, SEQ)
        dft_mid = part(ew, 0, KT, TT, 256)
        spectrum = part(ew, 4096, KT, SEQ)
        fq = part(ew, 16384, 16, SEQ)
        fv = part(ew, 20480, TT, D)
        fgate = part(ew, 22528, KT, SEQ)
        fexp = part(wk, 6144, 2, 384)
        fpT = part(wk, 6912, 2, 384)
        cum = part(wk, 8192, SEQ)[0:FOX_HEADS, :]
        ncum = part(wk, 8448, SEQ)[0:FOX_HEADS, :]
        flog = part(wk, 8704, 4, SEQ)[0:FOX_HEADS]
        hn_tok = part(wk, 0, TT, D)
        xg = part(wk, 2048, KT, P)
        act_h = part(wk, 3072, 2, 4 * SLOTS)
        sil = part(wk, 3584, 2, 4 * SLOTS)
        y_sb = part(wk, 4096, D)
        pick = part(wk, 5120, TT, P)
        pick_tmp = part(wk, 5376, TT, P)
        y_back = part(wk, 5632, 2 * TT, D)
        comb = part(wk, 9728, TT, D)
        rgate = part(wk, 0, 16, SEQ)
        ro = part(wk, 4096, 16, SEQ)
        rraw = ro
        rtmp = part(wk, 8192, 8, SEQ)
        r_s = part(wk, 8192, RET_HEADS, 384)
        decay = part(wk, 10240, RET_HEADS, 384)
        gn_rstd = part(wk, 10240, RET_HEADS, SEQ)
        rv = part(ew, 16384, TT, 2048)
        rqk = part(ew, 20480, 16, SEQ)
        lg = sb("lg", [P, TT, NR])
        pad8 = sb("pad8", [P, TT, 8])
        top = sb("top", [P, 4, 8])
        topi = sb("topi", [P, 4, 8], u32)
        e_in = sb("e_in", [P, TT, 8])
        pick_e = part(wk, 5632, 3, TT, E)
        pos = part(wk, 5824, TT, E)
        e_sum = part(wk, 5888, 4, E)
        rt = sb("rt", [P, 40])
        rel = sb("rel", [P, 2, TT])
        row_i = sb("row_i", [P, 2, TT], u32)
        over_f = sb("over_f", [P, 8])
        over_i = sb("over_i", [P, 8], i32)
        zrow = sb("zrow", [P, E])
        onehot_g = sb("onehot_g", [P, TT, GROUPS])

        tile_ready = S("tile_ready")
        evacuated = [S(f"evacuated_{b}") for b in range(BANKS)]
        dense_in = [S(f"dense_in_{j}") for j in range(RING)]
        expert_in = [S(f"expert_in_{j}") for j in range(6)]
        expert_used = S("expert_used")
        kgroup_used = S("kgroup_used")

        def bank(t):
            return ps[t % BANKS]

        def wait_tile(eng, t):
            eng.wait_ge(tile_ready, t + 1)

        def wait_evac(eng, t):
            eng.wait_ge(evacuated[t % BANKS], t // BANKS + 1)

        def open_bank(pe, t, i=0):
            if t >= BANKS:
                pe.wait_ge(evacuated[t % BANKS], t // BANKS + i)

        def evac(ins, t):
            return ins.then_inc(evacuated[t % BANKS], 1)

        DENSE = []
        n_rot = 0
        kg = 0
        for name, w, rot, wide, tile in [
                ("ada0", A["ada_w"][0], 6, 0, ("ada", 0)), ("ada1", A["ada_w"][1], 6, 0, ("ada", 6)),
                ("w_in", A["w_in"][0], 3, 0, "w_in"), ("mix", A["w_out_mix"][0], 1, 0, "mix"),
                ("w1_0", A["mlp_w1"][0], 4, 0, "w1_0"), ("w2_0", A["mlp_w2"][0], 4, 1, "w2_0"),
                ("fourier", A["w_out_fourier"][0], 1, 0, "fourier"),
                ("w1_1", A["mlp_w1"][1], 4, 0, "w1_1"), ("w2_1", A["mlp_w2"][1], 4, 1, "w2_1"),
                ("fox_in", A["fox_w_in_2"][0], 4, 0, "fox_in"), ("fox_out", A["fox_w_out_2"][0], 1, 0, "fox_out"),
                ("ret_in", A["ret_w_in_2"][0], 6, 0, "ret_in"), ("ret_out", A["ret_w_out_2"][0], 2, 1, "ret_out")]:
            DENSE.append(dict(name=name, w=w, rot=rot, wide=wide, tile=tile, rot0=n_rot, kg0=kg))
            n_rot += rot
            kg += 4 * (rot - 1) * wide
        DN = {m["name"]: m for m in DENSE}

        def wait_release(sp, m, i, j):
            last = isinstance(i, int) and i == m["rot"] - 1
            if m["wide"] and not last:
                sp.wait_ge(kgroup_used, m["kg0"] + 4 * i + j + 1)
            elif m["wide"]:
                sp.wait_ge(tile_ready, TILES[m["tile"]] + 2 * j + 2)
            elif isinstance(m["tile"], tuple):
                sp.wait_ge(tile_ready, TILES[m["tile"][0]] + m["tile"][1] + i + 1)
            elif m["name"] == "w_in" and last:
                sp.wait_ge(tile_ready, TILES["w_in"] + 16 + 4 * j + 4)
            else:
                sp.wait_ge(tile_ready, TILES[m["tile"]] + 8 * i + 2 * j + 2)

        def wait_chunk(pe, m, i, j):
            pe.wait_ge(dense_in[j], 16 * (m["rot0"] + i + 1))

        block = ctx.enter_context(nc.Block())

        @block.sync
        def _(sp):
            def load_chunk(m, i, j):
                w = m["w"]
                if m["wide"]:
                    src = w[ds(i * D, D), j * CHUNK:(j + 1) * CHUNK]
                else:
                    src = w[:, ds(i * RING * CHUNK + j * CHUNK, CHUNK)]
                sp.dma_start(dense_w[:, j], src.rearrange("(k p) n -> p k n", p=P)).then_inc(dense_in[j], 16)

            def first_rotation(n):
                for j in range(RING):
                    if n:
                        wait_release(sp, DENSE[n - 1], DENSE[n - 1]["rot"] - 1, j)
                    load_chunk(DENSE[n], 0, j)

            def other_rotations(n):
                m = DENSE[n]
                if m["rot"] > 1:
                    with sp.Fori(1, m["rot"]) as i:
                        for j in range(RING):
                            wait_release(sp, m, i - 1, j)
                            load_chunk(m, i, j)

            def load_expert(l, e, half, slot, sem=None):
                if half < 2:
                    src = A["expert_w_gu_2"][l, ds(e, 1), :, half * 512:(half + 1) * 512].rearrange(
                        "a (k p) n -> p (a k) n", p=P)
                    dst = expert_w[:, slot].rearrange("p (k n) -> p k n", k=KT)
                else:
                    src = A["expert_w_down_2"][l, ds(e, 1), :, :].rearrange("a (k p) n -> p (a k) n", p=P)
                    dst = expert_w[:, slot].rearrange("p (k n) -> p k n", k=4)
                sp.dma_start(dst, src).then_inc(sem or expert_in[slot], 16)

            SLOT = [(0, 0), (0, 1), (1, 0), (1, 1), (0, 2), (1, 2)]

            sp.dma_start(const[:, :], A["consts"]).then_inc(S("in_const"), 16)
            sp.dma_start(x_tok, A["x"][0].rearrange("(t p) d -> p t d", p=P)).then_inc(S("in_x"), 16)
            sp.dma_start(ctx_tok, A["ctx"][0].rearrange("(t p) d -> p t d", p=P)).then_inc(S("in_ctx"), 16)
            n_of = {m["name"]: n for n, m in enumerate(DENSE)}
            for name in ("ada0", "ada1", "w_in", "mix", "w1_0", "w2_0", "fourier", "w1_1", "w2_1"):
                first_rotation(n_of[name])
                other_rotations(n_of[name])
            wait_evac(sp, TILES["fourier"] + 7)
            for slot in range(4):
                load_expert(0, SLOT[slot][0], SLOT[slot][1], slot)
            for name in ("fox_in", "fox_out"):
                first_rotation(n_of[name])
                other_rotations(n_of[name])
            first_rotation(n_of["ret_in"])
            for l in range(DEPTH):
                wait_tile(sp, TILES["fox_out"] + 7 if l == 0 else TILES["gn_var"] + 3)
                for slot in (4, 5):
                    load_expert(l, SLOT[slot][0], SLOT[slot][1], slot)
                with sp.Fori(1, PAIRS) as i:
                    for slot in range(6):
                        sp.wait_ge(expert_used, 6 * PAIRS * l + 6 * (i - 1) + slot + 1)
                        load_expert(l, 2 * i + SLOT[slot][0], SLOT[slot][1], slot)
                sp.wait_ge(S(f"over_ready_{l}"), 1)
                n_over = sp.value_load(over_i[0:1, 7:8], min_val=0, max_val=OVER)
                sp.wait_ge(expert_used, 6 * PAIRS * (l + 1))
                with sp.Fori(0, OVER) as b:
                    with sp.If(b < n_over):
                        e = sp.value_load(over_i[0:1, ds(b, 1)], min_val=0, max_val=E - 1)
                        sp.wait_ge(S(f"over_used_{l}"), b + 1)
                        for half, slot in ((0, 0), (1, 1), (2, 4)):
                            load_expert(l, e, half, slot, S(f"over_in_{l}_{half}"))
                sp.wait_ge(S("experts_done"), l + 1)
                if l == 0:
                    for slot in range(4):
                        load_expert(1, SLOT[slot][0], SLOT[slot][1], slot)
                    wait_evac(sp, TILES["combine_0"] + 3)
                    sp.dma_start(decay, A["decay"].rearrange("p (a b) -> p a b", a=RET_HEADS)).then_inc(S("in_decay"), 16)
                    other_rotations(n_of["ret_in"])
                    first_rotation(n_of["ret_out"])
                    other_rotations(n_of["ret_out"])
            for t in range(TT):
                sp.wait_ge(S("out_act"), t + 1)
                sp.wait_ge(S("out_dve"), t + 1)
                sp.dma_start(out[0, t * P:(t + 1) * P, :], comb[:, t]).then_inc(S("out_stored"), 16)
            sp.wait_ge(S("out_stored"), 16 * TT)

        @block.tensor
        def _(pe):
            mm = nc.tensor.matmul
            ident = K("ident")

            def linear(name, tile, rot, rhs, at=0, hook=None, dyn=None):
                m = DN[name]

                def rotation(i):
                    for j in range(RING):
                        wait_chunk(pe, m, at + i, j)
                        for n in range(2):
                            t = tile + 2 * j + n
                            open_bank(pe, t, i)
                            for k in range(KT):
                                if hook is not None:
                                    hook(j, n, k)
                                last = mm(bank(t)[:, 0:SEQ], dense_w[:, j, k, n * P:(n + 1) * P], rhs[:, k, :],
                                          start=k == 0, stop=k == KT - 1)
                            last.then_inc(tile_ready, 1)
                if rot == 1:
                    rotation(0)
                else:
                    if hook is not None:
                        rotation(0)
                        hook = None
                        with pe.Fori(1, rot) as i:
                            rotation(i)
                    else:
                        with pe.Fori(0, rot) as i:
                            rotation(i)

            def token_major(name, tile, rot, at, lhs, tts):
                m = DN[name]

                def rotation(i):
                    for j in range(RING):
                        wait_chunk(pe, m, at + i, j)
                        for tt in range(tts):
                            t = tile + j * tts + tt
                            open_bank(pe, t, i)
                            for k in range(KT):
                                last = mm(bank(t)[:, 0:CHUNK], lhs[:, k, tt * P:(tt + 1) * P], dense_w[:, j, k, :],
                                          start=k == 0, stop=k == KT - 1)
                            last.then_inc(tile_ready, 1)
                if rot == 1:
                    rotation(0)
                else:
                    with pe.Fori(0, rot) as i:
                        rotation(i)

            def wide(name, tile, rhs, groups, ready):
                m = DN[name]

                def group(g, start, stop):
                    for j in range(RING):
                        wait_chunk(pe, m, g, j)
                        for n in range(2):
                            t = tile + 2 * j + n
                            if start:
                                open_bank(pe, t)
                            for k in range(KT):
                                at = g * KT + k
                                rh = rhs[:, at, :] if isinstance(at, int) else rhs[:, ds(at, 1), :].rearrange("p a n -> p (a n)")
                                last = mm(bank(t)[:, 0:SEQ], dense_w[:, j, k, n * P:(n + 1) * P],
                                          rh, start=start and k == 0, stop=stop and k == KT - 1)
                            if stop:
                                last.then_inc(tile_ready, 1)
                        if not stop:
                            last.then_inc(kgroup_used, 1)
                ready(0)
                group(0, True, False)
                if groups > 2:
                    with pe.Fori(1, groups - 1) as g:
                        ready(g)
                        group(g, False, False)
                ready(groups - 1)
                group(groups - 1, False, True)

            def stat(t, weights, src, tiles, ready):
                open_bank(pe, t)
                for k in range(tiles):
                    ready(k)
                    last = mm(bank(t)[:, 0:SEQ], weights, src[:, k, :], start=k == 0, stop=k == tiles - 1)
                last.then_inc(tile_ready, 1)

            def squares_ready(name):
                def ready(k):
                    if k % 4 == 0:
                        pe.wait_ge(S(f"{name}_squares"), k // 4 + 1)
                return ready

            def layer_norm(name, src, ready):
                t = TILES[name]
                stat(t, K("mean_d"), src, KT, ready)
                stat(t + 1, K("mean_d"), squares, KT, squares_ready(name))

            def rms_norm(name):
                stat(TILES[name], K("mean_d"), squares, KT, squares_ready(name))

            def normed(name):
                def hook(j, n, k):
                    if j == 0 and n == 0:
                        pe.wait_ge(S(f"{name}_out"), k + 1)
                return hook

            pe.wait_ge(S("in_const"), 16)
            pe.wait_ge(S("in_small"), 16 * 3)
            t = TILES["vecs"]
            nc.tensor.transpose(bank(t)[:, 0:P], vrow1, ident)
            nc.tensor.transpose(bank(t)[:, P:P + N_VEC2], vrow2[0:N_VEC2, :], ident[0:N_VEC2, 0:N_VEC2]).then_inc(tile_ready, 1)
            mm(bank(t + 1)[:, 0:N_ROW], K("ones")[0:1, :], rows_in[0:1, :], start=True, stop=True).then_inc(tile_ready, 1)
            for src, name in ((x_tok, "x"), (ctx_tok, "ctx")):
                pe.wait_ge(S(f"in_{name}"), 16)
                for q in range(4):
                    t = TILES[name] + q
                    open_bank(pe, t)
                    for k in range(2):
                        for tt in range(TT):
                            last = nc.tensor.transpose(bank(t)[:, k * SEQ + tt * P:k * SEQ + (tt + 1) * P],
                                                       src[:, tt, (2 * q + k) * P:(2 * q + k + 1) * P], ident)
                    last.then_inc(tile_ready, 1)
            pe.wait_ge(S("cond_ready"), 1)
            for l in range(DEPTH):
                m = DN[f"ada{l}"]
                for i in range(6):
                    t = TILES["ada"] + 6 * l + i
                    open_bank(pe, t)
                    for j in range(RING):
                        wait_chunk(pe, m, i, j)
                        for n in range(2):
                            c0 = 2 * (2 * j + n)
                            for k in range(KT):
                                last = mm(bank(t)[:, c0:c0 + 2], dense_w[:, j, k, n * P:(n + 1) * P], cond[:, k, :],
                                          start=k == 0, stop=k == KT - 1)
                    last.then_inc(tile_ready, 1)

            def x_ready(name):
                def ready(k):
                    if k % 2 == 0:
                        wait_evac(pe, TILES[name] + k // 2)
                return ready
            layer_norm("u", h, x_ready("x"))
            layer_norm("uc", ctxT, x_ready("ctx"))
            W = TILES["w_in"]
            linear("w_in", W, 2, u, hook=normed("u"))
            m = DN["w_in"]
            pe.wait_ge(S("uc_out"), KT)
            for j in range(2):
                wait_chunk(pe, m, 2, j)
                for n in range(2):
                    for s, src in enumerate((u, uc)):
                        t = W + 16 + 4 * j + 2 * n + s
                        open_bank(pe, t)
                        for k in range(KT):
                            last = mm(bank(t)[:, 0:SEQ], dense_w[:, j, k, n * P:(n + 1) * P], src[:, k, :],
                                      start=k == 0, stop=k == KT - 1)
                        last.then_inc(tile_ready, 1)
            for j in (2, 3):
                wait_chunk(pe, m, 2, j)
                for tt in range(4):
                    t = W + 24 + 4 * (j - 2) + tt
                    open_bank(pe, t)
                    src = (u, uc)[tt // 2]
                    for k in range(KT):
                        last = mm(bank(t)[:, 0:CHUNK], src[:, k, (tt % 2) * P:(tt % 2 + 1) * P], dense_w[:, j, k, :],
                                  start=k == 0, stop=k == KT - 1)
                    last.then_inc(tile_ready, 1)
            for n in range(8):
                t = TILES["rope"] + n
                if n < 4:
                    wait_evac(pe, W + 12 + n)
                else:
                    wait_evac(pe, W + 16 + 2 * (n - 4))
                open_bank(pe, t)
                src = proj[:, 12 + n, :] if n < 4 else kraw[:, n - 4, :]
                mm(bank(t)[:, 0:SEQ], K("swap"), src, start=True, stop=True).then_inc(tile_ready, 1)
            for n in range(8):
                wait_evac(pe, W + 24 + n)
            T0 = TILES["attn"]
            for step in range(N_DIFF + 1):
                if step < N_DIFF:
                    pe.wait_ge(S("rope_out"), step + 1)
                    pe.wait_ge(S("rope_out"), N_DIFF + step + 1)
                    for qt in range(TT):
                        for c in range(2):
                            t = T0 + diff_tile(step, 2 * qt + c)
                            open_bank(pe, t)
                            lo = c * DIFF_QK
                            mm(bank(t)[:, :], qrot[lo:lo + DIFF_QK, step, qt * P:(qt + 1) * P],
                               kall[lo:lo + DIFF_QK, step, :], start=True, stop=True).then_inc(tile_ready, 1)
                if step >= 1:
                    g = step - 1
                    for qt in range(TT):
                        t = T0 + diff_tile(g, 4 + qt)
                        pe.wait_ge(S("pd_ready"), 2 * g + qt + 1)
                        open_bank(pe, t)
                        for kt in range(4):
                            last = nc.tensor.transpose(bank(t)[:, kt * P:(kt + 1) * P], pd[:, qt, kt * P:(kt + 1) * P], ident)
                        last.then_inc(tile_ready, 1)
                    t = T0 + diff_tile(g, 6)
                    for qt in range(TT):
                        wait_evac(pe, T0 + diff_tile(g, 4 + qt))
                    open_bank(pe, t)
                    for kt in range(4):
                        last = mm(bank(t)[:, 0:SEQ], v_all[:, kt, g * P:(g + 1) * P], pdT[:, g % 2, kt, :],
                                  start=kt == 0, stop=kt == 3)
                    last.then_inc(tile_ready, 1)
                    t = T0 + diff_tile(g, 7)
                    pe.wait_ge(S("sub_squares"), g + 1)
                    open_bank(pe, t)
                    mm(bank(t)[:, 0:SEQ], K("mean_v"), sq_o, start=True, stop=True).then_inc(tile_ready, 1)
            pe.wait_ge(S("conv_out"), 4)
            for g in range(N_DIFF):
                wait_evac(pe, T0 + diff_tile(g, 6))
            linear("mix", TILES["mix"], 1, cat)

            def mlp(l):
                layer_norm(f"post1_{l}", resid, lambda k: wait_evac(pe, TILES["mix" if l == 0 else "fourier"] + k))
                layer_norm(f"mod2_{l}", h, lambda k: pe.wait_ge(S(f"post1_{l}_out"), k + 1))
                linear(f"w1_{l}", TILES[f"w1_{l}"], 4, u, hook=normed(f"mod2_{l}"))
                wide(f"w2_{l}", TILES[f"w2_{l}"], hidden, 4,
                     lambda g: pe.wait_ge(S("hidden_ready"), 32 * l + 8 * g + 8))
                layer_norm(f"post2_{l}", resid, lambda k: wait_evac(pe, TILES[f"w2_{l}"] + k))

            mlp(0)
            layer_norm("mod1_1", h, lambda k: pe.wait_ge(S("post2_0_out"), k + 1))
            pe.wait_ge(S("in_dft"), 16)
            for g in range(KT):
                t = TILES["dft_in"] + g
                pe.wait_ge(S("mod1_1_out"), g + 1)
                open_bank(pe, t)
                for tt in range(TT):
                    last = mm(bank(t)[:, tt * 256:(tt + 1) * 256], u[:, g, tt * P:(tt + 1) * P], dft[:, 0:2 * P],
                              start=True, stop=True)
                last.then_inc(tile_ready, 1)
            for g in range(KT):
                t = TILES["dft_out"] + g
                wait_evac(pe, TILES["dft_in"] + g)
                open_bank(pe, t)
                for tt in range(TT):
                    for cs in range(2):
                        at = 2 * P + (2 * cs + tt) * SEQ
                        last = mm(bank(t)[:, 0:SEQ], dft_mid[:, g, tt, cs * P:(cs + 1) * P], dft[:, at:at + SEQ],
                                  start=tt == 0 and cs == 0, stop=tt == 1 and cs == 1)
                last.then_inc(tile_ready, 1)
            linear("fourier", TILES["fourier"], 1, spectrum,
                   hook=lambda j, n, k: wait_evac(pe, TILES["dft_out"] + k) if j == 0 and n == 0 else None)
            mlp(1)

            rms_norm("fox_norm")
            t = TILES["forget"]
            open_bank(pe, t)
            pe.wait_ge(S("in_forget"), 32)
            for k in range(KT):
                pe.wait_ge(S("fox_norm_out"), k + 1)
                last = mm(bank(t)[0:FOX_HEADS, 0:SEQ], forget_w[:, k, :], u[:, k, :], start=k == 0, stop=k == KT - 1)
            last.then_inc(tile_ready, 1)
            F = TILES["fox_in"]
            linear("fox_in", F, 2, u)
            token_major("fox_in", F + 16, 1, 2, u, TT)
            linear("fox_in", F + 24, 1, u, at=3)
            T1 = TILES["fox_attn"]
            pe.wait_ge(S("cum_ready"), 2)
            for n in range(16):
                wait_evac(pe, F + n)
            for n in range(8):
                wait_evac(pe, F + 16 + n)
            for step in range(FOX_HEADS // 2 + 1):
                if step < FOX_HEADS // 2:
                    for a in range(2):
                        hd = 2 * step + a
                        t = T1 + fox_tile(step, a)
                        open_bank(pe, t)
                        lo = a * FOX_DIM
                        one = ident[0:FOX_HEADS, hd:hd + 1]
                        for qt, (c0, nk) in enumerate(((0, P), (P, SEQ))):
                            o = bank(t)[:, c0:c0 + nk]
                            q0 = qt * P
                            mm(o, fq[lo:lo + FOX_DIM, step, q0:q0 + P], fq[lo:lo + FOX_DIM, 8 + step, 0:nk],
                               start=True, stop=False)
                            mm(o, cum[:, q0:q0 + P], one.broadcast_to([FOX_HEADS, nk]), start=False, stop=False)
                            mm(o, one.broadcast_to([FOX_HEADS, P]), ncum[:, 0:nk], start=False, stop=False)
                            last = mm(bank(t)[:, c0 + nk - P:c0 + nk], ident, K("causal"), start=False, stop=True)
                        last.then_inc(tile_ready, 1)
                if step >= 1:
                    g = step - 1
                    for a in range(2):
                        t = T1 + fox_tile(g, 2 + a)
                        pe.wait_ge(S("fox_probs"), 2 * g + a + 1)
                        open_bank(pe, t)
                        for n in range(3):
                            last = nc.tensor.transpose(bank(t)[:, n * P:(n + 1) * P], fexp[:, a, n * P:(n + 1) * P], ident)
                        last.then_inc(tile_ready, 1)
                    t = T1 + fox_tile(g, 4)
                    open_bank(pe, t)
                    for a in range(2):
                        wait_evac(pe, T1 + fox_tile(g, 2 + a))
                        lo = a * FOX_DIM
                        c0 = (2 * g + a) * FOX_DIM
                        mm(bank(t)[lo:lo + FOX_DIM, 0:SEQ], fv[:, 0, c0:c0 + FOX_DIM], fpT[:, a, 0:SEQ],
                           start=True, stop=False)
                        last = mm(bank(t)[lo:lo + FOX_DIM, P:SEQ], fv[:, 1, c0:c0 + FOX_DIM], fpT[:, a, SEQ:SEQ + P],
                                  start=False, stop=True)
                    last.then_inc(tile_ready, 1)
            linear("fox_out", TILES["fox_out"], 1, fgate,
                   hook=lambda j, n, k: wait_evac(pe, T1 + fox_tile(k, 4)) if j == 0 and n == 0 else None)

            def experts(l):
                rms_norm(f"moe_norm_{l}")
                t = TILES[f"router_{l}"]
                open_bank(pe, t)
                pe.wait_ge(S("in_router"), 16 * DEPTH)
                pe.wait_ge(S(f"moe_norm_{l}_out"), KT)
                for tt in range(TT):
                    for k in range(KT):
                        last = mm(bank(t)[:, tt * NR:(tt + 1) * NR], u[:, k, tt * P:(tt + 1) * P], router_w[:, l, k, :],
                                  start=k == 0, stop=k == KT - 1)
                last.then_inc(tile_ready, 1)
                for q in range(4):
                    t = TILES[f"hn_{l}"] + q
                    open_bank(pe, t)
                    for n in range(4):
                        k = (q % 2) * 4 + n
                        last = nc.tensor.transpose(bank(t)[:, n * P:(n + 1) * P],
                                                   u[:, k, (q // 2) * P:(q // 2 + 1) * P], ident)
                    last.then_inc(tile_ready, 1)
                t = TILES[f"router_{l}"] + 1
                open_bank(pe, t)
                pe.wait_ge(S("choices"), l + 1)
                mm(bank(t)[:, 0:E], K("before"), pick_e[:, 2, 0, :], start=True, stop=True)
                mm(bank(t)[:, E:2 * E], K("ones"), pick_e[:, 2, 0, :], start=True, stop=False)
                mm(bank(t)[:, E:2 * E], K("before"), pick_e[:, 2, 1, :], start=False, stop=True)
                mm(bank(t)[:, 2 * E:3 * E], K("ones"), pick_e[:, 2, 0, :], start=True, stop=False)
                mm(bank(t)[:, 2 * E:3 * E], K("ones"), pick_e[:, 2, 1, :], start=False, stop=True).then_inc(tile_ready, 1)
                for q in range(4):
                    wait_evac(pe, TILES[f"hn_{l}"] + q)
                wait_evac(pe, TILES[f"router_{l}"] + 1)
                for b in range(BANKS):
                    pe.wait_ge(evacuated[b], (TILES[f"combine_{l}"] - b + BANKS - 1) // BANKS)

                def gather(n, done):
                    for k in range(KT):
                        for tt in range(TT):
                            last = mm(ps[2 + k // 4][:, (k % 4) * P:(k % 4) * P + n], hn_tok[:, tt, k * P:(k + 1) * P],
                                      pick[:, tt, 0:n], start=tt == 0, stop=tt == TT - 1)
                    last.then_inc(done, 1)

                def up(slots, b, cols, arrived, done):
                    for half in range(2):
                        arrived(half)
                        w = expert_w[:, slots[half]].rearrange("p (k n) -> p k n", k=KT)
                        for n in range(4):
                            c0 = (4 * half + n) * SLOTS
                            for k in range(KT):
                                last = mm(ps[b][:, c0:c0 + SLOTS], w[:, k, n * P:(n + 1) * P],
                                          xg[:, k, cols:cols + SLOTS], start=k == 0, stop=k == KT - 1)
                        if done is None:
                            last.then_inc(expert_used, 1)
                    if done is not None:
                        last.then_inc(done, 1)

                def down(slot, a, done):
                    w = expert_w[:, slot].rearrange("p (k n) -> p k n", k=4)
                    for half in range(2):
                        for k in range(4):
                            last = mm(ps[4 + half][a * SLOTS:(a + 1) * SLOTS, :], act_h[:, a, k * SLOTS:(k + 1) * SLOTS],
                                      w[:, k, half * 512:(half + 1) * 512], start=k == 0, stop=k == 3)
                    last.then_inc(done, 1)

                pe.wait_ge(S("pick_ready"), (PAIRS + 1) * l + 1)
                gather(P, S("gathered"))
                with pe.Fori(0, PAIRS) as i:
                    n = PAIRS * l + i
                    pe.wait_ge(S("xg_act"), (PAIRS + 1) * l + i + 1)
                    pe.wait_ge(S("xg_dve"), (PAIRS + 1) * l + i + 1)
                    for a in range(2):
                        up((2 * a, 2 * a + 1), a, a * SLOTS, lambda half: pe.wait_ge(expert_in[2 * a + half], 16 * (n + 1)), None)
                    pe.wait_ge(S("pick_ready"), (PAIRS + 1) * l + i + 2)
                    gather(P, S("gathered"))
                    for a in range(2):
                        pe.wait_ge(expert_in[4 + a], 16 * (n + 1))
                        pe.wait_ge(S("hidden_e"), 2 * n + a + 1)
                        down(4 + a, a, expert_used)
                pe.wait_ge(S("xg_act"), (PAIRS + 1) * (l + 1))
                pe.wait_ge(S("xg_dve"), (PAIRS + 1) * (l + 1))
                pe.wait_ge(S("y_act"), PAIRS * (l + 1))
                pe.wait_ge(S("y_dve"), PAIRS * (l + 1))
                pe.wait_ge(S(f"over_ready_{l}"), 1)
                n_over = pe.value_load(over_i[0:1, 7:8], min_val=0, max_val=OVER)
                pe.sem_inc(S(f"over_used_{l}"), 1)
                with pe.Fori(0, OVER) as b:
                    with pe.If(b < n_over):
                        pe.wait_ge(S(f"over_pick_{l}"), b + 1)
                        gather(SLOTS, S(f"over_gathered_{l}"))
                        pe.wait_ge(S(f"over_xg_{l}"), 2 * b + 2)
                        up((0, 1), 0, 0, lambda half: pe.wait_ge(S(f"over_in_{l}_{half}"), 16 * (b + 1)),
                           S(f"over_up_{l}"))
                        pe.wait_ge(S(f"over_in_{l}_2"), 16 * (b + 1))
                        pe.wait_ge(S(f"over_hidden_{l}"), b + 1)
                        down(4, 0, S(f"over_used_{l}"))
                        pe.wait_ge(S(f"over_y_act_{l}"), b + 1)
                        pe.wait_ge(S(f"over_y_dve_{l}"), b + 1)
                for q in range(4):
                    t = TILES[f"combine_{l}"] + q
                    open_bank(pe, t)
                    if q == 0:
                        pe.wait_ge(S("combined"), TT * (l + 1))
                    for k in range(2):
                        for tt in range(TT):
                            last = nc.tensor.transpose(bank(t)[:, k * SEQ + tt * P:k * SEQ + (tt + 1) * P],
                                                       comb[:, tt, (2 * q + k) * P:(2 * q + k + 1) * P], ident)
                    last.then_inc(tile_ready, 1)

            experts(0)
            rms_norm("ret_norm")
            R = TILES["ret_in"]
            linear("ret_in", R, 2, u, hook=normed("ret_norm"))
            token_major("ret_in", R + 16, 2, 2, u, TT)
            linear("ret_in", R + 32, 2, u, at=4)
            pe.wait_ge(S("rotated"), 2)
            for hd in range(RET_HEADS):
                t = TILES["ret_scores"] + hd
                open_bank(pe, t)
                for jt, (c0, i0, n) in enumerate(((0, 0, SEQ), (SEQ, P, P))):
                    for s in range(2):
                        last = mm(bank(t)[:, c0:c0 + n], rqk[:, 8 + 2 * hd + s, jt * P:(jt + 1) * P],
                                  rqk[:, 2 * hd + s, i0:i0 + n], start=s == 0, stop=s == 1)
                last.then_inc(tile_ready, 1)
            for n in range(16):
                wait_evac(pe, R + 16 + n)
            for n in range(8):
                t = TILES["ret_pv"] + n
                hd = n // 2
                open_bank(pe, t)
                wait_evac(pe, TILES["ret_scores"] + hd)
                for s in range(2):
                    c0 = (2 * n + s) * P
                    mm(bank(t)[:, s * SEQ:(s + 1) * SEQ], rv[:, 0, c0:c0 + P], r_s[:, hd, 0:SEQ], start=True, stop=False)
                    last = mm(bank(t)[:, s * SEQ + P:(s + 1) * SEQ], rv[:, 1, c0:c0 + P], r_s[:, hd, SEQ:SEQ + P],
                              start=False, stop=True)
                last.then_inc(tile_ready, 1)
            for hd in range(RET_HEADS):
                stat(TILES["gn_mean"] + hd, K("mean_gn"), ro[:, 4 * hd:4 * hd + 4, :], 4,
                     lambda k: wait_evac(pe, TILES["ret_pv"] + 2 * hd + k // 2))
            for hd in range(RET_HEADS):
                stat(TILES["gn_var"] + hd, K("mean_gn"), rqk[:, 4 * hd:4 * hd + 4, :], 4,
                     lambda k: pe.wait_ge(S("gn_squares"), hd + 1))
            wide("ret_out", TILES["ret_out"], rgate, 2, lambda g: pe.wait_ge(S("ret_gated"), 8 * g + 8))
            experts(1)
            rms_norm("final_norm")
            pe.wait_ge(S("final_norm_out"), KT)
            for q in range(4):
                t = TILES["final"] + q
                open_bank(pe, t)
                for n in range(4):
                    k = (q % 2) * 4 + n
                    last = nc.tensor.transpose(bank(t)[:, n * P:(n + 1) * P], u[:, k, (q // 2) * P:(q // 2 + 1) * P], ident)
                last.then_inc(tile_ready, 1)

        @block.scalar
        def _(act):
            fn = nc.scalar.activation

            def copy_out(t, dst, src, func=None, scale=1.0):
                wait_tile(act, t)
                return evac(fn(dst, src, func or ACT.Copy, scale=scale), t)

            def square(name, src, waits):
                waits()
                for half in range(2):
                    s = slice(4 * half, 4 * half + 4)
                    fn(squares[:, s, :], src[:, s, :], ACT.Square).then_inc(S(f"{name}_squares"), 1)

            def deviation(dst, t, eps=0):
                wait_tile(act, t)
                at = CONSTS["eps"][0] + eps
                evac(fn(dst, bank(t)[:, 0:SEQ], ACT.Sqrt, bias=const[:, at:at + 1]), t)

            def ln_squares(name):
                square(name, centered, lambda: wait_evac(act, TILES[name]))
                deviation(rstd, TILES[name] + 1)

            def rms_squares(name, waits):
                square(name, h, waits)
                deviation(rstd, TILES[name])

            act.dma_start(vrow1, A["vec1"]).then_inc(S("in_small"), 16)
            act.dma_start(vrow2[0:N_VEC2, :], A["vec2"]).then_inc(S("in_small"), 16)
            act.dma_start(rows_in[:, :], A["rows"]).then_inc(S("in_small"), 16)
            act.dma_start(dft, A["dft"]).then_inc(S("in_dft"), 16)
            for l in range(DEPTH):
                act.dma_start(router_w[:, l], A["router_w"][l].rearrange("(k p) n -> p k n", p=P)).then_inc(S("in_router"), 16)
            act.dma_start(forget_w[:, :, :], A["fox_w_in_2"][0, :, 4 * D:4 * D + FOX_HEADS].rearrange(
                "(k p) n -> p k n", p=P)).then_inc(S("in_forget"), 16)
            act.dma_start(forget_b[:, :], A["fox_b_f_2"].rearrange("a n -> n a")).then_inc(S("in_forget"), 16)

            wait_evac(act, TILES["vecs"])
            fn(cond[:, :, :], vec[:, 0:16].rearrange("p (a k) -> p k a", a=2), ACT.Silu).then_inc(S("cond_ready"), 1)
            for q in range(4):
                copy_out(TILES["ctx"] + q, ctxT[:, 2 * q:2 * q + 2, :],
                         bank(TILES["ctx"] + q)[:, :].rearrange("p (k n) -> p k n", k=2))
            ln_squares("u")
            ln_squares("uc")
            W = TILES["w_in"]
            with act.Fori(0, 2) as i:
                for j in range(8):
                    t = W + j
                    act.wait_ge(tile_ready, t + 8 * i + 1)
                    evac(fn(proj[:, ds(8 * i + j, 1), :].rearrange("p a n -> p (a n)"), bank(t)[:, 0:SEQ], ACT.Copy), t)
            for n in range(4):
                copy_out(W + 16 + 2 * n, kraw[:, n, :], bank(W + 16 + 2 * n)[:, 0:SEQ])
                copy_out(W + 17 + 2 * n, kall[:, n, SEQ:2 * SEQ], bank(W + 17 + 2 * n)[:, 0:SEQ])
            for n in range(8):
                copy_out(W + 24 + n, v_all[:, n % 4, (n // 4) * CHUNK:(n // 4 + 1) * CHUNK], bank(W + 24 + n)[:, 0:CHUNK])
            act.wait_ge(S("lam_sums"), 2)
            fn(small[:, 4:6], small[:, 0:2], ACT.Exp).then_inc(S("lam_exps"), 1)
            T0 = TILES["attn"]
            for step in range(N_DIFF + 1):
                if step < N_DIFF:
                    for n in range(4):
                        t = T0 + diff_tile(step, n)
                        qt, c = n // 2, n % 2
                        act.wait_ge(S("diff_max"), 4 * step + n + 1)
                        if step:
                            act.wait_ge(S("pd_ready"), 2 * (step - 1) + qt + 1)
                        evac(fn(expd[:, qt, c, :], bank(t)[:, :], ACT.Exp, bias=small[:, 16 + n:17 + n],
                                accum_out=small[:, 24 + n:25 + n]), t)
                if step >= 1:
                    g = step - 1
                    for qt in range(TT):
                        t = T0 + diff_tile(g, 4 + qt)
                        copy_out(t, pdT[:, g % 2, :, qt * P:(qt + 1) * P],
                                 bank(t)[:, :].rearrange("p (k n) -> p k n", k=4))
                    t = T0 + diff_tile(g, 6)
                    wait_tile(act, t)
                    if g:
                        wait_tile(act, T0 + diff_tile(g - 1, 7))
                    fn(sq_o, bank(t)[:, 0:SEQ], ACT.Square).then_inc(S("sub_squares"), 1)
                    if g:
                        wait_evac(act, T0 + diff_tile(g - 1, 6))
                    deviation(rstd, T0 + diff_tile(g, 7), 1)

            def mlp(l):
                ln_squares(f"post1_{l}")
                ln_squares(f"mod2_{l}")
                with act.Fori(0, 4) as i:
                    for j in range(8):
                        t = TILES[f"w1_{l}"] + j
                        act.wait_ge(tile_ready, t + 8 * i + 1)
                        evac(fn(hidden[:, ds(8 * i + j, 1), :].rearrange("p a n -> p (a n)"), bank(t)[:, 0:SEQ], ACT.Relu), t)
                ln_squares(f"post2_{l}")

            mlp(0)
            ln_squares("mod1_1")
            for g in range(KT):
                t = TILES["dft_in"] + g
                copy_out(t, dft_mid[:, g], bank(t)[:, :].rearrange("p (t n) -> p t n", t=TT))
            mlp(1)

            rms_squares("fox_norm", lambda: act.wait_ge(S("post2_1_out"), KT))
            t = TILES["forget"]
            act.wait_ge(S("forget_abs"), 1)
            fn(flog[:, 1, :], flog[:, 0, :], ACT.Exp, scale=-1.0).then_inc(S("forget_exp"), 1)
            act.wait_ge(S("forget_one"), 1)
            fn(flog[:, 1, :], flog[:, 1, :], ACT.Ln).then_inc(S("forget_ln"), 1)
            F = TILES["fox_in"]
            for i, scale in ((0, FOX_DIM ** -0.5), (1, 1.0)):
                for j in range(8):
                    t = F + 8 * i + j
                    copy_out(t, fq[:, 8 * i + j, :], bank(t)[:, 0:SEQ], scale=scale)
            for j in range(8):
                t = F + 16 + j
                copy_out(t, fv[:, j % 2, (j // 2) * CHUNK:(j // 2 + 1) * CHUNK], bank(t)[:, 0:CHUNK])
            for j in range(8):
                copy_out(F + 24 + j, fgate[:, j, :], bank(F + 24 + j)[:, 0:SEQ], ACT.Sigmoid)
            T1 = TILES["fox_attn"]
            for step in range(FOX_HEADS // 2 + 1):
                if step < FOX_HEADS // 2:
                    for a in range(2):
                        t = T1 + fox_tile(step, a)
                        act.wait_ge(S("fox_max"), 2 * (2 * step + a) + 2)
                        if step:
                            wait_tile(act, T1 + fox_tile(step - 1, 2 + a))
                        for qt, (c0, nk) in enumerate(((0, P), (P, SEQ))):
                            last = fn(fexp[:, a, c0:c0 + nk], bank(t)[:, c0:c0 + nk], ACT.Exp,
                                      bias=small[:, 32 + 2 * a + qt:33 + 2 * a + qt],
                                      accum_out=small[:, 36 + 2 * a + qt:37 + 2 * a + qt])
                        evac(last, t)
                if step >= 1:
                    g = step - 1
                    for a in range(2):
                        t = T1 + fox_tile(g, 2 + a)
                        if g:
                            wait_tile(act, T1 + fox_tile(g - 1, 4))
                        copy_out(t, fpT[:, a, :], bank(t)[:, 0:384])

            def experts(l):
                rms_squares(f"moe_norm_{l}", (lambda: [wait_evac(act, TILES["fox_out"] + n) for n in range(8)]) if l == 0 else
                       (lambda: [wait_evac(act, TILES["ret_out"] + n) for n in range(8)]))
                act.wait_ge(S("group_max"), TT * (l + 1))
                for tt in range(TT):
                    fn(rt[:, 0 + 4 * tt:4 + 4 * tt], lg[:, tt, 0:GROUPS], ACT.Exp, bias=rt[:, 8 + tt:9 + tt],
                       accum_out=rt[:, 10 + tt:11 + tt]).then_inc(S("group_exp"), 1)
                act.wait_ge(S("second_gap"), l + 1)
                fn(rt[:, 14:16], rt[:, 12:14], ACT.Exp).then_inc(S("second_exp"), 1)
                for q in (0, 2):
                    t = TILES[f"hn_{l}"] + q
                    copy_out(t, hn_tok[:, q // 2, 0:512], bank(t)[:, :])

                def silu(a, done):
                    fn(sil[:, a, :], ps[a][:, 0:4 * SLOTS], ACT.Silu).then_inc(done, 1)

                def take_xg(n, done):
                    fn(xg[:, 0:4, 0:n], ps[2][:, :].rearrange("p (k n) -> p k n", k=4)[:, :, 0:n], ACT.Copy).then_inc(done, 1)

                if l == 0:
                    act.sem_inc(S("y_stored"), 16)
                act.wait_ge(S("gathered"), (PAIRS + 1) * l + 1)
                take_xg(P, S("xg_act"))
                with act.Fori(0, PAIRS) as i:
                    n = PAIRS * l + i
                    for a in range(2):
                        act.wait_ge(expert_used, 6 * n + 2 * a + 2)
                        silu(a, S("silu_e"))
                    act.wait_ge(S("gathered"), (PAIRS + 1) * l + i + 2)
                    take_xg(P, S("xg_act"))
                    act.wait_ge(expert_used, 6 * n + 6)
                    act.wait_ge(S("y_stored"), 16 * (n + 1))
                    fn(y_sb[:, 0:512], ps[4][:, :], ACT.Copy).then_inc(S("y_act"), 1)
                    act.wait_ge(S("y_act"), n + 1)
                    act.wait_ge(S("y_dve"), n + 1)
                    act.dma_start(expert_rows[ds(i * P, P), :], y_sb).then_inc(S("y_stored"), 16)
                act.wait_ge(S("y_stored"), 16 * PAIRS * (l + 1) + 16)
                act.wait_ge(S(f"over_ready_{l}"), 1)
                n_over = act.value_load(over_i[0:1, 7:8], min_val=0, max_val=OVER)
                act.sem_inc(S(f"over_stored_{l}"), 16)
                with act.Fori(0, OVER) as b:
                    with act.If(b < n_over):
                        act.wait_ge(S(f"over_gathered_{l}"), b + 1)
                        take_xg(SLOTS, S(f"over_xg_{l}"))
                        act.wait_ge(S(f"over_up_{l}"), b + 1)
                        silu(0, S(f"over_silu_{l}"))
                        act.wait_ge(S(f"over_used_{l}"), b + 2)
                        act.wait_ge(S(f"over_stored_{l}"), 16 * (b + 1))
                        fn(y_sb[0:SLOTS, 0:512], ps[4][0:SLOTS, :], ACT.Copy).then_inc(S(f"over_y_act_{l}"), 1)
                        act.wait_ge(S(f"over_y_act_{l}"), b + 1)
                        act.wait_ge(S(f"over_y_dve_{l}"), b + 1)
                        act.dma_start(expert_rows[ds(E * SLOTS + b * SLOTS, SLOTS), :], y_sb[0:SLOTS, :]).then_inc(
                            S(f"over_stored_{l}"), 16)
                act.wait_ge(S(f"over_stored_{l}"), 16 * n_over + 16)
                act.sem_inc(S("experts_done"), 1)

            experts(0)
            rms_squares("ret_norm", lambda: [wait_evac(act, TILES["combine_0"] + q) for q in range(4)])
            R = TILES["ret_in"]
            for n in range(16):
                copy_out(R + n, rraw[:, n, :], bank(R + n)[:, 0:SEQ], scale=1.0 if n < 8 else (D // RET_HEADS) ** -0.5)
            for n in range(16):
                t = R + 16 + n
                copy_out(t, rv[:, n % 2, (n // 2) * CHUNK:(n // 2 + 1) * CHUNK], bank(t)[:, 0:CHUNK])
            for n in range(16):
                copy_out(R + 32 + n, rgate[:, n, :], bank(R + 32 + n)[:, 0:SEQ], ACT.Silu)
            for n in range(8):
                t = TILES["ret_pv"] + n
                copy_out(t, ro[:, 2 * n:2 * n + 2, :], bank(t)[:, :].rearrange("p (k n) -> p k n", k=2))
            for hd in range(RET_HEADS):
                wait_evac(act, TILES["gn_mean"] + hd)
                fn(rqk[:, 4 * hd:4 * hd + 4, :], ro[:, 4 * hd:4 * hd + 4, :], ACT.Square).then_inc(S("gn_squares"), 1)
            for hd in range(RET_HEADS):
                deviation(gn_rstd[:, hd, :], TILES["gn_var"] + hd)
            experts(1)
            rms_squares("final_norm", lambda: [wait_evac(act, TILES["combine_1"] + q) for q in range(4)])
            for q in (0, 2):
                t = TILES["final"] + q
                wait_tile(act, t)
                fn(comb[:, q // 2, 0:512], bank(t)[:, :], ACT.Copy).then_inc(S("out_act"), 1)

        @block.vector
        def _(dve):
            V = nc.vector
            chain = S("dve_chain")
            n_chain = [0]

            def link(ins):
                n_chain[0] += 1
                ins.then_inc(chain, 1)
                dve.wait_ge(chain, n_chain[0])

            def over_tiles(v, n):
                return v.unsqueeze(1).broadcast_to([P, n, SEQ])

            def inv_std(dst, t):
                wait_evac(dve, t)
                link(V.reciprocal(dst, dst))

            def layer_norm(name, src, dst, scale, shift, free=None):
                t = TILES[name]
                wait_tile(dve, t)
                evac(V.tensor_tensor(centered, src, over_tiles(bank(t)[:, 0:SEQ], KT), ALU.subtract), t)
                wait_evac(dve, t)
                inv_std(rstd, t + 1)
                link(V.tensor_tensor(centered, centered, over_tiles(rstd, KT), ALU.mult))
                for k in range(KT):
                    V.tensor_scalar(dst[:, k, :], centered[:, k, :], scale(k), shift(k), ALU.mult, ALU.add).then_inc(S(f"{name}_out"), 1)

            def rms_norm(name, gain):
                inv_std(rstd, TILES[name])
                for k in range(KT):
                    V.scalar_tensor_tensor(u[:, k, :], h[:, k, :], gain(k), rstd, ALU.mult, ALU.mult).then_inc(S(f"{name}_out"), 1)

            def vcol(at):
                return vec[:, at:at + 1]

            def mcol(l, at, c=0):
                return mod[:, l, at, c:c + 1]

            t = TILES["vecs"]
            wait_tile(dve, t)
            evac(V.tensor_copy(vec[:, :], bank(t)[:, 0:P + N_VEC2]), t)
            wait_tile(dve, t + 1)
            evac(V.tensor_copy(rowbc[:, :], bank(t + 1)[:, 0:N_ROW]), t + 1)
            wait_evac(dve, t)
            wait_evac(dve, t + 1)
            for n in range(2):
                V.tensor_tensor_reduce(out=small[:, 64:128], in0=rowbc[:, 128 * n:128 * n + 64],
                                       in1=rowbc[:, 128 * n + 64:128 * n + 128], scale=1.0, scalar=0.0,
                                       op0=ALU.mult, op1=ALU.add, accum_out=small[:, n:n + 1]).then_inc(S("lam_sums"), 1)
                dve.wait_ge(S("lam_sums"), n + 1)
            for q in range(4):
                t = TILES["x"] + q
                wait_tile(dve, t)
                evac(V.tensor_copy(h[:, 2 * q:2 * q + 2, :], bank(t)[:, :].rearrange("p (k n) -> p k n", k=2)), t)
            for n in range(12):
                t = TILES["ada"] + n
                l, i = n // 6, n % 6
                b0 = P * 0 + VEC1["ada_b"] + 48 * l + 8 * i
                wait_tile(dve, t)
                evac(V.tensor_tensor(mod[:, l, 8 * i:8 * i + 8, :], bank(t)[:, 0:16].rearrange("p (m a) -> p m a", a=2),
                                     vec[:, b0:b0 + 8].unsqueeze(2).broadcast_to([P, 8, 2]), ALU.add), t)
                wait_evac(dve, t)
            for at in (SC1, SC2):
                link(V.tensor_scalar(mod[:, :, at:at + KT, :], mod[:, :, at:at + KT, :], 1.0, None, ALU.add))
            for q in range(4):
                wait_evac(dve, TILES["x"] + q)
            layer_norm("u", h, u, lambda k: mcol(0, SC1 + k), lambda k: mcol(0, SH1 + k))
            for q in range(4):
                wait_evac(dve, TILES["ctx"] + q)
            dve.wait_ge(S("u_out"), KT)
            layer_norm("uc", ctxT, uc, lambda k: mcol(0, SC1 + k, 1), lambda k: mcol(0, SH1 + k, 1))
            W = TILES["w_in"]
            for n in range(4):
                for b in range(3):
                    wait_evac(dve, W + 4 * b + n)
                gb, gc, cv = (proj[:, 4 * b + n, :] for b in range(3))
                w0 = P + VEC2["conv"]
                link(V.tensor_tensor(gc, gc, cv, ALU.mult))
                link(V.tensor_scalar(cv, gc, vcol(w0 + 4 + n), None, ALU.mult))
                link(V.scalar_tensor_tensor(cv[:, 1:SEQ], gc[:, 0:SEQ - 1], vcol(w0 + n), cv[:, 1:SEQ], ALU.mult, ALU.add))
                link(V.scalar_tensor_tensor(cv[:, 0:SEQ - 1], gc[:, 1:SEQ], vcol(w0 + 8 + n), cv[:, 0:SEQ - 1], ALU.mult, ALU.add))
                V.tensor_tensor(cat[:, n, :], gb, cv, ALU.mult).then_inc(S("conv_out"), 1)
            for n in range(8):
                t = TILES["rope"] + n
                raw = proj[:, 12 + n, :] if n < 4 else kraw[:, n - 4, :]
                dst = qrot[:, n, :] if n < 4 else kall[:, n - 4, 0:SEQ]
                scale = DIFF_QK ** -0.5 if n < 4 else 1.0
                wait_tile(dve, t)
                V.scalar_tensor_tensor(rope_b, raw, scale, K("rope_cos"), ALU.mult, ALU.mult).then_inc(S("rope_cos_part"), 1)
                evac(V.scalar_tensor_tensor(rope_a, bank(t)[:, 0:SEQ], scale, K("rope_sin"), ALU.mult, ALU.mult), t)
                dve.wait_ge(S("rope_cos_part"), n + 1)
                wait_evac(dve, t)
                V.tensor_tensor(dst, rope_a, rope_b, ALU.add).then_inc(S("rope_out"), 1)
                dve.wait_ge(S("rope_out"), n + 1)
            dve.wait_ge(S("lam_exps"), 1)
            link(V.tensor_tensor(small[:, 6:7], small[:, 5:6], small[:, 4:5], ALU.subtract))
            link(V.tensor_scalar(small[:, 7:8], small[:, 6:7], LAM_INIT, None, ALU.subtract))
            link(V.tensor_scalar(small[:, 8:9], vcol(P + VEC2["subln"]), 1.0 - LAM_INIT, None, ALU.mult))
            T0 = TILES["attn"]
            for step in range(N_DIFF + 1):
                if step < N_DIFF:
                    for n in range(4):
                        t = T0 + diff_tile(step, n)
                        wait_tile(dve, t)
                        V.tensor_reduce(small[:, 16 + n:17 + n], bank(t)[:, :], AX.X, ALU.max, negate=True).then_inc(S("diff_max"), 1)
                    for qt in range(TT):
                        for c in range(2):
                            wait_evac(dve, T0 + diff_tile(step, 2 * qt + c))
                        link(V.reciprocal(small[:, 128 + 2 * qt:130 + 2 * qt], small[:, 24 + 2 * qt:26 + 2 * qt]))
                        link(V.tensor_scalar(small[:, 129 + 2 * qt:130 + 2 * qt], small[:, 129 + 2 * qt:130 + 2 * qt],
                                             small[:, 7:8], None, ALU.mult))
                        link(V.tensor_scalar(expd[:, qt, 0, :], expd[:, qt, 0, :], small[:, 128 + 2 * qt:129 + 2 * qt], None, ALU.mult))
                        if step:
                            wait_tile(dve, T0 + diff_tile(step - 1, 4 + qt))
                        V.scalar_tensor_tensor(pd[:, qt, :], expd[:, qt, 1, :], small[:, 129 + 2 * qt:130 + 2 * qt],
                                               expd[:, qt, 0, :], ALU.mult, ALU.add).then_inc(S("pd_ready"), 1)
                if step >= 1:
                    g = step - 1
                    inv_std(rstd, T0 + diff_tile(g, 7))
                    t = T0 + diff_tile(g, 6)
                    evac(V.scalar_tensor_tensor(cat[:, 4 + g, :], bank(t)[:, 0:SEQ], small[:, 8:9], rstd, ALU.mult, ALU.mult), t)
                    wait_evac(dve, t)
            S("sub_out")

            def residual(name, l, gate):
                link(V.tensor_scalar(resid, h[:, :, :], ALPHA, None, ALU.mult))
                for k in range(KT):
                    t = TILES[name] + k
                    wait_tile(dve, t)
                    evac(V.scalar_tensor_tensor(resid[:, k, :], bank(t)[:, 0:SEQ], mcol(l, gate + k), resid[:, k, :],
                                                ALU.mult, ALU.add), t)

            def mlp(l):
                name = "mix" if l == 0 else "fourier"
                if l == 0:
                    dve.wait_ge(S("rows_zeroed"), 16)
                g0, b0 = P + VEC2["ln_g"] + 16 * l, P + VEC2["ln_b"] + 16 * l
                residual(name, l, G1)
                layer_norm(f"post1_{l}", resid, h, lambda k: vcol(g0 + k), lambda k: vcol(b0 + k))
                dve.wait_ge(S(f"post1_{l}_out"), KT)
                layer_norm(f"mod2_{l}", h, u, lambda k: mcol(l, SC2 + k), lambda k: mcol(l, SH2 + k))
                with dve.Fori(0, 4) as i:
                    for j in range(8):
                        t = TILES[f"w1_{l}"] + j
                        dve.wait_ge(evacuated[t % BANKS], t // BANKS + 1 + i)
                        v = hidden[:, ds(8 * i + j, 1), :].rearrange("p a n -> p (a n)")
                        V.tensor_tensor(v, v, v, ALU.mult).then_inc(S("hidden_ready"), 1)
                residual(f"w2_{l}", l, G2)
                layer_norm(f"post2_{l}", resid, h, lambda k: vcol(g0 + 8 + k), lambda k: vcol(b0 + 8 + k))
                dve.wait_ge(S(f"post2_{l}_out"), KT)

            mlp(0)
            layer_norm("mod1_1", h, u, lambda k: mcol(1, SC1 + k), lambda k: mcol(1, SH1 + k))
            for g in range(KT):
                t = TILES["dft_out"] + g
                wait_tile(dve, t)
                evac(V.tensor_copy(spectrum[:, g, :], bank(t)[:, 0:SEQ]), t)
            mlp(1)

            rms_norm("fox_norm", lambda k: vcol(P + VEC2["mix"] + k))
            t = TILES["forget"]
            dve.wait_ge(S("in_forget"), 32)
            wait_tile(dve, t)
            evac(V.tensor_scalar(flog[:, 2, :], bank(t)[0:FOX_HEADS, 0:SEQ], forget_b[:, 0:1], None, ALU.add), t)
            wait_evac(dve, t)
            V.scalar_tensor_tensor(flog[:, 0, :], flog[:, 2, :], -1.0, flog[:, 2, :], ALU.mult, ALU.max).then_inc(S("forget_abs"), 1)
            dve.wait_ge(S("forget_abs"), 1)
            link(V.tensor_scalar(flog[:, 2, :], flog[:, 2, :], 0.0, None, ALU.min))
            link(V.memset(flog[:, 3, :], 1.0))
            dve.wait_ge(S("forget_exp"), 1)
            V.tensor_scalar(flog[:, 1, :], flog[:, 1, :], 1.0, None, ALU.add).then_inc(S("forget_one"), 1)
            dve.wait_ge(S("forget_ln"), 1)
            link(V.tensor_tensor(flog[:, 2, :], flog[:, 2, :], flog[:, 1, :], ALU.subtract))
            V.tensor_tensor_scan(cum, flog[:, 3, :], flog[:, 2, :], 0.0, ALU.mult, ALU.add).then_inc(S("cum_ready"), 1)
            dve.wait_ge(S("cum_ready"), 1)
            V.tensor_scalar(ncum, cum, -1.0, None, ALU.mult).then_inc(S("cum_ready"), 1)
            F, T1 = TILES["fox_in"], TILES["fox_attn"]
            for step in range(FOX_HEADS // 2 + 1):
                if step < FOX_HEADS // 2:
                    for a in range(2):
                        t = T1 + fox_tile(step, a)
                        wait_tile(dve, t)
                        for qt, (c0, nk) in enumerate(((0, P), (P, SEQ))):
                            V.tensor_reduce(small[:, 32 + 2 * a + qt:33 + 2 * a + qt], bank(t)[:, c0:c0 + nk], AX.X, ALU.max,
                                            negate=True).then_inc(S("fox_max"), 1)
                    for a in range(2):
                        wait_evac(dve, T1 + fox_tile(step, a))
                        link(V.reciprocal(small[:, 40 + 2 * a:42 + 2 * a], small[:, 36 + 2 * a:38 + 2 * a]))
                        link(V.tensor_scalar(fexp[:, a, 0:P], fexp[:, a, 0:P], small[:, 40 + 2 * a:41 + 2 * a], None, ALU.mult))
                        V.tensor_scalar(fexp[:, a, P:384], fexp[:, a, P:384], small[:, 41 + 2 * a:42 + 2 * a], None,
                                        ALU.mult).then_inc(S("fox_probs"), 1)
                if step >= 1:
                    g = step - 1
                    t = T1 + fox_tile(g, 4)
                    wait_tile(dve, t)
                    wait_evac(dve, F + 24 + g)
                    evac(V.tensor_tensor(fgate[:, g, :], fgate[:, g, :], bank(t)[:, 0:SEQ], ALU.mult), t)

            def add_to_h(name):
                for k in range(KT):
                    t = TILES[name] + k
                    wait_tile(dve, t)
                    evac(V.tensor_tensor(h[:, k, :], h[:, k, :], bank(t)[:, 0:SEQ], ALU.add), t)

            add_to_h("fox_out")

            def experts(l):
                rms_norm(f"moe_norm_{l}", lambda k: vcol(P + VEC2["ffn"] + 8 * l + k))
                if l == 0:
                    link(V.memset(zrow[:, :], 0.0))
                iota = K("iota")
                bias = rowbc[:, ROW_ROUTER + NR * l:ROW_ROUTER + NR * (l + 1)]
                t = TILES[f"router_{l}"]
                wait_tile(dve, t)
                evac(V.tensor_tensor(lg[:, :, :], bank(t)[:, 0:TT * NR].rearrange("p (t n) -> p t n", t=TT),
                                     bias.unsqueeze(1).broadcast_to([P, TT, NR]), ALU.add), t)
                wait_evac(dve, t)
                link(V.memset(pad8[:, :, :], -3.0e38))
                link(V.tensor_copy(pad8[:, :, 0:GROUPS], lg[:, :, 0:GROUPS]))
                for tt in range(TT):
                    link(V.max(top[:, tt, :], pad8[:, tt, :]))
                    link(V.max_index(topi[:, tt, :], top[:, tt, :], pad8[:, tt, :]))
                    V.tensor_scalar(rt[:, 8 + tt:9 + tt], top[:, tt, 0:1], -1.0, None, ALU.mult).then_inc(S("group_max"), 1)
                    link(V.tensor_copy(rt[:, 16 + tt:17 + tt], topi[:, tt, 0:1]))
                    link(V.tensor_scalar(onehot_g[:, tt, :], iota[:, 0:GROUPS], rt[:, 16 + tt:17 + tt], None, ALU.is_equal))
                    link(V.tensor_scalar(e_in[:, tt, :], lg[:, tt, GROUPS:GROUPS + EPG], onehot_g[:, tt, 0:1], None, ALU.mult))
                    for g in range(1, GROUPS):
                        link(V.scalar_tensor_tensor(e_in[:, tt, :], lg[:, tt, GROUPS + EPG * g:GROUPS + EPG * (g + 1)],
                                                    onehot_g[:, tt, g:g + 1], e_in[:, tt, :], ALU.mult, ALU.add))
                    link(V.max(top[:, 2 + tt, :], e_in[:, tt, :]))
                    link(V.max_index(topi[:, 2 + tt, :], top[:, 2 + tt, :], e_in[:, tt, :]))
                    link(V.tensor_tensor(rt[:, 12 + tt:13 + tt], top[:, 2 + tt, 1:2], top[:, 2 + tt, 0:1], ALU.subtract))
                    link(V.tensor_copy(rt[:, 18 + 2 * tt:20 + 2 * tt], topi[:, 2 + tt, 0:2]))
                    link(V.scalar_tensor_tensor(rt[:, 22 + 2 * tt:24 + 2 * tt], rt[:, 16 + tt:17 + tt].broadcast_to([P, 2]), float(EPG),
                                                rt[:, 18 + 2 * tt:20 + 2 * tt], ALU.mult, ALU.add))
                    for c in range(2):
                        link(V.tensor_scalar(pick_e[:, c, tt, :], iota[:, 0:E], rt[:, 22 + 2 * tt + c:23 + 2 * tt + c], None, ALU.is_equal))
                V.tensor_tensor(pick_e[:, 2, :, :], pick_e[:, 0, :, :], pick_e[:, 1, :, :], ALU.add).then_inc(S("choices"), 1)
                V.tensor_copy(rt[:, 12:14], rt[:, 12:14]).then_inc(S("second_gap"), 1)
                for q in (1, 3):
                    t = TILES[f"hn_{l}"] + q
                    wait_tile(dve, t)
                    evac(V.tensor_copy(hn_tok[:, q // 2, 512:1024], bank(t)[:, :]), t)
                t = TILES[f"router_{l}"] + 1
                wait_tile(dve, t)
                link(V.tensor_copy(pos[:, :, :], bank(t)[:, 0:TT * E].rearrange("p (t n) -> p t n", t=TT)))
                evac(V.tensor_copy(e_sum[:, 0, :], bank(t)[:, 2 * E:3 * E]), t)
                wait_evac(dve, t)
                link(V.tensor_scalar(e_sum[:, 1, :], e_sum[:, 0, :], float(SLOTS), None, ALU.is_gt))
                for n in range(2, SEQ // SLOTS):
                    link(V.scalar_tensor_tensor(e_sum[:, 1, :], e_sum[:, 0, :], float(n * SLOTS), e_sum[:, 1, :], ALU.is_gt, ALU.add))
                link(V.tensor_tensor_scan(e_sum[:, 2, :], e_sum[:, 1, :], zrow[:, :], 0.0, ALU.add, ALU.add))
                link(V.tensor_tensor(e_sum[:, 3, :], e_sum[:, 2, :], e_sum[:, 1, :], ALU.subtract))
                for b in range(OVER):
                    link(V.tensor_scalar(pick_tmp[:, 0, 0:E], e_sum[:, 2, :], float(b), None, ALU.is_le))
                    link(V.tensor_reduce(over_f[:, b:b + 1], pick_tmp[:, 0, 0:E], AX.X, ALU.add))
                link(V.tensor_scalar(over_f[:, 0:OVER], over_f[:, 0:OVER], float(E - 1), None, ALU.min))
                link(V.tensor_copy(over_f[:, 7:8], e_sum[:, 2, E - 1:E]))
                V.tensor_copy(over_i[:, :], over_f[:, :]).then_inc(S(f"over_ready_{l}"), 1)
                for c in range(2):
                    for src, at in ((pos[:, :, :], 26), (e_sum[:, 3, :].unsqueeze(1).broadcast_to([P, TT, E]), 28)):
                        tmp = pick_tmp[:, :, 0:E]
                        link(V.tensor_tensor(tmp, pick_e[:, c, :, :], src, ALU.mult))
                        link(V.tensor_reduce(rt[:, at:at + 2], tmp, AX.X, ALU.add))
                    eid = rt[:, 22:26].rearrange("p (t c) -> p t c", t=TT)[:, :, c]
                    link(V.tensor_scalar(rt[:, 30:32], rt[:, 26:28], float(SLOTS), None, ALU.is_ge))
                    link(V.tensor_scalar(rt[:, 28:30], rt[:, 28:30], float(SLOTS), float((E - 1) * SLOTS), ALU.mult, ALU.add))
                    link(V.tensor_scalar(rt[:, 32:34], eid, float(SLOTS), None, ALU.mult))
                    link(V.tensor_tensor(rt[:, 28:30], rt[:, 28:30], rt[:, 32:34], ALU.subtract))
                    link(V.tensor_tensor(rt[:, 28:30], rt[:, 28:30], rt[:, 30:32], ALU.mult))
                    link(V.tensor_tensor(rt[:, 28:30], rt[:, 28:30], rt[:, 32:34], ALU.add))
                    link(V.tensor_tensor(rel[:, c, :], rt[:, 28:30], rt[:, 26:28], ALU.add))
                V.tensor_copy(row_i[:, :, :], rel[:, :, :]).then_inc(S("rows_known"), 1)
                dve.wait_ge(S("group_exp"), TT * (l + 1))
                dve.wait_ge(S("second_exp"), l + 1)
                link(V.tensor_scalar(rt[:, 34:36], rt[:, 14:16], 1.0, None, ALU.add))
                link(V.tensor_tensor(rt[:, 34:36], rt[:, 34:36], rt[:, 10:12], ALU.mult))
                link(V.reciprocal(rt[:, 36:38], rt[:, 34:36]))
                link(V.tensor_tensor(rt[:, 38:40], rt[:, 36:38], rt[:, 14:16], ALU.mult))

                def build_pick(n, done, step, linked):
                    for tt in range(TT):
                        linked(V.tensor_scalar(pick_tmp[:, tt, 0:n], iota[:, 0:n], rel[:, 0, tt:tt + 1], None, ALU.is_equal))
                        last = V.scalar_tensor_tensor(pick[:, tt, 0:n], iota[:, 0:n], rel[:, 1, tt:tt + 1], pick_tmp[:, tt, 0:n],
                                                      ALU.is_equal, ALU.add)
                        if tt < TT - 1:
                            linked(last)
                    return last

                def next_rows(step):
                    return V.tensor_scalar(rel[:, :, :], rel[:, :, :], float(-step), None, ALU.add)

                build_pick(P, None, P, link).then_inc(S("pick_ready"), 1)
                dve.wait_ge(S("pick_ready"), (PAIRS + 1) * l + 1)
                link(next_rows(P))
                dve.wait_ge(S("gathered"), (PAIRS + 1) * l + 1)

                def hidden_e(a, done):
                    V.tensor_tensor(act_h[:, a, :], sil[:, a, :], ps[a][:, 4 * SLOTS:8 * SLOTS], ALU.mult).then_inc(done, 1)

                def take_xg(n, done):
                    V.tensor_copy(xg[:, 4:8, 0:n], ps[3][:, :].rearrange("p (k n) -> p k n", k=4)[:, :, 0:n]).then_inc(done, 1)

                take_xg(P, S("xg_dve"))
                loop_chain = S(f"pick_chain_{l}")
                with dve.Fori(0, PAIRS) as i:
                    n = PAIRS * l + i
                    at = [0]

                    def linked(ins):
                        at[0] += 1
                        ins.then_inc(loop_chain, 1)
                        dve.wait_ge(loop_chain, 4 * i + at[0])
                    dve.wait_ge(S("gathered"), (PAIRS + 1) * l + i + 1)
                    build_pick(P, None, P, linked).then_inc(S("pick_ready"), 1)
                    dve.wait_ge(S("pick_ready"), (PAIRS + 1) * l + i + 2)
                    linked(next_rows(P))
                    for a in range(2):
                        dve.wait_ge(S("silu_e"), 2 * n + a + 1)
                        hidden_e(a, S("hidden_e"))
                    dve.wait_ge(S("gathered"), (PAIRS + 1) * l + i + 2)
                    take_xg(P, S("xg_dve"))
                    dve.wait_ge(expert_used, 6 * n + 6)
                    dve.wait_ge(S("y_stored"), 16 * (n + 1))
                    V.tensor_copy(y_sb[:, 512:1024], ps[5][:, :]).then_inc(S("y_dve"), 1)
                link(next_rows(-P))
                n_over = dve.value_load(over_i[0:1, 7:8], min_val=0, max_val=OVER)
                over_chain = S(f"over_chain_{l}")
                with dve.Fori(0, OVER) as b:
                    with dve.If(b < n_over):
                        at = [0]

                        def linked(ins):
                            at[0] += 1
                            ins.then_inc(over_chain, 1)
                            dve.wait_ge(over_chain, 4 * b + at[0])
                        build_pick(SLOTS, None, SLOTS, linked).then_inc(S(f"over_pick_{l}"), 1)
                        dve.wait_ge(S(f"over_pick_{l}"), b + 1)
                        linked(next_rows(SLOTS))
                        dve.wait_ge(S(f"over_gathered_{l}"), b + 1)
                        take_xg(SLOTS, S(f"over_xg_{l}"))
                        dve.wait_ge(S(f"over_silu_{l}"), b + 1)
                        hidden_e(0, S(f"over_hidden_{l}"))
                        dve.wait_ge(S(f"over_used_{l}"), b + 2)
                        dve.wait_ge(S(f"over_stored_{l}"), 16 * (b + 1))
                        V.tensor_copy(y_sb[0:SLOTS, 512:1024], ps[5][0:SLOTS, :]).then_inc(S(f"over_y_dve_{l}"), 1)
                for tt in range(TT):
                    dve.wait_ge(S(f"rows_back_{tt}_0"), 16 * (l + 1))
                    dve.wait_ge(S(f"rows_back_{tt}_1"), 16 * (l + 1))
                    link(V.tensor_scalar(comb[:, tt, :], y_back[:, 2 * tt, :], rt[:, 36 + tt:37 + tt], None, ALU.mult))
                    V.scalar_tensor_tensor(comb[:, tt, :], y_back[:, 2 * tt + 1, :], rt[:, 38 + tt:39 + tt], comb[:, tt, :],
                                           ALU.mult, ALU.add).then_inc(S("combined"), 1)
                for q in range(4):
                    t = TILES[f"combine_{l}"] + q
                    wait_tile(dve, t)
                    hv = h[:, 2 * q:2 * q + 2, :]
                    evac(V.tensor_tensor(hv, hv, bank(t)[:, :].rearrange("p (k n) -> p k n", k=2), ALU.add), t)
                for q in range(4):
                    wait_evac(dve, TILES[f"combine_{l}"] + q)

            for n in range(8):
                wait_evac(dve, TILES["fox_out"] + n)
            experts(0)
            rms_norm("ret_norm", lambda k: vcol(P + VEC2["mix"] + 8 + k))
            R = TILES["ret_in"]
            for qk in range(2):
                for n in range(8):
                    wait_evac(dve, R + 8 * qk + n)
                raw = rraw[:, 8 * qk:8 * qk + 8, :].rearrange("p (a s) n -> p a s n", s=2)
                dst = rqk[:, 8 * qk:8 * qk + 8, :].rearrange("p (a s) n -> p a s n", s=2)
                cos, sin = over_tiles(K("ret_cos"), 4), over_tiles(K("ret_sin"), 4)
                tmp = rtmp[:, 0:4, :]
                link(V.tensor_tensor(dst[:, :, 0, :], raw[:, :, 0, :], cos, ALU.mult))
                link(V.tensor_tensor(tmp, raw[:, :, 1, :], sin, ALU.mult))
                link(V.tensor_tensor(dst[:, :, 0, :], dst[:, :, 0, :], tmp, ALU.subtract))
                link(V.tensor_tensor(dst[:, :, 1, :], raw[:, :, 1, :], cos, ALU.mult))
                link(V.tensor_tensor(tmp, raw[:, :, 0, :], sin, ALU.mult))
                V.tensor_tensor(dst[:, :, 1, :], dst[:, :, 1, :], tmp, ALU.add).then_inc(S("rotated"), 1)
                dve.wait_ge(S("rotated"), qk + 1)
            dve.wait_ge(S("in_decay"), 16)
            for hd in range(RET_HEADS):
                t = TILES["ret_scores"] + hd
                wait_tile(dve, t)
                evac(V.tensor_tensor(r_s[:, hd, :], bank(t)[:, 0:384], decay[:, hd, :], ALU.mult), t)
            for hd in range(RET_HEADS):
                t = TILES["gn_mean"] + hd
                wait_tile(dve, t)
                o = ro[:, 4 * hd:4 * hd + 4, :]
                evac(V.tensor_tensor(o, o, over_tiles(bank(t)[:, 0:SEQ], 4), ALU.subtract), t)
            for hd in range(RET_HEADS):
                wait_evac(dve, TILES["ret_scores"] + hd)
                wait_evac(dve, TILES["gn_mean"] + hd)
                inv_std(gn_rstd[:, hd, :], TILES["gn_var"] + hd)
                o = ro[:, 4 * hd:4 * hd + 4, :]
                link(V.tensor_tensor(o, o, over_tiles(gn_rstd[:, hd, :], 4), ALU.mult))
                for n in range(4 * hd, 4 * hd + 4):
                    wait_evac(dve, R + 32 + n)
                    V.scalar_tensor_tensor(rgate[:, n, :], ro[:, n, :], vcol(VEC1["gn"] + n), rgate[:, n, :],
                                           ALU.mult, ALU.mult).then_inc(S("ret_gated"), 1)
            add_to_h("ret_out")
            for n in range(8):
                wait_evac(dve, TILES["ret_out"] + n)
            experts(1)
            rms_norm("final_norm", lambda k: vcol(P + VEC2["final"] + k))
            for q in (1, 3):
                t = TILES["final"] + q
                wait_tile(dve, t)
                V.tensor_copy(comb[:, q // 2, 512:1024], bank(t)[:, :]).then_inc(S("out_dve"), 1)

        @block.gpsimd
        def _(pool):
            zeros = work[0:SLOTS, 0:D]
            nc.gpsimd.memset(zeros, 0.0).then_inc(S("zeros"), 1)
            pool.wait_ge(S("zeros"), 1)
            pool.dma_start(expert_rows[E * SLOTS:ROWS, :].rearrange("(b p) d -> p b d", p=SLOTS),
                           zeros.unsqueeze(1).broadcast_to([SLOTS, OVER, D])).then_inc(S("rows_zeroed"), 16)
            for l in range(DEPTH):
                pool.wait_ge(S("rows_known"), l + 1)
                pool.wait_ge(S("experts_done"), l + 1)
                pool.wait_ge(S("rows_zeroed"), 16)
                for tt in range(TT):
                    for c in range(2):
                        nc.gpsimd.indirect_dma_start(
                            out=y_back[:, 2 * tt + c, :], out_offset=None, in_=expert_rows[:, :],
                            in_offset=bass.IndirectOffsetOnAxis(ap=row_i[:, c, tt:tt + 1], axis=0),
                        ).then_inc(S(f"rows_back_{tt}_{c}"), 16)


def diff_tile(head, n):
    if n < 4:
        return (0 if head == 0 else 4 + 8 * (head - 1)) + n
    step = head + 1
    return (4 + 8 * head) + (4 if step < N_DIFF else 0) + n - 4


def fox_tile(pair, n):
    if n < 2:
        return (0 if pair == 0 else 2 + 5 * (pair - 1)) + n
    return (2 + 5 * pair) + (2 if pair + 1 < FOX_HEADS // 2 else 0) + n - 2


def constants():
    f = np.float32
    c = np.zeros((P, N_CONST), f)

    def put(name, v):
        at, n = CONSTS[name]
        c[:, at:at + n] = v
    p = np.arange(P)
    put("ident", np.eye(P))
    put("ones", 1.0)
    put("mean_d", 1.0 / D)
    put("mean_v", 1.0 / P)
    put("mean_gn", 1.0 / (RET_V_TILES * P))
    swap = np.zeros((P, P), f)
    for m in range(P):
        if m % 32 < 16:
            swap[m + 16, m] = -1.0
        else:
            swap[m - 16, m] = 1.0
    put("swap", swap)
    put("causal", np.where(p[None, :] <= p[:, None], 0.0, -1e30))
    put("before", (p[:, None] < p[None, :]).astype(f))
    put("iota", np.broadcast_to(p.astype(f), (P, P)))
    put("eps", np.array([[LN_EPS, SUBLN_EPS]], f))
    n = np.arange(SEQ)
    inv = (f(10000.0) ** (-np.arange(16, dtype=f) / f(16))).astype(f)
    where = np.where((p % 64 < 32)[:, None], (n // GRID_W)[None, :], (n % GRID_W)[None, :]).astype(f)
    ang = where * inv[p % 16][:, None]
    put("rope_cos", np.cos(ang))
    put("rope_sin", np.sin(ang))
    inv = (f(1.0) / (f(10000.0) ** np.linspace(0.0, 1.0, P, dtype=f))).astype(f)
    ang = n[None, :].astype(f) * inv[:, None]
    put("ret_cos", np.cos(ang))
    put("ret_sin", np.sin(ang))
    d = np.zeros((P, N_DFT), np.float64)
    th = 2 * np.pi * np.outer(p, p) / P
    d[:, 0:P], d[:, P:2 * P] = np.cos(th), np.sin(th)
    norm = 1.0 / math.sqrt(SEQ * P)
    for tt in range(TT):
        th = 2 * np.pi * (np.outer(p + tt * P, n) % SEQ) / SEQ
        d[:, 2 * P + tt * SEQ:2 * P + (tt + 1) * SEQ] = norm * np.cos(th)
        d[:, 2 * P + (2 + tt) * SEQ:2 * P + (3 + tt) * SEQ] = -norm * np.sin(th)
    g = np.zeros((P, RET_HEADS, SEQ + P), np.float64)
    for hd in range(RET_HEADS):
        log_g = math.log(1.0 - 2.0 ** (-5.0 - hd))
        r = n[None, :] - p[:, None]
        g[:, hd, 0:SEQ] = np.where(r >= 0, np.exp(log_g * np.maximum(r, 0)), 0.0)
        r = p[None, :] - p[:, None]
        g[:, hd, SEQ:] = np.where(r >= 0, np.exp(log_g * np.maximum(r, 0)), 0.0)
    return c, d.astype(f), g.reshape(P, N_DECAY).astype(f)


_DIRECT = ["x", "ctx", "ada_w", "mlp_w1", "mlp_w2", "w_in", "w_out_mix", "w_out_fourier", "fox_w_in_2", "fox_b_f_2",
           "fox_w_out_2", "ret_w_in_2", "ret_w_out_2", "expert_w_gu_2", "expert_w_down_2"]


def layout(inputs):
    get = {k: np.asarray(v) for k, v in inputs.items()}
    arrays = {k: np.ascontiguousarray(get[k]) for k in _DIRECT}
    arrays["vec1"] = np.concatenate([get[k].reshape(-1, P) for k in ("c", "c_ctx", "ada_b", "ret_gn_gain_2")])
    arrays["vec2"] = np.concatenate([get[k].reshape(-1, P) for k in
                                     ("ln_g", "ln_b", "norm_mix_2", "norm_ffn_2", "norm_final_2", "subln_g", "conv_w")])
    arrays["rows"] = np.concatenate([get["lambda_qk"].reshape(1, -1)] + [
        get[k][l].reshape(1, -1) for l in range(DEPTH) for k in ("router_group_b_2", "router_expert_b_2")], axis=1)
    arrays["router_w"] = np.concatenate([get["router_group_w_2"], get["router_expert_w_2"]], axis=2)
    arrays["consts"], arrays["dft"], arrays["decay"] = constants()
    return arrays


def declare(nc, arrays):
    A = {k: nc.dram_tensor(f"in_{k}", v.shape, mybir.dt.from_np(v.dtype), kind="ExternalInput").ap()
         for k, v in arrays.items()}
    return A, nc.dram_tensor("out_0", (1, SEQ, D), mybir.dt.float32, kind="ExternalOutput").ap()


def kernel(**inputs):
    import concourse.bacc as bacc
    from concourse.bass_utils import run_bass_kernel_spmd as run
    nc = bacc.Bacc("TRN2", target_bir_lowering=False, num_devices=1)
    arrays = layout(inputs)
    A, out = declare(nc, arrays)
    build(nc, A, out)
    r = run(nc, [{f"in_{k}": v for k, v in arrays.items()}], core_ids=[0])
    return r.results[0]["out_0"]
```

```python
import math
from contextlib import ExitStack

import numpy as np

import concourse.bass as bass
from concourse import mybir

P = 128
D = 1024
KT = D // P
SEQ = 256
TT = SEQ // P
GRID_W = 64
DEPTH = 2
D_CONV = 512
N_DIFF = 4
DIFF_QK = 64
FF = 4 * D
FOX_HEADS = 16
FOX_DIM = D // FOX_HEADS
RET_HEADS = 4
RET_V_TILES = 4
E = 32
GROUPS = 4
EPG = E // GROUPS
EXPERT_FF = 512
SLOTS = 64
PAIRS = E // 2
FURTHER = SEQ // SLOTS - 1
ROUND_KEY = E * SLOTS
ALPHA = (2.0 * DEPTH) ** 0.25
LN_EPS, SUBLN_EPS = 1e-6, 1e-5
LAM_INIT = 0.8 - 0.6 * math.exp(-0.3 * 0)
CHUNK = 256
RING = 4
BANKS = 8
SH1, SC1, G1, SH2, SC2, G2 = (KT * i for i in range(6))

CONSTS = {}
_at = 0
for _name, _n in [("ident", P), ("ones", P), ("mean_d", P), ("mean_v", P), ("mean_gn", P), ("swap", P),
                  ("causal", P), ("before", P), ("iota", P), ("eps", 2), ("fold", 2), ("rope_cos", SEQ), ("rope_sin", SEQ),
                  ("ret_cos", SEQ), ("ret_sin", SEQ)]:
    CONSTS[_name] = (_at, _n)
    _at += _n
N_CONST = _at
N_DFT = 2 * P + 4 * SEQ
N_DECAY = RET_HEADS * (SEQ + P)

VEC1 = {"c": 0, "c_ctx": 8, "ada_b": 16, "gn": 112}
VEC2 = {"ln_g": 0, "ln_b": 32, "mix": 64, "ffn": 80, "final": 96, "subln": 104, "conv": 105}
N_VEC2 = 117
ROW_ROUTER = 256
N_ROW = 256 + DEPTH * (GROUPS + E)
NR = GROUPS + E

TILES = {}
_at = 0
for _name, _n in ([("vecs", 2), ("x", 4), ("ctx", 4), ("u", 1), ("ada_0", 4), ("u_var", 1), ("uc", 1), ("ada_1", 4),
                   ("uc_var", 1), ("w_in", 32), ("w_kv", 16), ("rope", 8), ("attn", 52), ("ada_11", 4), ("mix", 8), ("post1_0", 2), ("mod2_0", 2), ("w1_0", 32), ("w2_0", 8),
                   ("post2_0", 2), ("mod1_1", 2), ("dft_in", 8), ("dft_out", 8), ("fourier", 8), ("post1_1", 2),
                   ("mod2_1", 2), ("w1_1", 32), ("w2_1", 8), ("post2_1", 2),
                   ("fox_norm", 1), ("forget", 1), ("fox_in", 32), ("fox_attn", 40), ("fox_out", 8),
                   ("moe_norm_0", 1), ("router_0", 2), ("hn_0", 4), ("combine_0", 4),
                   ("ret_norm", 1), ("ret_in", 48), ("ret_scores", 4), ("ret_pv", 8), ("gn_mean", 4), ("gn_var", 4),
                   ("ret_out", 8), ("moe_norm_1", 1), ("router_1", 2), ("hn_1", 4), ("combine_1", 4),
                   ("final_norm", 1), ("final", 4)]):
    TILES[_name] = _at
    _at += _n


def build(nc, A, out):
    f32, f32r, i32, u32 = mybir.dt.float32, mybir.dt.float32r, mybir.dt.int32, mybir.dt.uint32
    ALU, ACT, AX = mybir.AluOpType, mybir.ActivationFunctionType, mybir.AxisListType
    ds = bass.ds

    with ExitStack() as ctx:
        start_of = {}

        def sb(name, shape, dt=f32):
            start_of[name] = -(-nc.sbuf_base // 32) * 32
            return ctx.enter_context(nc.sbuf_tensor(name, shape, dt))[tuple(slice(None) for _ in shape)]

        sems = {}

        def S(name):
            if name not in sems:
                sems[name] = ctx.enter_context(nc.semaphore(name))
            return sems[name]

        dense_w = sb("dense_w", [P, RING, KT, CHUNK])
        expert_w = sb("expert_w", [P, 6, KT * 512])
        h = sb("h", [P, KT, SEQ])
        u = sb("u", [P, KT, SEQ])
        work = sb("work", [P, 11776])
        const = sb("const", [P, N_CONST])
        vec = sb("vec", [P, P + N_VEC2])
        mod = sb("mod", [P, DEPTH, 6 * KT, 2])
        cond = work[:, D:D + KT * 32].rearrange("p (k n) -> p k n", k=KT)
        ada_rows = work[:, 0:D].rearrange("p (q n) -> p q n", q=2)
        rowbc = sb("rowbc", [P, N_ROW])
        rows_in = sb("rows_in", [1, N_ROW])
        router_w = sb("router_w", [P, DEPTH, KT, NR])
        forget_w = sb("forget_w", [P, KT, FOX_HEADS])
        forget_b = sb("forget_b", [FOX_HEADS, 1])
        small = sb("small", [P, 136])
        ps = [ctx.enter_context(nc.psum_tensor(f"bank{b}", [P, 512], f32)) for b in range(BANKS)]

        ew = expert_w[:, :, :].rearrange("p s n -> p (s n)")

        def K(name, n=None):
            at, w = CONSTS[name]
            return const[:, at:at + (n or w)]

        def part(t, at, *shape):
            n = int(np.prod(shape))
            v = t[:, at:at + n]
            if len(shape) == 2:
                return v.rearrange("p (a b) -> p a b", a=shape[0])
            if len(shape) == 3:
                return v.rearrange("p (a b c) -> p a b c", a=shape[0], b=shape[1])
            return v

        wk = work[:, :]
        resid = part(wk, 0, KT, SEQ)
        centered = part(wk, 2048, KT, SEQ)
        squares = part(wk, 4096, KT, SEQ)
        pd = part(wk, 6144, TT, 512)
        rstd = part(wk, 7168, SEQ)
        sq_o = part(wk, 7424, SEQ)
        rope_a = part(wk, 7680, SEQ)
        rope_b = part(wk, 7936, SEQ)
        dft = part(wk, 8192, N_DFT)
        vrow1 = part(wk, 9728, P)
        vrow2 = part(wk, 9856, P)
        x_tok = part(ew, 0, TT, D)
        ctx_tok = part(ew, 2048, TT, D)
        ctxT = part(ew, 4096, KT, SEQ)
        uc = part(ew, 6144, KT, SEQ)
        proj = part(ew, 8192, 16, SEQ)
        kraw = part(ew, 12288, 4, SEQ)
        qrot = part(ew, 13312, 4, SEQ)
        kall = part(ew, 14336, 4, 512)
        v_all = part(ew, 16384, 4, 512)
        cat = part(ew, 18432, KT, SEQ)
        pdT = part(ew, 20480, 2, 4, SEQ)
        expd = part(ew, 22528, 2, 2, 512)
        dft_mid = part(ew, 16384, KT, TT, 256)
        spectrum = part(ew, 20480, KT, SEQ)
        def parts(name, place, at, shape):
            t = nc.alloc_sbuf_tensor_at(name, [P] + shape, f32r, offset=start_of[place] + 4 * at)
            return t[tuple(slice(None) for _ in range(len(shape) + 1))]
        w_high = parts("w_high", "expert_w", 0, [RING, KT * CHUNK])
        w_low = parts("w_low", "dense_w", 0, [RING, KT, CHUNK])
        hidden = part(ew, 8192, 32, SEQ)
        hidden_low = parts("hidden_low", "expert_w", 8192, [32, SEQ])
        hidden_high = parts("hidden_high", "expert_w", 16384, [32, SEQ])
        u_parts = {"mlp": (parts("u_high_mlp", "work", 4096, [KT, SEQ]), parts("u_low_mlp", "work", 0, [KT, SEQ])),
                   "second": (parts("u_high", "expert_w", 8192, [KT, SEQ]), parts("u_low", "expert_w", 10240, [KT, SEQ]))}
        fq = part(ew, 16384, 16, SEQ)
        fv = part(ew, 20480, TT, D)
        fgate = part(ew, 22528, KT, SEQ)
        fexp = part(wk, 6144, 2, 384)
        fpT = part(wk, 6912, 2, 384)
        cum = part(wk, 8192, SEQ)[0:FOX_HEADS, :]
        ncum = part(wk, 8448, SEQ)[0:FOX_HEADS, :]
        flog = part(wk, 8704, 4, SEQ)[0:FOX_HEADS]
        hn_tok = part(wk, 0, TT, D)
        xg = part(wk, 2048, KT, P)
        xg_more = part(wk, 3072, KT, P)
        sil = part(wk, 4096, 512)
        hid = part(wk, 4608, 512)
        hidT = part(wk, 5120, 4, P)
        y_sb = part(wk, 5632, D)
        pick = part(wk, 6656, TT, P)
        pick_w = part(wk, 6912, TT, P)
        pick_more = part(wk, 7168, TT, P)
        pick_w_more = part(wk, 7424, TT, P)
        pick_wT = part(wk, 7680, TT, P)
        is_first = part(wk, 7936, TT, P)
        is_second = part(wk, 8192, TT, P)
        first_w = part(wk, 8448, TT, P)
        out_tok = part(wk, 8704, TT, D)
        rgate = part(wk, 0, 16, SEQ)
        ro = part(wk, 4096, 16, SEQ)
        rraw = ro
        rtmp = part(wk, 8192, 8, SEQ)
        r_s = part(wk, 8192, RET_HEADS, 384)
        decay = part(wk, 10240, RET_HEADS, 384)
        gn_rstd = part(wk, 10240, RET_HEADS, SEQ)
        rv = part(ew, 16384, TT, 2048)
        rqk = part(ew, 20480, 16, SEQ)
        lg = sb("lg", [P, TT, NR])
        pad8 = sb("pad8", [P, TT, 8])
        top = sb("top", [P, 4, 8])
        topi = sb("topi", [P, 4, 8], u32)
        e_in = sb("e_in", [P, TT, 8])
        pick_e = part(wk, 10752, 3, TT, E)
        pos = part(wk, 10944, TT, E)
        e_sum = part(wk, 11008, 4, E)
        pos_e = part(wk, 11136, TT, E)
        rt = sb("rt", [P, 40])
        rel = sb("rel", [P, 2, TT])
        rel_more = sb("rel_more", [P, 2, TT])
        more_i = sb("more_i", [P, 2 * PAIRS], i32)
        zrow = sb("zrow", [P, E])
        onehot_g = sb("onehot_g", [P, TT, GROUPS])

        tile_ready = S("tile_ready")
        evacuated = [S(f"evacuated_{b}") for b in range(BANKS)]
        dense_in = [S(f"dense_in_{j}") for j in range(RING)]
        expert_in = [S(f"expert_in_{j}") for j in range(6)]
        expert_used = S("expert_used")
        kgroup_used = S("kgroup_used")

        def bank(t):
            return ps[t % BANKS]

        def wait_tile(eng, t):
            eng.wait_ge(tile_ready, t + 1)

        def wait_evac(eng, t):
            eng.wait_ge(evacuated[t % BANKS], t // BANKS + 1)

        def open_bank(pe, t, i=0):
            if t >= BANKS:
                pe.wait_ge(evacuated[t % BANKS], t // BANKS + i)

        def evac(ins, t):
            return ins.then_inc(evacuated[t % BANKS], 1)

        FIRST = [("ada", 0), ("ada", 1), ("w_in", 0), ("ada", 2), ("ada", 3), ("w_in", 1), ("ada", 4), ("ada", 5),
                 ("w_in", 2)] + [("ada", r) for r in range(6, 6 * DEPTH)] + [("mix", 0)]

        def ada_tile(r):
            if r < 2:
                return TILES[f"ada_{r}"]
            if r < 6:
                return TILES["w_in"] + 16 * ((r - 2) // 2) + 8 + 4 * (r % 2)
            if r < 7 + N_DIFF:
                return TILES["attn"] + diff_start(r - 6) + diff_size(r - 6)
            return TILES["ada_11"]

        def in_tile(n):
            return TILES["w_in"] + 16 * (n // 8) + n % 8

        DENSE = []
        n_rot = len(FIRST) - 1
        kg = 0
        for name, w, rot, wide, tile in [
                ("mix", A["w_out_mix"][0], 1, 0, "mix"),
                ("w1_0", A["mlp_w1"][0], 4, 0, "w1_0"), ("w2_0", A["mlp_w2"][0], 4, 1, "w2_0"),
                ("fourier", A["w_out_fourier"][0], 1, 0, "fourier"),
                ("w1_1", A["mlp_w1"][1], 4, 0, "w1_1"), ("w2_1", A["mlp_w2"][1], 4, 1, "w2_1"),
                ("fox_in", A["fox_w_in_2"][0], 4, 0, "fox_in"), ("fox_out", A["fox_w_out_2"][0], 1, 0, "fox_out"),
                ("ret_in", A["ret_w_in_2"][0], 6, 0, "ret_in"), ("ret_out", A["ret_w_out_2"][0], 2, 1, "ret_out")]:
            DENSE.append(dict(name=name, w=w, rot=rot, wide=wide, tile=tile, rot0=n_rot, kg0=kg))
            n_rot += rot
            kg += 4 * (rot - 1) * wide
        DN = {m["name"]: m for m in DENSE}

        split0 = {}
        for m in DENSE:
            if m["name"] in ("w1_0", "w2_0", "w1_1", "w2_1", "fox_in", "ret_in"):
                split0[m["name"]] = 4 * sum(DN[n]["rot"] for n in split0)

        def wait_release(sp, m, i, j):
            last = isinstance(i, int) and i == m["rot"] - 1
            if m["wide"] and not last:
                sp.wait_ge(kgroup_used, m["kg0"] + 4 * i + j + 1)
            elif m["wide"]:
                sp.wait_ge(tile_ready, TILES[m["tile"]] + 2 * j + 2)
            else:
                sp.wait_ge(tile_ready, TILES[m["tile"]] + 8 * i + 2 * j + 2)

        def wait_chunk(pe, m, i, j):
            pe.wait_ge(dense_in[j], 16 * (m["rot0"] + i + 1))

        def split_high(act, name, i, j):
            wait_chunk(act, DN[name], i, j)
            nc.scalar.activation(w_high[:, j, :], dense_w[:, j].rearrange("p k n -> p (k n)"), ACT.Copy).then_inc(
                S("w_high_ready"), 1)

        def split_low(dve, name, i, j):
            dve.wait_ge(S("w_high_ready"), split0[name] + 4 * i + j + 1)
            flat = dense_w[:, j].rearrange("p k n -> p (k n)")
            nc.vector.tensor_tensor(w_low[:, j].rearrange("p k n -> p (k n)"), flat, w_high[:, j, :].bitcast(f32), ALU.subtract).then_inc(
                S("w_split"), 1)

        def ahead(name, after, i, j):
            i, j = i + (j + 2) // RING, (j + 2) % RING
            if isinstance(i, int) and i == DN[name]["rot"]:
                return (after, 0, j) if after else None
            return name, i, j

        def wait_first_release(sp, name, i, j):
            if name == "ada":
                sp.wait_ge(tile_ready, ada_tile(i) + j // 2 + 1)
            elif i < 2:
                sp.wait_ge(tile_ready, in_tile(8 * i + 2 * j + 1) + 1)
            else:
                sp.wait_ge(tile_ready, TILES["w_kv"] + 4 * j + 4)

        block = ctx.enter_context(nc.Block())

        @block.sync
        def _(sp):
            def load_chunk(m, i, j):
                w = m["w"]
                if m["wide"]:
                    src = w[ds(i * D, D), j * CHUNK:(j + 1) * CHUNK]
                else:
                    src = w[:, ds(i * RING * CHUNK + j * CHUNK, CHUNK)]
                sp.dma_start(dense_w[:, j], src.rearrange("(k p) n -> p k n", p=P)).then_inc(dense_in[j], 16)

            def first_rotation(n):
                for j in range(RING):
                    if n:
                        wait_release(sp, DENSE[n - 1], DENSE[n - 1]["rot"] - 1, j)
                    load_chunk(DENSE[n], 0, j)

            def other_rotations(n):
                m = DENSE[n]
                if m["rot"] > 1:
                    with sp.Fori(1, m["rot"]) as i:
                        for j in range(RING):
                            wait_release(sp, m, i - 1, j)
                            load_chunk(m, i, j)

            def load_expert(l, pair, slot):
                e, half = 2 * pair + slot % 2, slot // 2
                if half < 2:
                    src = A["expert_w_gu_2"][l, ds(e, 1), :, half * 512:(half + 1) * 512].rearrange(
                        "a (k p) n -> p (a k) n", p=P)
                    dst = expert_w[:, slot].rearrange("p (k n) -> p k n", k=KT)
                else:
                    src = A["expert_w_down_2"][l, ds(e, 1), :, :].rearrange("a (k p) n -> p (a k) n", p=P)
                    dst = expert_w[:, slot].rearrange("p (k n) -> p k n", k=4)
                sp.dma_start(dst, src).then_inc(expert_in[slot], 16)

            sp.dma_start(const[:, :], A["consts"]).then_inc(S("in_const"), 16)
            sp.dma_start(x_tok, A["x"][0].rearrange("(t p) d -> p t d", p=P)).then_inc(S("in_x"), 16)
            sp.dma_start(ctx_tok, A["ctx"][0].rearrange("(t p) d -> p t d", p=P)).then_inc(S("in_ctx"), 16)
            for n, (name, i) in enumerate(FIRST):
                w = {"ada": A["ada_w"][i // 6], "w_in": A["w_in"][0], "mix": A["w_out_mix"][0]}[name]
                for j in range(RING):
                    if n:
                        wait_first_release(sp, *FIRST[n - 1], j)
                    c0 = (i % 6) * RING * CHUNK + j * CHUNK
                    sp.dma_start(dense_w[:, j], w[:, c0:c0 + CHUNK].rearrange("(k p) n -> p k n", p=P)).then_inc(dense_in[j], 16)
            n_of = {m["name"]: n for n, m in enumerate(DENSE)}
            for name in ("w1_0", "w2_0", "fourier", "w1_1", "w2_1"):
                first_rotation(n_of[name])
                other_rotations(n_of[name])
            for name in ("fox_in", "fox_out"):
                first_rotation(n_of[name])
                other_rotations(n_of[name])
            wait_tile(sp, TILES["fox_in"] + 31)
            for slot in range(4):
                load_expert(0, 0, slot)
            first_rotation(n_of["ret_in"])
            for l in range(DEPTH):
                wait_tile(sp, TILES["fox_out"] + 7 if l == 0 else TILES["gn_var"] + 3)
                for slot in (4, 5):
                    load_expert(l, 0, slot)
                with sp.Fori(1, PAIRS) as i:
                    for slot in range(6):
                        sp.wait_ge(expert_used, 3 * PAIRS * l + 3 * (i - 1) + slot // 2 + 1)
                        load_expert(l, i, slot)
                if l == 0:
                    other_rotations(n_of["ret_in"])
                    for q in range(4):
                        wait_evac(sp, TILES["combine_0"] + q)
                    sp.dma_start(decay, A["decay"].rearrange("p (a b) -> p a b", a=RET_HEADS)).then_inc(S("in_decay"), 16)
                    first_rotation(n_of["ret_out"])
                    wait_tile(sp, TILES["ret_in"] + 47)
                    for slot in range(4):
                        load_expert(1, 0, slot)
                    other_rotations(n_of["ret_out"])
            for t in range(TT):
                sp.wait_ge(S("out_act"), t + 1)
                sp.wait_ge(S("out_dve"), t + 1)
                sp.dma_start(out[0, t * P:(t + 1) * P, :], out_tok[:, t]).then_inc(S("out_stored"), 16)
            sp.wait_ge(S("out_stored"), 16 * TT)

        @block.tensor
        def _(pe):
            mm = nc.tensor.matmul
            ident = K("ident")

            def linear(name, tile, rot, rhs, at=0, hook=None, dyn=None):
                m = DN[name]

                def rotation(i):
                    for j in range(RING):
                        wait_chunk(pe, m, at + i, j)
                        for n in range(2):
                            t = tile + 2 * j + n
                            open_bank(pe, t, i)
                            for k in range(KT):
                                if hook is not None:
                                    hook(j, n, k)
                                last = mm(bank(t)[:, 0:SEQ], dense_w[:, j, k, n * P:(n + 1) * P], rhs[:, k, :],
                                          start=k == 0, stop=k == KT - 1)
                            last.then_inc(tile_ready, 1)
                if rot == 1:
                    rotation(0)
                else:
                    if hook is not None:
                        rotation(0)
                        hook = None
                        with pe.Fori(1, rot) as i:
                            rotation(i)
                    else:
                        with pe.Fori(0, rot) as i:
                            rotation(i)

            def token_major(name, tile, rot, at, lhs, tts):
                m = DN[name]

                def rotation(i):
                    for j in range(RING):
                        wait_chunk(pe, m, at + i, j)
                        for tt in range(tts):
                            t = tile + j * tts + tt
                            open_bank(pe, t, i)
                            for k in range(KT):
                                last = mm(bank(t)[:, 0:CHUNK], lhs[:, k, tt * P:(tt + 1) * P], dense_w[:, j, k, :],
                                          start=k == 0, stop=k == KT - 1)
                            last.then_inc(tile_ready, 1)
                if rot == 1:
                    rotation(0)
                else:
                    with pe.Fori(0, rot) as i:
                        rotation(i)

            def three(out, w_part, x_part, hook, start=True, stop=True, tokens_still=False):
                for p, (wp, xp) in enumerate(((0, 0), (1, 0), (0, 1))):
                    for k in range(KT):
                        if hook is not None:
                            hook(p, k)
                        w, x = w_part(wp, k), x_part(xp, k)
                        last = mm(out, x if tokens_still else w, w if tokens_still else x,
                                  start=start and p == 0 and k == 0, stop=stop and p == 2 and k == KT - 1)
                return last

            def w_at(j, k, part, lo, hi):
                return w_low[:, j, k, lo:hi] if part else w_high[:, j, k * CHUNK + lo:k * CHUNK + hi]

            def linear_split(name, tile, rot, x, at=0, norm=None):
                def rotation(i, norm):
                    for j in range(RING):
                        pe.wait_ge(S("w_split"), split0[name] + 4 * (at + i) + j + 1)
                        for n in range(2):
                            t = tile + 2 * j + n
                            open_bank(pe, t, i)

                            def hook(p, k):
                                if norm and j == 0 and n == 0 and p != 1:
                                    pe.wait_ge(S(f"{norm}_low" if p else f"{norm}_high"), k + 1)
                            three(bank(t)[:, 0:SEQ], lambda part, k: w_at(j, k, part, n * P, (n + 1) * P),
                                  lambda part, k: x[part][:, k, :], hook).then_inc(tile_ready, 1)
                if norm:
                    rotation(0, norm)
                    with pe.Fori(1, rot) as i:
                        rotation(i, None)
                elif rot == 1:
                    rotation(0, None)
                else:
                    with pe.Fori(0, rot) as i:
                        rotation(i, None)

            def token_major_split(name, tile, rot, at, x):
                def rotation(i):
                    for j in range(RING):
                        pe.wait_ge(S("w_split"), split0[name] + 4 * (at + i) + j + 1)
                        for tt in range(TT):
                            t = tile + j * TT + tt
                            open_bank(pe, t, i)
                            three(bank(t)[:, 0:CHUNK], lambda part, k: w_at(j, k, part, 0, CHUNK),
                                  lambda part, k: x[part][:, k, tt * P:(tt + 1) * P], None,
                                  tokens_still=True).then_inc(tile_ready, 1)
                if rot == 1:
                    rotation(0)
                else:
                    with pe.Fori(0, rot) as i:
                        rotation(i)

            def wide_split(name, tile, x, groups, ready):
                def group(g, start, stop):
                    for j in range(RING):
                        pe.wait_ge(S("w_split"), split0[name] + 4 * g + j + 1)
                        for n in range(2):
                            t = tile + 2 * j + n
                            if start:
                                open_bank(pe, t)

                            def x_part(part, k):
                                at = g * KT + k
                                if isinstance(at, int):
                                    return x[part][:, at, :]
                                return x[part][:, ds(at, 1), :].rearrange("p a n -> p (a n)")
                            last = three(bank(t)[:, 0:SEQ], lambda part, k: w_at(j, k, part, n * P, (n + 1) * P), x_part,
                                         None, start, stop)
                            if stop:
                                last.then_inc(tile_ready, 1)
                        if not stop:
                            last.then_inc(kgroup_used, 1)
                ready(0)
                group(0, True, False)
                with pe.Fori(1, groups - 1) as g:
                    ready(g)
                    group(g, False, False)
                ready(groups - 1)
                group(groups - 1, False, True)

            def wide(name, tile, rhs, groups, ready):
                m = DN[name]

                def group(g, start, stop):
                    for j in range(RING):
                        wait_chunk(pe, m, g, j)
                        for n in range(2):
                            t = tile + 2 * j + n
                            if start:
                                open_bank(pe, t)
                            for k in range(KT):
                                at = g * KT + k
                                rh = rhs[:, at, :] if isinstance(at, int) else rhs[:, ds(at, 1), :].rearrange("p a n -> p (a n)")
                                last = mm(bank(t)[:, 0:SEQ], dense_w[:, j, k, n * P:(n + 1) * P],
                                          rh, start=start and k == 0, stop=stop and k == KT - 1)
                            if stop:
                                last.then_inc(tile_ready, 1)
                        if not stop:
                            last.then_inc(kgroup_used, 1)
                ready(0)
                group(0, True, False)
                if groups > 2:
                    with pe.Fori(1, groups - 1) as g:
                        ready(g)
                        group(g, False, False)
                ready(groups - 1)
                group(groups - 1, False, True)

            def stat(t, weights, src, tiles, ready):
                open_bank(pe, t)
                for k in range(tiles):
                    ready(k)
                    last = mm(bank(t)[:, 0:SEQ], weights, src[:, k, :], start=k == 0, stop=k == tiles - 1)
                last.then_inc(tile_ready, 1)

            def squares_ready(name):
                def ready(k):
                    if k % 4 == 0:
                        pe.wait_ge(S(f"{name}_squares"), k // 4 + 1)
                return ready

            def layer_norm(name, src, ready, between=None):
                t = TILES[name]
                stat(t, K("mean_d"), src, KT, ready)
                if between is not None:
                    between()
                stat(TILES[f"{name}_var"] if between is not None else t + 1, K("mean_d"), squares, KT, squares_ready(name))

            def rms_norm(name):
                stat(TILES[name], K("mean_d"), squares, KT, squares_ready(name))

            def normed(name):
                def hook(j, n, k):
                    if j == 0 and n == 0:
                        pe.wait_ge(S(f"{name}_out"), k + 1)
                return hook

            pe.wait_ge(S("in_const"), 16)
            pe.wait_ge(S("in_small"), 16 * 3)
            t = TILES["vecs"]
            nc.tensor.transpose(bank(t)[:, 0:P], vrow1, ident)
            nc.tensor.transpose(bank(t)[:, P:P + N_VEC2], vrow2[0:N_VEC2, :], ident[0:N_VEC2, 0:N_VEC2]).then_inc(tile_ready, 1)
            mm(bank(t + 1)[:, 0:N_ROW], K("ones")[0:1, :], rows_in[0:1, :], start=True, stop=True).then_inc(tile_ready, 1)
            for src, name in ((x_tok, "x"), (ctx_tok, "ctx")):
                pe.wait_ge(S(f"in_{name}"), 16)
                for q in range(4):
                    t = TILES[name] + q
                    open_bank(pe, t)
                    for k in range(2):
                        for tt in range(TT):
                            last = nc.tensor.transpose(bank(t)[:, k * SEQ + tt * P:k * SEQ + (tt + 1) * P],
                                                       src[:, tt, (2 * q + k) * P:(2 * q + k + 1) * P], ident)
                    last.then_inc(tile_ready, 1)
            def ada(t, at, i=0):
                for q in range(2):
                    open_bank(pe, t + q, 2 * i)
                    for j in (2 * q, 2 * q + 1):
                        pe.wait_ge(dense_in[j], 16 * (at + 1))
                        for k in range(KT):
                            g = 32 * (k % 4)
                            last = mm(bank(t + q)[g:g + 32, (j % 2) * CHUNK:(j % 2 + 1) * CHUNK], cond[:, k, :], dense_w[:, j, k, :],
                                      start=k < 4, stop=k >= 4)
                    last.then_inc(tile_ready, 1)
                for q in range(2):
                    open_bank(pe, t + 2 + q, 2 * i)
                    pe.wait_ge(evacuated[(t + q) % BANKS], (t + q) // BANKS + 1 + 2 * i)
                    for n in range(4):
                        last = mm(bank(t + 2 + q)[:, 2 * n:2 * n + 2], ada_rows[:, q, n * P:(n + 1) * P], K("fold"),
                                  start=True, stop=True)
                    last.then_inc(tile_ready, 1)

            def x_ready(name):
                def ready(k):
                    if k % 2 == 0:
                        wait_evac(pe, TILES[name] + k // 2)
                return ready
            pe.wait_ge(S("cond_ready"), 1)
            layer_norm("u", h, x_ready("x"), lambda: ada(ada_tile(0), 0))
            layer_norm("uc", ctxT, x_ready("ctx"), lambda: ada(ada_tile(1), 1))
            W = TILES["w_in"]
            with pe.Fori(0, 2) as i:
                for j in range(RING):
                    pe.wait_ge(dense_in[j], 16 * (3 * i + 3))
                    for n in range(2):
                        t = W + 2 * j + n
                        open_bank(pe, t, 2 * i)
                        for k in range(KT):
                            normed("u")(j, n, k)
                            last = mm(bank(t)[:, 0:SEQ], dense_w[:, j, k, n * P:(n + 1) * P], u[:, k, :],
                                      start=k == 0, stop=k == KT - 1)
                        last.then_inc(tile_ready, 1)
                for s in range(2):
                    ada(W + 8 + 4 * s, 3 * i + 3 + s, i)
            W = TILES["w_kv"]
            pe.wait_ge(S("uc_out"), KT)
            for j in range(2):
                pe.wait_ge(dense_in[j], 16 * (FIRST.index(("w_in", 2)) + 1))
                for n in range(2):
                    for s, src in enumerate((u, uc)):
                        t = W + 4 * j + 2 * n + s
                        open_bank(pe, t)
                        for k in range(KT):
                            last = mm(bank(t)[:, 0:SEQ], dense_w[:, j, k, n * P:(n + 1) * P], src[:, k, :],
                                      start=k == 0, stop=k == KT - 1)
                        last.then_inc(tile_ready, 1)
            for j in (2, 3):
                pe.wait_ge(dense_in[j], 16 * (FIRST.index(("w_in", 2)) + 1))
                for tt in range(4):
                    t = W + 8 + 4 * (j - 2) + tt
                    open_bank(pe, t)
                    src = (u, uc)[tt // 2]
                    for k in range(KT):
                        last = mm(bank(t)[:, 0:CHUNK], src[:, k, (tt % 2) * P:(tt % 2 + 1) * P], dense_w[:, j, k, :],
                                  start=k == 0, stop=k == KT - 1)
                    last.then_inc(tile_ready, 1)
            for n in range(8):
                t = TILES["rope"] + n
                if n < 4:
                    wait_evac(pe, in_tile(12 + n))
                else:
                    wait_evac(pe, W + 2 * (n - 4))
                open_bank(pe, t)
                src = proj[:, 12 + n, :] if n < 4 else kraw[:, n - 4, :]
                mm(bank(t)[:, 0:SEQ], K("swap"), src, start=True, stop=True).then_inc(tile_ready, 1)
            for n in range(8):
                wait_evac(pe, W + 8 + n)
            T0 = TILES["attn"]
            for step in range(N_DIFF + 1):
                if step < N_DIFF:
                    pe.wait_ge(S("rope_out"), step + 1)
                    pe.wait_ge(S("rope_out"), N_DIFF + step + 1)
                    for qt in range(TT):
                        for c in range(2):
                            t = T0 + diff_tile(step, 2 * qt + c)
                            open_bank(pe, t)
                            lo = c * DIFF_QK
                            mm(bank(t)[:, :], qrot[lo:lo + DIFF_QK, step, qt * P:(qt + 1) * P],
                               kall[lo:lo + DIFF_QK, step, :], start=True, stop=True).then_inc(tile_ready, 1)
                if step >= 1:
                    g = step - 1
                    for qt in range(TT):
                        t = T0 + diff_tile(g, 4 + qt)
                        pe.wait_ge(S("pd_ready"), 2 * g + qt + 1)
                        open_bank(pe, t)
                        for kt in range(4):
                            last = nc.tensor.transpose(bank(t)[:, kt * P:(kt + 1) * P], pd[:, qt, kt * P:(kt + 1) * P], ident)
                        last.then_inc(tile_ready, 1)
                    t = T0 + diff_tile(g, 6)
                    for qt in range(TT):
                        wait_evac(pe, T0 + diff_tile(g, 4 + qt))
                    open_bank(pe, t)
                    for kt in range(4):
                        last = mm(bank(t)[:, 0:SEQ], v_all[:, kt, g * P:(g + 1) * P], pdT[:, g % 2, kt, :],
                                  start=kt == 0, stop=kt == 3)
                    last.then_inc(tile_ready, 1)
                    t = T0 + diff_tile(g, 7)
                    pe.wait_ge(S("sub_squares"), g + 1)
                    open_bank(pe, t)
                    mm(bank(t)[:, 0:SEQ], K("mean_v"), sq_o, start=True, stop=True).then_inc(tile_ready, 1)
                ada(ada_tile(6 + step), FIRST.index(("ada", 6 + step)))
            ada(ada_tile(11), FIRST.index(("ada", 11)))
            pe.wait_ge(S("conv_out"), 4)
            for g in range(N_DIFF):
                wait_evac(pe, T0 + diff_tile(g, 6))
            linear("mix", TILES["mix"], 1, cat)

            def mlp(l):
                layer_norm(f"post1_{l}", resid, lambda k: wait_evac(pe, TILES["mix" if l == 0 else "fourier"] + k))
                layer_norm(f"mod2_{l}", h, lambda k: pe.wait_ge(S(f"post1_{l}_out"), k + 1))
                linear_split(f"w1_{l}", TILES[f"w1_{l}"], 4, u_parts["mlp"], norm=f"mod2_{l}")
                wide_split(f"w2_{l}", TILES[f"w2_{l}"], (hidden_high, hidden_low), 4,
                           lambda g: pe.wait_ge(S("hidden_ready"), 16 * l + 4 * g + 4))
                layer_norm(f"post2_{l}", resid, lambda k: wait_evac(pe, TILES[f"w2_{l}"] + k))

            mlp(0)
            layer_norm("mod1_1", h, lambda k: pe.wait_ge(S("post2_0_out"), k + 1))
            pe.wait_ge(S("in_dft"), 16)
            for g in range(KT):
                t = TILES["dft_in"] + g
                pe.wait_ge(S("mod1_1_out"), g + 1)
                open_bank(pe, t)
                for tt in range(TT):
                    last = mm(bank(t)[:, tt * 256:(tt + 1) * 256], u[:, g, tt * P:(tt + 1) * P], dft[:, 0:2 * P],
                              start=True, stop=True)
                last.then_inc(tile_ready, 1)
            for g in range(KT):
                t = TILES["dft_out"] + g
                wait_evac(pe, TILES["dft_in"] + g)
                open_bank(pe, t)
                for tt in range(TT):
                    for cs in range(2):
                        at = 2 * P + (2 * cs + tt) * SEQ
                        last = mm(bank(t)[:, 0:SEQ], dft_mid[:, g, tt, cs * P:(cs + 1) * P], dft[:, at:at + SEQ],
                                  start=tt == 0 and cs == 0, stop=tt == 1 and cs == 1)
                last.then_inc(tile_ready, 1)
            linear("fourier", TILES["fourier"], 1, spectrum,
                   hook=lambda j, n, k: wait_evac(pe, TILES["dft_out"] + k) if j == 0 and n == 0 else None)
            mlp(1)

            rms_norm("fox_norm")
            t = TILES["forget"]
            open_bank(pe, t)
            pe.wait_ge(S("in_forget"), 32)
            for k in range(KT):
                pe.wait_ge(S("fox_norm_out"), k + 1)
                last = mm(bank(t)[0:FOX_HEADS, 0:SEQ], forget_w[:, k, :], u[:, k, :], start=k == 0, stop=k == KT - 1)
            last.then_inc(tile_ready, 1)
            F = TILES["fox_in"]
            linear_split("fox_in", F, 2, u_parts["second"], norm="fox_norm")
            token_major_split("fox_in", F + 16, 1, 2, u_parts["second"])
            linear_split("fox_in", F + 24, 1, u_parts["second"], at=3)
            T1 = TILES["fox_attn"]
            pe.wait_ge(S("cum_ready"), 2)
            for n in range(16):
                wait_evac(pe, F + n)
            for n in range(8):
                wait_evac(pe, F + 16 + n)
            for step in range(FOX_HEADS // 2 + 1):
                if step < FOX_HEADS // 2:
                    for a in range(2):
                        hd = 2 * step + a
                        t = T1 + fox_tile(step, a)
                        open_bank(pe, t)
                        lo = a * FOX_DIM
                        one = ident[0:FOX_HEADS, hd:hd + 1]
                        for qt, (c0, nk) in enumerate(((0, P), (P, SEQ))):
                            o = bank(t)[:, c0:c0 + nk]
                            q0 = qt * P
                            mm(o, fq[lo:lo + FOX_DIM, step, q0:q0 + P], fq[lo:lo + FOX_DIM, 8 + step, 0:nk],
                               start=True, stop=False)
                            mm(o, cum[:, q0:q0 + P], one.broadcast_to([FOX_HEADS, nk]), start=False, stop=False)
                            mm(o, one.broadcast_to([FOX_HEADS, P]), ncum[:, 0:nk], start=False, stop=False)
                            last = mm(bank(t)[:, c0 + nk - P:c0 + nk], ident, K("causal"), start=False, stop=True)
                        last.then_inc(tile_ready, 1)
                if step >= 1:
                    g = step - 1
                    for a in range(2):
                        t = T1 + fox_tile(g, 2 + a)
                        pe.wait_ge(S("fox_probs"), 2 * g + a + 1)
                        open_bank(pe, t)
                        for n in range(3):
                            last = nc.tensor.transpose(bank(t)[:, n * P:(n + 1) * P], fexp[:, a, n * P:(n + 1) * P], ident)
                        last.then_inc(tile_ready, 1)
                    t = T1 + fox_tile(g, 4)
                    open_bank(pe, t)
                    for a in range(2):
                        wait_evac(pe, T1 + fox_tile(g, 2 + a))
                        lo = a * FOX_DIM
                        c0 = (2 * g + a) * FOX_DIM
                        mm(bank(t)[lo:lo + FOX_DIM, 0:SEQ], fv[:, 0, c0:c0 + FOX_DIM], fpT[:, a, 0:SEQ],
                           start=True, stop=False)
                        last = mm(bank(t)[lo:lo + FOX_DIM, P:SEQ], fv[:, 1, c0:c0 + FOX_DIM], fpT[:, a, SEQ:SEQ + P],
                                  start=False, stop=True)
                    last.then_inc(tile_ready, 1)
            linear("fox_out", TILES["fox_out"], 1, fgate,
                   hook=lambda j, n, k: wait_evac(pe, T1 + fox_tile(k, 4)) if j == 0 and n == 0 else None)

            def experts(l):
                rms_norm(f"moe_norm_{l}")
                t = TILES[f"router_{l}"]
                open_bank(pe, t)
                pe.wait_ge(S("in_router"), 16 * DEPTH)
                pe.wait_ge(S(f"moe_norm_{l}_out"), KT)
                for tt in range(TT):
                    for k in range(KT):
                        last = mm(bank(t)[:, tt * NR:(tt + 1) * NR], u[:, k, tt * P:(tt + 1) * P], router_w[:, l, k, :],
                                  start=k == 0, stop=k == KT - 1)
                last.then_inc(tile_ready, 1)
                for q in range(4):
                    t = TILES[f"hn_{l}"] + q
                    open_bank(pe, t)
                    for n in range(4):
                        k = (q % 2) * 4 + n
                        last = nc.tensor.transpose(bank(t)[:, n * P:(n + 1) * P],
                                                   u[:, k, (q // 2) * P:(q // 2 + 1) * P], ident)
                    last.then_inc(tile_ready, 1)
                t = TILES[f"router_{l}"] + 1
                open_bank(pe, t)
                pe.wait_ge(S("choices"), l + 1)
                mm(bank(t)[:, 0:E], K("before"), pick_e[:, 2, 0, :], start=True, stop=True)
                mm(bank(t)[:, E:2 * E], K("ones"), pick_e[:, 2, 0, :], start=True, stop=False)
                mm(bank(t)[:, E:2 * E], K("before"), pick_e[:, 2, 1, :], start=False, stop=True)
                mm(bank(t)[:, 2 * E:3 * E], K("ones"), pick_e[:, 2, 0, :], start=True, stop=False)
                mm(bank(t)[:, 2 * E:3 * E], K("ones"), pick_e[:, 2, 1, :], start=False, stop=True).then_inc(tile_ready, 1)
                A0 = TILES[f"combine_{l}"]
                total, free = [bank(A0 + q) for q in range(4)], [bank(A0 + 4 + q) for q in range(4)]
                for q in range(4):
                    open_bank(pe, A0 + q)
                    mm(total[q][:, :], ident, h[:, 2 * q:2 * q + 2, :].rearrange("p k n -> p (k n)"), start=True, stop=False)
                for q in range(4):
                    wait_evac(pe, TILES[f"hn_{l}"] + q)
                wait_evac(pe, TILES[f"router_{l}"] + 1)
                for b in range(BANKS):
                    pe.wait_ge(evacuated[b], (A0 - b + BANKS - 1) // BANKS)

                def gather(source, done):
                    for k in range(KT):
                        for tt in range(TT):
                            last = mm(free[k // 4][:, (k % 4) * P:(k % 4 + 1) * P], hn_tok[:, tt, k * P:(k + 1) * P],
                                      source[:, tt, :], start=tt == 0, stop=tt == TT - 1)
                    last.then_inc(done, 1)

                def project(half, rows):
                    for k in range(KT):
                        for a in range(2):
                            w = expert_w[:, 2 * half + a].rearrange("p (k n) -> p k n", k=KT)
                            last = mm(free[half][a * SLOTS:(a + 1) * SLOTS, :], rows[:, k, a * SLOTS:(a + 1) * SLOTS],
                                      w[:, k, :], start=k == 0, stop=k == KT - 1)
                    return last

                def turn_pick(source, done):
                    for tt in range(TT):
                        last = nc.tensor.transpose(free[3][:, tt * P:(tt + 1) * P], source[:, tt, :], ident)
                    last.then_inc(done, 1)

                def turn_hidden(done):
                    for f in range(4):
                        last = nc.tensor.transpose(free[2][:, f * P:(f + 1) * P], hid[:, f * P:(f + 1) * P], ident)
                    last.then_inc(done, 1)

                def down():
                    for half in range(2):
                        for f in range(4):
                            for a in range(2):
                                w = expert_w[:, 4 + a].rearrange("p (k n) -> p k n", k=4)
                                last = mm(free[2 + half][a * SLOTS:(a + 1) * SLOTS, :], hidT[:, f, a * SLOTS:(a + 1) * SLOTS],
                                          w[:, f, half * 512:(half + 1) * 512], start=f == 0, stop=f == 3)
                    return last

                def add_up(done):
                    for k in range(KT):
                        last = mm(total[k // 2][:, (k % 2) * SEQ:(k % 2 + 1) * SEQ], y_sb[:, k * P:(k + 1) * P],
                                  pick_wT.rearrange("p t n -> p (t n)"), start=False, stop=False)
                    last.then_inc(done, 1)

                pe.wait_ge(S("pick_ready"), (PAIRS + 1) * l + 1)
                gather(pick, S("gathered"))
                pe.wait_ge(S(f"more_known_{l}"), 1)
                with pe.Fori(0, PAIRS) as i:
                    n = PAIRS * l + i
                    pe.wait_ge(S("xg_act"), (PAIRS + 1) * l + i + 1)
                    pe.wait_ge(S("xg_dve"), (PAIRS + 1) * l + i + 1)
                    n_more = pe.value_load(more_i[0:1, ds(i, 1)], min_val=0, max_val=FURTHER)
                    before = pe.value_load(more_i[0:1, ds(i + PAIRS, 1)], min_val=0, max_val=2 * SEQ // SLOTS)
                    with pe.Fori(0, FURTHER) as r:
                        with pe.If(r < n_more):
                            c = before + r
                            pe.wait_ge(S(f"more_pick_ready_{l}"), c + 1)
                            gather(pick_more, S(f"more_gathered_{l}"))
                            pe.wait_ge(S(f"more_xg_act_{l}"), c + 1)
                            pe.wait_ge(S(f"more_xg_dve_{l}"), c + 1)
                            for a in range(2):
                                pe.wait_ge(expert_in[a], 16 * (n + 1))
                            project(0, xg_more).then_inc(S(f"more_gate_{l}"), 1)
                            for a in range(2):
                                pe.wait_ge(expert_in[2 + a], 16 * (n + 1))
                            project(1, xg_more).then_inc(S(f"more_up_{l}"), 1)
                            turn_pick(pick_w_more, S(f"more_pick_turned_{l}"))
                            pe.wait_ge(S(f"more_hidden_{l}"), c + 1)
                            turn_hidden(S(f"more_hidden_turned_{l}"))
                            pe.wait_ge(S(f"more_hidT_{l}"), c + 1)
                            pe.wait_ge(S(f"more_pick_wT_{l}"), c + 1)
                            for a in range(2):
                                pe.wait_ge(expert_in[4 + a], 16 * (n + 1))
                            down().then_inc(S(f"more_down_{l}"), 1)
                            pe.wait_ge(S(f"more_y_act_{l}"), c + 1)
                            pe.wait_ge(S(f"more_y_dve_{l}"), c + 1)
                            add_up(S(f"more_added_{l}"))
                    for a in range(2):
                        pe.wait_ge(expert_in[a], 16 * (n + 1))
                    project(0, xg).then_inc(expert_used, 1)
                    for a in range(2):
                        pe.wait_ge(expert_in[2 + a], 16 * (n + 1))
                    project(1, xg).then_inc(expert_used, 1)
                    pe.wait_ge(S("pick_w_ready"), (PAIRS + 1) * l + i + 1)
                    turn_pick(pick_w, S("pick_turned"))
                    pe.wait_ge(S("hidden_e"), n + 1)
                    turn_hidden(S("hidden_turned"))
                    pe.wait_ge(S("hidT_ready"), n + 1)
                    pe.wait_ge(S("pick_wT_ready"), n + 1)
                    for a in range(2):
                        pe.wait_ge(expert_in[4 + a], 16 * (n + 1))
                    down().then_inc(expert_used, 1)
                    pe.wait_ge(S("pick_ready"), (PAIRS + 1) * l + i + 2)
                    gather(pick, S("gathered"))
                    pe.wait_ge(S("y_act"), n + 1)
                    pe.wait_ge(S("y_dve"), n + 1)
                    add_up(S("added"))
                for q in range(4):
                    mm(total[q][:, 0:2], ident, zrow[:, 0:2], start=False, stop=True).then_inc(tile_ready, 1)
                pe.wait_ge(S("xg_act"), (PAIRS + 1) * (l + 1))
                pe.wait_ge(S("xg_dve"), (PAIRS + 1) * (l + 1))
            experts(0)
            rms_norm("ret_norm")
            R = TILES["ret_in"]
            linear_split("ret_in", R, 2, u_parts["second"], norm="ret_norm")
            token_major_split("ret_in", R + 16, 2, 2, u_parts["second"])
            linear_split("ret_in", R + 32, 2, u_parts["second"], at=4)
            pe.wait_ge(S("rotated"), 2)
            for hd in range(RET_HEADS):
                t = TILES["ret_scores"] + hd
                open_bank(pe, t)
                for jt, (c0, i0, n) in enumerate(((0, 0, SEQ), (SEQ, P, P))):
                    for s in range(2):
                        last = mm(bank(t)[:, c0:c0 + n], rqk[:, 8 + 2 * hd + s, jt * P:(jt + 1) * P],
                                  rqk[:, 2 * hd + s, i0:i0 + n], start=s == 0, stop=s == 1)
                last.then_inc(tile_ready, 1)
            for n in range(16):
                wait_evac(pe, R + 16 + n)
            for n in range(8):
                t = TILES["ret_pv"] + n
                hd = n // 2
                open_bank(pe, t)
                wait_evac(pe, TILES["ret_scores"] + hd)
                for s in range(2):
                    c0 = (2 * n + s) * P
                    mm(bank(t)[:, s * SEQ:(s + 1) * SEQ], rv[:, 0, c0:c0 + P], r_s[:, hd, 0:SEQ], start=True, stop=False)
                    last = mm(bank(t)[:, s * SEQ + P:(s + 1) * SEQ], rv[:, 1, c0:c0 + P], r_s[:, hd, SEQ:SEQ + P],
                              start=False, stop=True)
                last.then_inc(tile_ready, 1)
            for hd in range(RET_HEADS):
                stat(TILES["gn_mean"] + hd, K("mean_gn"), ro[:, 4 * hd:4 * hd + 4, :], 4,
                     lambda k: wait_evac(pe, TILES["ret_pv"] + 2 * hd + k // 2))
            for hd in range(RET_HEADS):
                stat(TILES["gn_var"] + hd, K("mean_gn"), rqk[:, 4 * hd:4 * hd + 4, :], 4,
                     lambda k: pe.wait_ge(S("gn_squares"), hd + 1))
            wide("ret_out", TILES["ret_out"], rgate, 2, lambda g: pe.wait_ge(S("ret_gated"), 8 * g + 8))
            experts(1)
            rms_norm("final_norm")
            pe.wait_ge(S("final_norm_out"), KT)
            for q in range(4):
                t = TILES["final"] + q
                open_bank(pe, t)
                for n in range(4):
                    k = (q % 2) * 4 + n
                    last = nc.tensor.transpose(bank(t)[:, n * P:(n + 1) * P], u[:, k, (q // 2) * P:(q // 2 + 1) * P], ident)
                last.then_inc(tile_ready, 1)

        @block.scalar
        def _(act):
            fn = nc.scalar.activation

            def copy_out(t, dst, src, func=None, scale=1.0):
                wait_tile(act, t)
                return evac(fn(dst, src, func or ACT.Copy, scale=scale), t)

            def square(name, src, waits):
                waits()
                for half in range(2):
                    s = slice(4 * half, 4 * half + 4)
                    fn(squares[:, s, :], src[:, s, :], ACT.Square).then_inc(S(f"{name}_squares"), 1)

            def deviation(dst, t, eps=0):
                wait_tile(act, t)
                at = CONSTS["eps"][0] + eps
                evac(fn(dst, bank(t)[:, 0:SEQ], ACT.Sqrt, bias=const[:, at:at + 1]), t)

            def ln_squares(name, between=None):
                square(name, centered, lambda: wait_evac(act, TILES[name]))
                if between is not None:
                    between()
                deviation(rstd, TILES[f"{name}_var"] if between is not None else TILES[name] + 1)

            def take_ada(t, i=0):
                for q in range(2):
                    act.wait_ge(tile_ready, t + q + 1 + 16 * i)
                    evac(fn(ada_rows[:, q, :], bank(t + q)[:, :], ACT.Copy), t + q)

            def rms_squares(name, waits):
                square(name, h, waits)
                deviation(rstd, TILES[name])

            def high_of_u(name, where):
                for k in range(KT):
                    act.wait_ge(S(f"{name}_out"), k + 1)
                    fn(u_parts[where][0][:, k, :], u[:, k, :], ACT.Copy).then_inc(S(f"{name}_high"), 1)

            def split_ahead(name, after, i, j):
                a = ahead(name, after, i, j)
                if a:
                    split_high(act, *a)

            act.dma_start(vrow1, A["vec1"]).then_inc(S("in_small"), 16)
            act.dma_start(vrow2[0:N_VEC2, :], A["vec2"]).then_inc(S("in_small"), 16)
            act.dma_start(rows_in[:, :], A["rows"]).then_inc(S("in_small"), 16)
            act.dma_start(dft, A["dft"]).then_inc(S("in_dft"), 16)
            for l in range(DEPTH):
                act.dma_start(router_w[:, l], A["router_w"][l].rearrange("(k p) n -> p k n", p=P)).then_inc(S("in_router"), 16)
            act.dma_start(forget_w[:, :, :], A["fox_w_in_2"][0, :, 4 * D:4 * D + FOX_HEADS].rearrange(
                "(k p) n -> p k n", p=P)).then_inc(S("in_forget"), 16)
            act.dma_start(forget_b[:, :], A["fox_b_f_2"].rearrange("a n -> n a")).then_inc(S("in_forget"), 16)

            wait_evac(act, TILES["vecs"])
            act.wait_ge(S("cond_zero"), 1)
            fn(cond[:, :, 0:2], vec[:, 0:16].rearrange("p (a k) -> p k a", a=2), ACT.Silu).then_inc(S("cond_ready"), 1)
            for q in range(4):
                copy_out(TILES["ctx"] + q, ctxT[:, 2 * q:2 * q + 2, :],
                         bank(TILES["ctx"] + q)[:, :].rearrange("p (k n) -> p k n", k=2))
            ln_squares("u", lambda: take_ada(ada_tile(0)))
            ln_squares("uc", lambda: take_ada(ada_tile(1)))
            W = TILES["w_in"]
            with act.Fori(0, 2) as i:
                for j in range(8):
                    t = W + j
                    act.wait_ge(tile_ready, t + 16 * i + 1)
                    evac(fn(proj[:, ds(8 * i + j, 1), :].rearrange("p a n -> p (a n)"), bank(t)[:, 0:SEQ], ACT.Copy), t)
                for s in range(2):
                    take_ada(W + 8 + 4 * s, i)
            W = TILES["w_kv"]
            for n in range(4):
                copy_out(W + 2 * n, kraw[:, n, :], bank(W + 2 * n)[:, 0:SEQ])
                copy_out(W + 1 + 2 * n, kall[:, n, SEQ:2 * SEQ], bank(W + 1 + 2 * n)[:, 0:SEQ])
            for n in range(8):
                copy_out(W + 8 + n, v_all[:, n % 4, (n // 4) * CHUNK:(n // 4 + 1) * CHUNK], bank(W + 8 + n)[:, 0:CHUNK])
            act.wait_ge(S("lam_sums"), 2)
            fn(small[:, 4:6], small[:, 0:2], ACT.Exp).then_inc(S("lam_exps"), 1)
            T0 = TILES["attn"]
            for step in range(N_DIFF + 1):
                if step < N_DIFF:
                    for n in range(4):
                        t = T0 + diff_tile(step, n)
                        qt, c = n // 2, n % 2
                        act.wait_ge(S("diff_max"), 4 * step + n + 1)
                        if step:
                            act.wait_ge(S("pd_ready"), 2 * (step - 1) + qt + 1)
                        evac(fn(expd[:, qt, c, :], bank(t)[:, :], ACT.Exp, bias=small[:, 16 + n:17 + n],
                                accum_out=small[:, 24 + n:25 + n]), t)
                if step >= 1:
                    g = step - 1
                    for qt in range(TT):
                        t = T0 + diff_tile(g, 4 + qt)
                        copy_out(t, pdT[:, g % 2, :, qt * P:(qt + 1) * P],
                                 bank(t)[:, :].rearrange("p (k n) -> p k n", k=4))
                    t = T0 + diff_tile(g, 6)
                    wait_tile(act, t)
                    if g:
                        wait_tile(act, T0 + diff_tile(g - 1, 7))
                    fn(sq_o, bank(t)[:, 0:SEQ], ACT.Square).then_inc(S("sub_squares"), 1)
                    if g:
                        wait_evac(act, T0 + diff_tile(g - 1, 6))
                    deviation(rstd, T0 + diff_tile(g, 7), 1)
                take_ada(ada_tile(6 + step))
            take_ada(ada_tile(11))

            def mlp(l):
                w1, w2 = f"w1_{l}", f"w2_{l}"
                for j in range(2):
                    split_high(act, w1, 0, j)
                ln_squares(f"post1_{l}")
                ln_squares(f"mod2_{l}")
                high_of_u(f"mod2_{l}", "mlp")

                def rotation(i):
                    for j in range(RING):
                        split_ahead(w1, w2, i, j)
                        for n in (2 * j, 2 * j + 1):
                            t = TILES[w1] + n
                            act.wait_ge(tile_ready, t + 8 * i + 1)
                            evac(fn(hidden[:, ds(8 * i + n, 1), :].rearrange("p a n -> p (a n)"), bank(t)[:, 0:SEQ], ACT.Relu), t)
                        act.wait_ge(S("hidden_done"), 16 * l + 4 * i + j + 1)
                        at = ds(8 * i + 2 * j, 2)
                        fn(hidden_high[:, at, :], hidden[:, at, :], ACT.Copy).then_inc(S("hidden_high"), 1)
                with act.Fori(0, 3) as i:
                    rotation(i)
                rotation(3)
                for j in (2, 3):
                    split_high(act, w2, 0, j)
                with act.Fori(1, 4) as i:
                    for j in range(RING):
                        split_high(act, w2, i, j)
                ln_squares(f"post2_{l}")

            mlp(0)
            ln_squares("mod1_1")
            for g in range(KT):
                t = TILES["dft_in"] + g
                copy_out(t, dft_mid[:, g], bank(t)[:, :].rearrange("p (t n) -> p t n", t=TT))
            mlp(1)

            for j in range(2):
                split_high(act, "fox_in", 0, j)
            rms_squares("fox_norm", lambda: act.wait_ge(S("post2_1_out"), KT))
            high_of_u("fox_norm", "second")
            for j in (2, 3):
                split_high(act, "fox_in", 0, j)
            t = TILES["forget"]
            act.wait_ge(S("forget_abs"), 1)
            fn(flog[:, 1, :], flog[:, 0, :], ACT.Exp, scale=-1.0).then_inc(S("forget_exp"), 1)
            act.wait_ge(S("forget_one"), 1)
            fn(flog[:, 1, :], flog[:, 1, :], ACT.Ln).then_inc(S("forget_ln"), 1)
            F = TILES["fox_in"]
            for i in range(4):
                for j in range(RING):
                    if (i, j) >= (0, 2):
                        split_ahead("fox_in", None, i, j)
                    for n in (2 * j, 2 * j + 1):
                        t = F + 8 * i + n
                        if i < 2:
                            copy_out(t, fq[:, 8 * i + n, :], bank(t)[:, 0:SEQ], scale=1.0 if i else FOX_DIM ** -0.5)
                        elif i == 2:
                            copy_out(t, fv[:, n % 2, j * CHUNK:(j + 1) * CHUNK], bank(t)[:, 0:CHUNK])
                        else:
                            copy_out(t, fgate[:, n, :], bank(t)[:, 0:SEQ], ACT.Sigmoid)
            T1 = TILES["fox_attn"]
            for step in range(FOX_HEADS // 2 + 1):
                if step < FOX_HEADS // 2:
                    for a in range(2):
                        t = T1 + fox_tile(step, a)
                        act.wait_ge(S("fox_max"), 2 * (2 * step + a) + 2)
                        if step:
                            wait_tile(act, T1 + fox_tile(step - 1, 2 + a))
                        for qt, (c0, nk) in enumerate(((0, P), (P, SEQ))):
                            last = fn(fexp[:, a, c0:c0 + nk], bank(t)[:, c0:c0 + nk], ACT.Exp,
                                      bias=small[:, 32 + 2 * a + qt:33 + 2 * a + qt],
                                      accum_out=small[:, 36 + 2 * a + qt:37 + 2 * a + qt])
                        evac(last, t)
                if step >= 1:
                    g = step - 1
                    for a in range(2):
                        t = T1 + fox_tile(g, 2 + a)
                        if g:
                            wait_tile(act, T1 + fox_tile(g - 1, 4))
                        copy_out(t, fpT[:, a, :], bank(t)[:, 0:384])

            def experts(l):
                rms_squares(f"moe_norm_{l}", (lambda: [wait_evac(act, TILES["fox_out"] + n) for n in range(8)]) if l == 0 else
                       (lambda: [wait_evac(act, TILES["ret_out"] + n) for n in range(8)]))
                act.wait_ge(S("group_max"), TT * (l + 1))
                for tt in range(TT):
                    fn(rt[:, 0 + 4 * tt:4 + 4 * tt], lg[:, tt, 0:GROUPS], ACT.Exp, bias=rt[:, 8 + tt:9 + tt],
                       accum_out=rt[:, 10 + tt:11 + tt]).then_inc(S("group_exp"), 1)
                act.wait_ge(S("second_gap"), l + 1)
                fn(rt[:, 14:16], rt[:, 12:14], ACT.Exp).then_inc(S("second_exp"), 1)
                for q in (0, 2):
                    t = TILES[f"hn_{l}"] + q
                    copy_out(t, hn_tok[:, q // 2, 0:512], bank(t)[:, :])

                free = [bank(TILES[f"combine_{l}"] + 4 + q) for q in range(4)]

                def silu(done):
                    fn(sil, free[0][:, :], ACT.Silu).then_inc(done, 1)

                def take_xg(rows, done):
                    fn(rows[:, 0:4, :], free[0][:, :].rearrange("p (k n) -> p k n", k=4), ACT.Copy).then_inc(done, 1)

                def take_hidT(done):
                    fn(hidT, free[2][:, :].rearrange("p (f n) -> p f n", f=4), ACT.Copy).then_inc(done, 1)

                def take_y(done):
                    fn(y_sb[:, 0:512], free[2][:, :], ACT.Copy).then_inc(done, 1)

                act.wait_ge(S("gathered"), (PAIRS + 1) * l + 1)
                take_xg(xg, S("xg_act"))
                act.wait_ge(S(f"more_known_{l}"), 1)
                with act.Fori(0, PAIRS) as i:
                    n = PAIRS * l + i
                    n_more = act.value_load(more_i[0:1, ds(i, 1)], min_val=0, max_val=FURTHER)
                    before = act.value_load(more_i[0:1, ds(i + PAIRS, 1)], min_val=0, max_val=2 * SEQ // SLOTS)
                    with act.Fori(0, FURTHER) as r:
                        with act.If(r < n_more):
                            c = before + r
                            act.wait_ge(S(f"more_gathered_{l}"), c + 1)
                            take_xg(xg_more, S(f"more_xg_act_{l}"))
                            act.wait_ge(S(f"more_gate_{l}"), c + 1)
                            silu(S(f"more_silu_{l}"))
                            act.wait_ge(S(f"more_hidden_turned_{l}"), c + 1)
                            take_hidT(S(f"more_hidT_{l}"))
                            act.wait_ge(S(f"more_down_{l}"), c + 1)
                            take_y(S(f"more_y_act_{l}"))
                    act.wait_ge(expert_used, 3 * n + 1)
                    silu(S("silu_e"))
                    act.wait_ge(S("hidden_turned"), n + 1)
                    take_hidT(S("hidT_ready"))
                    act.wait_ge(expert_used, 3 * n + 3)
                    take_y(S("y_act"))
                    act.wait_ge(S("gathered"), (PAIRS + 1) * l + i + 2)
                    take_xg(xg, S("xg_act"))
                for q in (0, 2):
                    t = TILES[f"combine_{l}"] + q
                    wait_tile(act, t)
                    evac(fn(h[:, 2 * q:2 * q + 2, :], bank(t)[:, :].rearrange("p (k n) -> p k n", k=2), ACT.Copy), t)

            experts(0)
            for j in range(2):
                split_high(act, "ret_in", 0, j)
            rms_squares("ret_norm", lambda: [wait_evac(act, TILES["combine_0"] + q) for q in range(4)])
            high_of_u("ret_norm", "second")
            R = TILES["ret_in"]
            for i in range(6):
                for j in range(RING):
                    split_ahead("ret_in", None, i, j)
                    for n in (2 * j, 2 * j + 1):
                        t = R + 8 * i + n
                        if i < 2:
                            copy_out(t, rraw[:, 8 * i + n, :], bank(t)[:, 0:SEQ], scale=(D // RET_HEADS) ** -0.5 if i else 1.0)
                        elif i < 4:
                            c0 = (4 * (i - 2) + j) * CHUNK
                            copy_out(t, rv[:, n % 2, c0:c0 + CHUNK], bank(t)[:, 0:CHUNK])
                        else:
                            copy_out(t, rgate[:, 8 * (i - 4) + n, :], bank(t)[:, 0:SEQ], ACT.Silu)
            for n in range(8):
                t = TILES["ret_pv"] + n
                copy_out(t, ro[:, 2 * n:2 * n + 2, :], bank(t)[:, :].rearrange("p (k n) -> p k n", k=2))
            for hd in range(RET_HEADS):
                wait_evac(act, TILES["gn_mean"] + hd)
                fn(rqk[:, 4 * hd:4 * hd + 4, :], ro[:, 4 * hd:4 * hd + 4, :], ACT.Square).then_inc(S("gn_squares"), 1)
            for hd in range(RET_HEADS):
                deviation(gn_rstd[:, hd, :], TILES["gn_var"] + hd)
            experts(1)
            rms_squares("final_norm", lambda: [wait_evac(act, TILES["combine_1"] + q) for q in range(4)])
            for q in (0, 2):
                t = TILES["final"] + q
                wait_tile(act, t)
                fn(out_tok[:, q // 2, 0:512], bank(t)[:, :], ACT.Copy).then_inc(S("out_act"), 1)

        @block.vector
        def _(dve):
            V = nc.vector
            chain = S("dve_chain")
            n_chain = [0]

            def link(ins):
                n_chain[0] += 1
                ins.then_inc(chain, 1)
                dve.wait_ge(chain, n_chain[0])

            def over_tiles(v, n):
                return v.unsqueeze(1).broadcast_to([P, n, SEQ])

            def inv_std(dst, t):
                wait_evac(dve, t)
                link(V.reciprocal(dst, dst))

            def low_of_u(name, where):
                high, low = u_parts[where]
                for k in range(KT):
                    dve.wait_ge(S(f"{name}_high"), k + 1)
                    V.tensor_tensor(low[:, k, :], u[:, k, :], high[:, k, :].bitcast(f32), ALU.subtract).then_inc(S(f"{name}_low"), 1)

            def split_ahead(name, after, i, j):
                a = ahead(name, after, i, j)
                if a:
                    split_low(dve, *a)

            def standardize(name, src, dst, between=None, idle=None):
                t = TILES[name]
                wait_tile(dve, t)
                evac(V.tensor_tensor(centered, src, over_tiles(bank(t)[:, 0:SEQ], KT), ALU.subtract), t)
                wait_evac(dve, t)
                if between is not None:
                    between()
                if idle is not None:
                    idle()
                inv_std(rstd, TILES[f"{name}_var"] if between is not None else t + 1)
                link(V.tensor_tensor(dst, centered, over_tiles(rstd, KT), ALU.mult))

            def scale_shift(name, src, dst, scale, shift):
                for k in range(KT):
                    V.tensor_scalar(dst[:, k, :], src[:, k, :], scale(k), shift(k), ALU.mult, ALU.add).then_inc(S(f"{name}_out"), 1)

            def layer_norm(name, src, dst, scale, shift, idle=None):
                standardize(name, src, centered, idle=idle)
                scale_shift(name, centered, dst, scale, shift)

            def take_ada(t, r, i=0):
                for q in range(2):
                    dve.wait_ge(tile_ready, t + 3 + q + 16 * i)
                    at = 8 * r + 4 * q
                    evac(V.tensor_tensor(mod_all[:, ds(at, 4), :], bank(t + 2 + q)[:, 0:8].rearrange("p (m a) -> p m a", a=2),
                                         vec[:, ds(at + VEC1["ada_b"], 4)].unsqueeze(2).broadcast_to([P, 4, 2]), ALU.add), t + 2 + q)
                for q in range(2):
                    dve.wait_ge(evacuated[(t + 2 + q) % BANKS], (t + 2 + q) // BANKS + 1 + 2 * i)

            mod_all = mod[:, :, :, :].rearrange("p l m a -> p (l m) a")

            def rms_norm(name, gain):
                inv_std(rstd, TILES[name])
                for k in range(KT):
                    V.scalar_tensor_tensor(u[:, k, :], h[:, k, :], gain(k), rstd, ALU.mult, ALU.mult).then_inc(S(f"{name}_out"), 1)

            def vcol(at):
                return vec[:, at:at + 1]

            def mcol(l, at, c=0):
                return mod[:, l, at, c:c + 1]

            V.memset(cond[:, :, :], 0.0).then_inc(S("cond_zero"), 1)
            t = TILES["vecs"]
            wait_tile(dve, t)
            evac(V.tensor_copy(vec[:, :], bank(t)[:, 0:P + N_VEC2]), t)
            wait_tile(dve, t + 1)
            evac(V.tensor_copy(rowbc[:, :], bank(t + 1)[:, 0:N_ROW]), t + 1)
            wait_evac(dve, t)
            wait_evac(dve, t + 1)
            for n in range(2):
                V.tensor_tensor_reduce(out=small[:, 64:128], in0=rowbc[:, 128 * n:128 * n + 64],
                                       in1=rowbc[:, 128 * n + 64:128 * n + 128], scale=1.0, scalar=0.0,
                                       op0=ALU.mult, op1=ALU.add, accum_out=small[:, n:n + 1]).then_inc(S("lam_sums"), 1)
                dve.wait_ge(S("lam_sums"), n + 1)
            for q in range(4):
                t = TILES["x"] + q
                wait_tile(dve, t)
                evac(V.tensor_copy(h[:, 2 * q:2 * q + 2, :], bank(t)[:, :].rearrange("p (k n) -> p k n", k=2)), t)
            for q in range(4):
                wait_evac(dve, TILES["x"] + q)
            standardize("u", h, u, lambda: take_ada(ada_tile(0), 0))
            for q in range(4):
                wait_evac(dve, TILES["ctx"] + q)
            standardize("uc", ctxT, uc, lambda: take_ada(ada_tile(1), 1))
            link(V.tensor_scalar(mod[:, 0, SC1:SC1 + KT, :], mod[:, 0, SC1:SC1 + KT, :], 1.0, None, ALU.add))
            scale_shift("u", u, u, lambda k: mcol(0, SC1 + k), lambda k: mcol(0, SH1 + k))
            scale_shift("uc", uc, uc, lambda k: mcol(0, SC1 + k, 1), lambda k: mcol(0, SH1 + k, 1))
            with dve.Fori(0, 2) as i:
                for s in range(2):
                    take_ada(TILES["w_in"] + 8 + 4 * s, 2 * i + 2 + s, i)
            for n in range(4):
                for b in range(3):
                    wait_evac(dve, in_tile(4 * b + n))
                gb, gc, cv = (proj[:, 4 * b + n, :] for b in range(3))
                w0 = P + VEC2["conv"]
                link(V.tensor_tensor(gc, gc, cv, ALU.mult))
                link(V.tensor_scalar(cv, gc, vcol(w0 + 4 + n), None, ALU.mult))
                link(V.scalar_tensor_tensor(cv[:, 1:SEQ], gc[:, 0:SEQ - 1], vcol(w0 + n), cv[:, 1:SEQ], ALU.mult, ALU.add))
                link(V.scalar_tensor_tensor(cv[:, 0:SEQ - 1], gc[:, 1:SEQ], vcol(w0 + 8 + n), cv[:, 0:SEQ - 1], ALU.mult, ALU.add))
                V.tensor_tensor(cat[:, n, :], gb, cv, ALU.mult).then_inc(S("conv_out"), 1)
            for n in range(8):
                t = TILES["rope"] + n
                raw = proj[:, 12 + n, :] if n < 4 else kraw[:, n - 4, :]
                dst = qrot[:, n, :] if n < 4 else kall[:, n - 4, 0:SEQ]
                scale = DIFF_QK ** -0.5 if n < 4 else 1.0
                wait_tile(dve, t)
                V.scalar_tensor_tensor(rope_b, raw, scale, K("rope_cos"), ALU.mult, ALU.mult).then_inc(S("rope_cos_part"), 1)
                evac(V.scalar_tensor_tensor(rope_a, bank(t)[:, 0:SEQ], scale, K("rope_sin"), ALU.mult, ALU.mult), t)
                dve.wait_ge(S("rope_cos_part"), n + 1)
                wait_evac(dve, t)
                V.tensor_tensor(dst, rope_a, rope_b, ALU.add).then_inc(S("rope_out"), 1)
                dve.wait_ge(S("rope_out"), n + 1)
            dve.wait_ge(S("lam_exps"), 1)
            link(V.tensor_tensor(small[:, 6:7], small[:, 5:6], small[:, 4:5], ALU.subtract))
            link(V.tensor_scalar(small[:, 7:8], small[:, 6:7], LAM_INIT, None, ALU.subtract))
            link(V.tensor_scalar(small[:, 8:9], vcol(P + VEC2["subln"]), 1.0 - LAM_INIT, None, ALU.mult))
            T0 = TILES["attn"]
            for step in range(N_DIFF + 1):
                if step < N_DIFF:
                    for n in range(4):
                        t = T0 + diff_tile(step, n)
                        wait_tile(dve, t)
                        V.tensor_reduce(small[:, 16 + n:17 + n], bank(t)[:, :], AX.X, ALU.max, negate=True).then_inc(S("diff_max"), 1)
                    for qt in range(TT):
                        for c in range(2):
                            wait_evac(dve, T0 + diff_tile(step, 2 * qt + c))
                        link(V.reciprocal(small[:, 128 + 2 * qt:130 + 2 * qt], small[:, 24 + 2 * qt:26 + 2 * qt]))
                        link(V.tensor_scalar(small[:, 129 + 2 * qt:130 + 2 * qt], small[:, 129 + 2 * qt:130 + 2 * qt],
                                             small[:, 7:8], None, ALU.mult))
                        link(V.tensor_scalar(expd[:, qt, 0, :], expd[:, qt, 0, :], small[:, 128 + 2 * qt:129 + 2 * qt], None, ALU.mult))
                        if step:
                            wait_tile(dve, T0 + diff_tile(step - 1, 4 + qt))
                        V.scalar_tensor_tensor(pd[:, qt, :], expd[:, qt, 1, :], small[:, 129 + 2 * qt:130 + 2 * qt],
                                               expd[:, qt, 0, :], ALU.mult, ALU.add).then_inc(S("pd_ready"), 1)
                if step >= 1:
                    g = step - 1
                    inv_std(rstd, T0 + diff_tile(g, 7))
                    t = T0 + diff_tile(g, 6)
                    evac(V.scalar_tensor_tensor(cat[:, 4 + g, :], bank(t)[:, 0:SEQ], small[:, 8:9], rstd, ALU.mult, ALU.mult), t)
                    wait_evac(dve, t)
                take_ada(ada_tile(6 + step), 6 + step)
            take_ada(ada_tile(11), 11)
            for l, at in ((0, SC2), (1, SC1), (1, SC2)):
                link(V.tensor_scalar(mod[:, l, at:at + KT, :], mod[:, l, at:at + KT, :], 1.0, None, ALU.add))

            def residual(name, l, gate):
                link(V.tensor_scalar(resid, h[:, :, :], ALPHA, None, ALU.mult))
                for k in range(KT):
                    t = TILES[name] + k
                    wait_tile(dve, t)
                    evac(V.scalar_tensor_tensor(resid[:, k, :], bank(t)[:, 0:SEQ], mcol(l, gate + k), resid[:, k, :],
                                                ALU.mult, ALU.add), t)

            def mlp(l):
                name = "mix" if l == 0 else "fourier"
                g0, b0 = P + VEC2["ln_g"] + 16 * l, P + VEC2["ln_b"] + 16 * l
                residual(name, l, G1)
                w1, w2 = f"w1_{l}", f"w2_{l}"
                layer_norm(f"post1_{l}", resid, h, lambda k: vcol(g0 + k), lambda k: vcol(b0 + k),
                           idle=lambda: [split_low(dve, w1, 0, j) for j in range(2)])
                dve.wait_ge(S(f"post1_{l}_out"), KT)
                layer_norm(f"mod2_{l}", h, u, lambda k: mcol(l, SC2 + k), lambda k: mcol(l, SH2 + k))
                low_of_u(f"mod2_{l}", "mlp")

                def rotation(i):
                    for j in range(RING):
                        split_ahead(w1, w2, i, j)
                        for n in (2 * j, 2 * j + 1):
                            t = TILES[w1] + n
                            dve.wait_ge(evacuated[t % BANKS], t // BANKS + 1 + i)
                        v = hidden[:, ds(8 * i + 2 * j, 2), :]
                        V.tensor_tensor(v, v, v, ALU.mult).then_inc(S("hidden_done"), 1)
                        dve.wait_ge(S("hidden_high"), 16 * l + 4 * i + j + 1)
                        at = ds(8 * i + 2 * j, 2)
                        V.tensor_tensor(hidden_low[:, at, :], hidden[:, at, :], hidden_high[:, at, :].bitcast(f32),
                                        ALU.subtract).then_inc(S("hidden_ready"), 1)
                with dve.Fori(0, 3) as i:
                    rotation(i)
                rotation(3)
                for j in (2, 3):
                    split_low(dve, w2, 0, j)
                with dve.Fori(1, 4) as i:
                    for j in range(RING):
                        split_low(dve, w2, i, j)
                residual(f"w2_{l}", l, G2)
                layer_norm(f"post2_{l}", resid, h, lambda k: vcol(g0 + 8 + k), lambda k: vcol(b0 + 8 + k))
                dve.wait_ge(S(f"post2_{l}_out"), KT)

            mlp(0)
            layer_norm("mod1_1", h, u, lambda k: mcol(1, SC1 + k), lambda k: mcol(1, SH1 + k))
            for g in range(KT):
                t = TILES["dft_out"] + g
                wait_tile(dve, t)
                evac(V.tensor_copy(spectrum[:, g, :], bank(t)[:, 0:SEQ]), t)
            mlp(1)

            for j in range(2):
                split_low(dve, "fox_in", 0, j)
            rms_norm("fox_norm", lambda k: vcol(P + VEC2["mix"] + k))
            low_of_u("fox_norm", "second")
            for j in (2, 3):
                split_low(dve, "fox_in", 0, j)
            t = TILES["forget"]
            dve.wait_ge(S("in_forget"), 32)
            wait_tile(dve, t)
            evac(V.tensor_scalar(flog[:, 2, :], bank(t)[0:FOX_HEADS, 0:SEQ], forget_b[:, 0:1], None, ALU.add), t)
            wait_evac(dve, t)
            V.scalar_tensor_tensor(flog[:, 0, :], flog[:, 2, :], -1.0, flog[:, 2, :], ALU.mult, ALU.max).then_inc(S("forget_abs"), 1)
            dve.wait_ge(S("forget_abs"), 1)
            link(V.tensor_scalar(flog[:, 2, :], flog[:, 2, :], 0.0, None, ALU.min))
            link(V.memset(flog[:, 3, :], 1.0))
            dve.wait_ge(S("forget_exp"), 1)
            V.tensor_scalar(flog[:, 1, :], flog[:, 1, :], 1.0, None, ALU.add).then_inc(S("forget_one"), 1)
            dve.wait_ge(S("forget_ln"), 1)
            link(V.tensor_tensor(flog[:, 2, :], flog[:, 2, :], flog[:, 1, :], ALU.subtract))
            V.tensor_tensor_scan(cum, flog[:, 3, :], flog[:, 2, :], 0.0, ALU.mult, ALU.add).then_inc(S("cum_ready"), 1)
            dve.wait_ge(S("cum_ready"), 1)
            V.tensor_scalar(ncum, cum, -1.0, None, ALU.mult).then_inc(S("cum_ready"), 1)
            for i in range(1, 4):
                for j in range(RING):
                    split_low(dve, "fox_in", i, j)
            F, T1 = TILES["fox_in"], TILES["fox_attn"]
            for step in range(FOX_HEADS // 2 + 1):
                if step < FOX_HEADS // 2:
                    for a in range(2):
                        t = T1 + fox_tile(step, a)
                        wait_tile(dve, t)
                        for qt, (c0, nk) in enumerate(((0, P), (P, SEQ))):
                            V.tensor_reduce(small[:, 32 + 2 * a + qt:33 + 2 * a + qt], bank(t)[:, c0:c0 + nk], AX.X, ALU.max,
                                            negate=True).then_inc(S("fox_max"), 1)
                    for a in range(2):
                        wait_evac(dve, T1 + fox_tile(step, a))
                        link(V.reciprocal(small[:, 40 + 2 * a:42 + 2 * a], small[:, 36 + 2 * a:38 + 2 * a]))
                        link(V.tensor_scalar(fexp[:, a, 0:P], fexp[:, a, 0:P], small[:, 40 + 2 * a:41 + 2 * a], None, ALU.mult))
                        V.tensor_scalar(fexp[:, a, P:384], fexp[:, a, P:384], small[:, 41 + 2 * a:42 + 2 * a], None,
                                        ALU.mult).then_inc(S("fox_probs"), 1)
                if step >= 1:
                    g = step - 1
                    t = T1 + fox_tile(g, 4)
                    wait_tile(dve, t)
                    wait_evac(dve, F + 24 + g)
                    evac(V.tensor_tensor(fgate[:, g, :], fgate[:, g, :], bank(t)[:, 0:SEQ], ALU.mult), t)

            def add_to_h(name):
                for k in range(KT):
                    t = TILES[name] + k
                    wait_tile(dve, t)
                    evac(V.tensor_tensor(h[:, k, :], h[:, k, :], bank(t)[:, 0:SEQ], ALU.add), t)

            add_to_h("fox_out")

            def experts(l):
                rms_norm(f"moe_norm_{l}", lambda k: vcol(P + VEC2["ffn"] + 8 * l + k))
                if l == 0:
                    link(V.memset(zrow[:, :], 0.0))
                iota = K("iota")
                bias = rowbc[:, ROW_ROUTER + NR * l:ROW_ROUTER + NR * (l + 1)]
                t = TILES[f"router_{l}"]
                wait_tile(dve, t)
                evac(V.tensor_tensor(lg[:, :, :], bank(t)[:, 0:TT * NR].rearrange("p (t n) -> p t n", t=TT),
                                     bias.unsqueeze(1).broadcast_to([P, TT, NR]), ALU.add), t)
                wait_evac(dve, t)
                link(V.memset(pad8[:, :, :], -3.0e38))
                link(V.tensor_copy(pad8[:, :, 0:GROUPS], lg[:, :, 0:GROUPS]))
                for tt in range(TT):
                    link(V.max(top[:, tt, :], pad8[:, tt, :]))
                    link(V.max_index(topi[:, tt, :], top[:, tt, :], pad8[:, tt, :]))
                    V.tensor_scalar(rt[:, 8 + tt:9 + tt], top[:, tt, 0:1], -1.0, None, ALU.mult).then_inc(S("group_max"), 1)
                    link(V.tensor_copy(rt[:, 16 + tt:17 + tt], topi[:, tt, 0:1]))
                    link(V.tensor_scalar(onehot_g[:, tt, :], iota[:, 0:GROUPS], rt[:, 16 + tt:17 + tt], None, ALU.is_equal))
                    link(V.tensor_scalar(e_in[:, tt, :], lg[:, tt, GROUPS:GROUPS + EPG], onehot_g[:, tt, 0:1], None, ALU.mult))
                    for g in range(1, GROUPS):
                        link(V.scalar_tensor_tensor(e_in[:, tt, :], lg[:, tt, GROUPS + EPG * g:GROUPS + EPG * (g + 1)],
                                                    onehot_g[:, tt, g:g + 1], e_in[:, tt, :], ALU.mult, ALU.add))
                    link(V.max(top[:, 2 + tt, :], e_in[:, tt, :]))
                    link(V.max_index(topi[:, 2 + tt, :], top[:, 2 + tt, :], e_in[:, tt, :]))
                    link(V.tensor_tensor(rt[:, 12 + tt:13 + tt], top[:, 2 + tt, 1:2], top[:, 2 + tt, 0:1], ALU.subtract))
                    link(V.tensor_copy(rt[:, 18 + 2 * tt:20 + 2 * tt], topi[:, 2 + tt, 0:2]))
                    link(V.scalar_tensor_tensor(rt[:, 22 + 2 * tt:24 + 2 * tt], rt[:, 16 + tt:17 + tt].broadcast_to([P, 2]), float(EPG),
                                                rt[:, 18 + 2 * tt:20 + 2 * tt], ALU.mult, ALU.add))
                    for c in range(2):
                        link(V.tensor_scalar(pick_e[:, c, tt, :], iota[:, 0:E], rt[:, 22 + 2 * tt + c:23 + 2 * tt + c], None, ALU.is_equal))
                V.tensor_tensor(pick_e[:, 2, :, :], pick_e[:, 0, :, :], pick_e[:, 1, :, :], ALU.add).then_inc(S("choices"), 1)
                V.tensor_copy(rt[:, 12:14], rt[:, 12:14]).then_inc(S("second_gap"), 1)
                for q in (1, 3):
                    t = TILES[f"hn_{l}"] + q
                    wait_tile(dve, t)
                    evac(V.tensor_copy(hn_tok[:, q // 2, 512:1024], bank(t)[:, :]), t)
                t = TILES[f"router_{l}"] + 1
                wait_tile(dve, t)
                link(V.tensor_copy(pos[:, :, :], bank(t)[:, 0:TT * E].rearrange("p (t n) -> p t n", t=TT)))
                evac(V.tensor_copy(e_sum[:, 0, :], bank(t)[:, 2 * E:3 * E]), t)
                wait_evac(dve, t)
                tmp = pos_e
                for c in range(2):
                    link(V.tensor_tensor(tmp, pick_e[:, c, :, :], pos[:, :, :], ALU.mult))
                    link(V.tensor_reduce(rt[:, 26 + 2 * c:28 + 2 * c], tmp, AX.X, ALU.add))
                place = rt[:, 26:30].rearrange("p (c t) -> p c t", c=2)
                eid = rt[:, 22:26].rearrange("p (t c) -> p c t", t=TT)
                link(V.scalar_tensor_tensor(rel[:, :, :], eid, float(SLOTS), place, ALU.mult, ALU.add))
                for n in range(1, FURTHER + 1):
                    link(V.tensor_scalar(rel_more[:, :, :], place, float(n * SLOTS), float(ROUND_KEY - SLOTS), ALU.is_ge, ALU.mult))
                    link(V.tensor_tensor(rel[:, :, :], rel[:, :, :], rel_more[:, :, :], ALU.add))

                def build_pick(keys, plain, weighted, linked, plain_done, weighted_done):
                    for tt in range(TT):
                        V.tensor_scalar(is_first[:, tt, :], iota, keys[:, 0, tt:tt + 1], None, ALU.is_equal)
                        last = V.tensor_scalar(is_second[:, tt, :], iota, keys[:, 1, tt:tt + 1], None, ALU.is_equal)
                    linked(last)
                    V.tensor_tensor(plain, is_first, is_second, ALU.add).then_inc(plain_done, 1)
                    weigh(weighted, linked, weighted_done) if weighted is not None else None

                def weigh(weighted, linked, weighted_done):
                    for tt in range(TT):
                        last = V.tensor_scalar(first_w[:, tt, :], is_first[:, tt, :], rt[:, 36 + tt:37 + tt], None, ALU.mult)
                    linked(last)
                    for tt in range(TT):
                        last = V.scalar_tensor_tensor(weighted[:, tt, :], is_second[:, tt, :], rt[:, 38 + tt:39 + tt],
                                                      first_w[:, tt, :], ALU.mult, ALU.add)
                    last.then_inc(weighted_done, 1)

                build_pick(rel, pick, None, link, S("pick_ready"), None)
                link(V.tensor_scalar(rel[:, :, :], rel[:, :, :], float(-P), None, ALU.add))
                dve.wait_ge(S("group_exp"), TT * (l + 1))
                dve.wait_ge(S("second_exp"), l + 1)
                link(V.tensor_scalar(rt[:, 34:36], rt[:, 14:16], 1.0, None, ALU.add))
                link(V.tensor_tensor(rt[:, 34:36], rt[:, 34:36], rt[:, 10:12], ALU.mult))
                link(V.reciprocal(rt[:, 36:38], rt[:, 34:36]))
                link(V.tensor_tensor(rt[:, 38:40], rt[:, 36:38], rt[:, 14:16], ALU.mult))
                weigh(pick_w, link, S("pick_w_ready"))
                pair = e_sum[:, 0, :].rearrange("p (i a) -> p i a", a=2)
                crowd, more, upto = (e_sum[:, b, 0:PAIRS] for b in (1, 2, 3))
                link(V.tensor_tensor(crowd, pair[:, :, 0], pair[:, :, 1], ALU.max))
                link(V.tensor_scalar(more, crowd, float(SLOTS), None, ALU.is_gt))
                for n in range(2, FURTHER + 1):
                    link(V.scalar_tensor_tensor(more, crowd, float(n * SLOTS), more, ALU.is_gt, ALU.add))
                link(V.tensor_tensor_scan(upto, more, zrow[:, 0:PAIRS], 0.0, ALU.add, ALU.add))
                link(V.tensor_tensor(upto, upto, more, ALU.subtract))
                V.tensor_copy(more_i[:, 0:PAIRS], more)
                V.tensor_copy(more_i[:, PAIRS:2 * PAIRS], upto).then_inc(S(f"more_known_{l}"), 1)
                dve.wait_ge(S(f"more_known_{l}"), 1)
                free = [bank(TILES[f"combine_{l}"] + 4 + q) for q in range(4)]

                def make_hidden(done):
                    V.tensor_tensor(hid, sil, free[1][:, :], ALU.mult).then_inc(done, 1)

                def take_xg(rows, done):
                    V.tensor_copy(rows[:, 4:8, :], free[1][:, :].rearrange("p (k n) -> p k n", k=4)).then_inc(done, 1)

                def take_pick_wT(done):
                    V.tensor_copy(pick_wT, free[3][:, 0:SEQ].rearrange("p (t n) -> p t n", t=TT)).then_inc(done, 1)

                def take_y(done):
                    V.tensor_copy(y_sb[:, 512:1024], free[3][:, :]).then_inc(done, 1)

                dve.wait_ge(S("gathered"), (PAIRS + 1) * l + 1)
                take_xg(xg, S("xg_dve"))
                loop_chain, more_chain = S(f"pick_chain_{l}"), S(f"more_chain_{l}")
                with dve.Fori(0, PAIRS) as i:
                    n = PAIRS * l + i
                    at = [0]

                    def linked(ins):
                        at[0] += 1
                        ins.then_inc(loop_chain, 1)
                        dve.wait_ge(loop_chain, 4 * i + at[0])
                    n_more = dve.value_load(more_i[0:1, ds(i, 1)], min_val=0, max_val=FURTHER)
                    before = dve.value_load(more_i[0:1, ds(i + PAIRS, 1)], min_val=0, max_val=2 * SEQ // SLOTS)
                    V.tensor_scalar(rel_more[:, :, :], rel[:, :, :], float(P - ROUND_KEY), None, ALU.add).then_inc(loop_chain, 1)
                    at[0] += 1
                    with dve.Fori(0, FURTHER) as r:
                        with dve.If(r < n_more):
                            c = before + r
                            more_at = [0]

                            def linked_more(ins):
                                more_at[0] += 1
                                ins.then_inc(more_chain, 1)
                                dve.wait_ge(more_chain, 3 * c + more_at[0])
                            dve.wait_ge(loop_chain, 4 * i + 1)
                            build_pick(rel_more, pick_more, pick_w_more, linked_more, S(f"more_pick_ready_{l}"),
                                       S(f"more_pick_w_ready_{l}"))
                            linked_more(V.tensor_scalar(rel_more[:, :, :], rel_more[:, :, :], float(-ROUND_KEY), None, ALU.add))
                            dve.wait_ge(S(f"more_gathered_{l}"), c + 1)
                            take_xg(xg_more, S(f"more_xg_dve_{l}"))
                            dve.wait_ge(S(f"more_up_{l}"), c + 1)
                            dve.wait_ge(S(f"more_silu_{l}"), c + 1)
                            make_hidden(S(f"more_hidden_{l}"))
                            dve.wait_ge(S(f"more_pick_turned_{l}"), c + 1)
                            take_pick_wT(S(f"more_pick_wT_{l}"))
                            dve.wait_ge(S(f"more_down_{l}"), c + 1)
                            take_y(S(f"more_y_dve_{l}"))
                    dve.wait_ge(S("silu_e"), n + 1)
                    dve.wait_ge(expert_used, 3 * n + 2)
                    make_hidden(S("hidden_e"))
                    dve.wait_ge(S("pick_turned"), n + 1)
                    take_pick_wT(S("pick_wT_ready"))
                    build_pick(rel, pick, pick_w, linked, S("pick_ready"), S("pick_w_ready"))
                    linked(V.tensor_scalar(rel[:, :, :], rel[:, :, :], float(-P), None, ALU.add))
                    dve.wait_ge(expert_used, 3 * n + 3)
                    take_y(S("y_dve"))
                    dve.wait_ge(S("gathered"), (PAIRS + 1) * l + i + 2)
                    take_xg(xg, S("xg_dve"))
                for q in (1, 3):
                    t = TILES[f"combine_{l}"] + q
                    wait_tile(dve, t)
                    evac(V.tensor_copy(h[:, 2 * q:2 * q + 2, :], bank(t)[:, :].rearrange("p (k n) -> p k n", k=2)), t)
                for q in range(4):
                    wait_evac(dve, TILES[f"combine_{l}"] + q)

            for n in range(8):
                wait_evac(dve, TILES["fox_out"] + n)
            experts(0)
            for j in range(2):
                split_low(dve, "ret_in", 0, j)
            rms_norm("ret_norm", lambda k: vcol(P + VEC2["mix"] + 8 + k))
            low_of_u("ret_norm", "second")
            for j in (2, 3):
                split_low(dve, "ret_in", 0, j)
            for j in range(RING):
                split_low(dve, "ret_in", 1, j)
            R = TILES["ret_in"]
            for qk in range(2):
                for n in range(8):
                    wait_evac(dve, R + 8 * qk + n)
                raw = rraw[:, 8 * qk:8 * qk + 8, :].rearrange("p (a s) n -> p a s n", s=2)
                dst = rqk[:, 8 * qk:8 * qk + 8, :].rearrange("p (a s) n -> p a s n", s=2)
                cos, sin = over_tiles(K("ret_cos"), 4), over_tiles(K("ret_sin"), 4)
                tmp = rtmp[:, 0:4, :]
                link(V.tensor_tensor(dst[:, :, 0, :], raw[:, :, 0, :], cos, ALU.mult))
                link(V.tensor_tensor(tmp, raw[:, :, 1, :], sin, ALU.mult))
                link(V.tensor_tensor(dst[:, :, 0, :], dst[:, :, 0, :], tmp, ALU.subtract))
                link(V.tensor_tensor(dst[:, :, 1, :], raw[:, :, 1, :], cos, ALU.mult))
                link(V.tensor_tensor(tmp, raw[:, :, 0, :], sin, ALU.mult))
                V.tensor_tensor(dst[:, :, 1, :], dst[:, :, 1, :], tmp, ALU.add).then_inc(S("rotated"), 1)
                dve.wait_ge(S("rotated"), qk + 1)
                for i in ((2,), (3, 4, 5))[qk]:
                    for j in range(RING):
                        split_low(dve, "ret_in", i, j)
            dve.wait_ge(S("in_decay"), 16)
            for hd in range(RET_HEADS):
                t = TILES["ret_scores"] + hd
                wait_tile(dve, t)
                evac(V.tensor_tensor(r_s[:, hd, :], bank(t)[:, 0:384], decay[:, hd, :], ALU.mult), t)
            for hd in range(RET_HEADS):
                t = TILES["gn_mean"] + hd
                wait_tile(dve, t)
                o = ro[:, 4 * hd:4 * hd + 4, :]
                evac(V.tensor_tensor(o, o, over_tiles(bank(t)[:, 0:SEQ], 4), ALU.subtract), t)
            for hd in range(RET_HEADS):
                wait_evac(dve, TILES["ret_scores"] + hd)
                wait_evac(dve, TILES["gn_mean"] + hd)
                inv_std(gn_rstd[:, hd, :], TILES["gn_var"] + hd)
                o = ro[:, 4 * hd:4 * hd + 4, :]
                link(V.tensor_tensor(o, o, over_tiles(gn_rstd[:, hd, :], 4), ALU.mult))
                for n in range(4 * hd, 4 * hd + 4):
                    wait_evac(dve, R + 32 + n)
                    V.scalar_tensor_tensor(rgate[:, n, :], ro[:, n, :], vcol(VEC1["gn"] + n), rgate[:, n, :],
                                           ALU.mult, ALU.mult).then_inc(S("ret_gated"), 1)
            add_to_h("ret_out")
            for n in range(8):
                wait_evac(dve, TILES["ret_out"] + n)
            experts(1)
            rms_norm("final_norm", lambda k: vcol(P + VEC2["final"] + k))
            for q in (1, 3):
                t = TILES["final"] + q
                wait_tile(dve, t)
                V.tensor_copy(out_tok[:, q // 2, 512:1024], bank(t)[:, :]).then_inc(S("out_dve"), 1)


def diff_start(step):
    return 0 if step == 0 else 8 + 12 * (step - 1)


def diff_size(step):
    return 4 if step in (0, N_DIFF) else 8


def diff_tile(head, n):
    if n < 4:
        return diff_start(head) + n
    return diff_start(head + 1) + diff_size(head + 1) - 4 + n - 4


def fox_tile(pair, n):
    if n < 2:
        return (0 if pair == 0 else 2 + 5 * (pair - 1)) + n
    return (2 + 5 * pair) + (2 if pair + 1 < FOX_HEADS // 2 else 0) + n - 2


def constants():
    f = np.float32
    c = np.zeros((P, N_CONST), f)

    def put(name, v):
        at, n = CONSTS[name]
        c[:, at:at + n] = v
    p = np.arange(P)
    put("ident", np.eye(P))
    put("ones", 1.0)
    put("mean_d", 1.0 / D)
    put("mean_v", 1.0 / P)
    put("mean_gn", 1.0 / (RET_V_TILES * P))
    swap = np.zeros((P, P), f)
    for m in range(P):
        if m % 32 < 16:
            swap[m + 16, m] = -1.0
        else:
            swap[m - 16, m] = 1.0
    put("swap", swap)
    put("causal", np.where(p[None, :] <= p[:, None], 0.0, -1e30))
    put("before", (p[:, None] < p[None, :]).astype(f))
    put("iota", np.broadcast_to(p.astype(f), (P, P)))
    put("fold", np.tile(np.eye(32, 2), (4, 1)))
    put("eps", np.array([[LN_EPS, SUBLN_EPS]], f))
    n = np.arange(SEQ)
    inv = (f(10000.0) ** (-np.arange(16, dtype=f) / f(16))).astype(f)
    where = np.where((p % 64 < 32)[:, None], (n // GRID_W)[None, :], (n % GRID_W)[None, :]).astype(f)
    ang = where * inv[p % 16][:, None]
    put("rope_cos", np.cos(ang))
    put("rope_sin", np.sin(ang))
    inv = (f(1.0) / (f(10000.0) ** np.linspace(0.0, 1.0, P, dtype=f))).astype(f)
    ang = n[None, :].astype(f) * inv[:, None]
    put("ret_cos", np.cos(ang))
    put("ret_sin", np.sin(ang))
    d = np.zeros((P, N_DFT), np.float64)
    th = 2 * np.pi * np.outer(p, p) / P
    d[:, 0:P], d[:, P:2 * P] = np.cos(th), np.sin(th)
    norm = 1.0 / math.sqrt(SEQ * P)
    for tt in range(TT):
        th = 2 * np.pi * (np.outer(p + tt * P, n) % SEQ) / SEQ
        d[:, 2 * P + tt * SEQ:2 * P + (tt + 1) * SEQ] = norm * np.cos(th)
        d[:, 2 * P + (2 + tt) * SEQ:2 * P + (3 + tt) * SEQ] = -norm * np.sin(th)
    g = np.zeros((P, RET_HEADS, SEQ + P), np.float64)
    for hd in range(RET_HEADS):
        log_g = math.log(1.0 - 2.0 ** (-5.0 - hd))
        r = n[None, :] - p[:, None]
        g[:, hd, 0:SEQ] = np.where(r >= 0, np.exp(log_g * np.maximum(r, 0)), 0.0)
        r = p[None, :] - p[:, None]
        g[:, hd, SEQ:] = np.where(r >= 0, np.exp(log_g * np.maximum(r, 0)), 0.0)
    return c, d.astype(f), g.reshape(P, N_DECAY).astype(f)


_DIRECT = ["x", "ctx", "ada_w", "mlp_w1", "mlp_w2", "w_in", "w_out_mix", "w_out_fourier", "fox_w_in_2", "fox_b_f_2",
           "fox_w_out_2", "ret_w_in_2", "ret_w_out_2", "expert_w_gu_2", "expert_w_down_2"]


def layout(inputs):
    get = {k: np.asarray(v) for k, v in inputs.items()}
    arrays = {k: np.ascontiguousarray(get[k]) for k in _DIRECT}
    arrays["vec1"] = np.concatenate([get[k].reshape(-1, P) for k in ("c", "c_ctx", "ada_b", "ret_gn_gain_2")])
    arrays["vec2"] = np.concatenate([get[k].reshape(-1, P) for k in
                                     ("ln_g", "ln_b", "norm_mix_2", "norm_ffn_2", "norm_final_2", "subln_g", "conv_w")])
    arrays["rows"] = np.concatenate([get["lambda_qk"].reshape(1, -1)] + [
        get[k][l].reshape(1, -1) for l in range(DEPTH) for k in ("router_group_b_2", "router_expert_b_2")], axis=1)
    arrays["router_w"] = np.concatenate([get["router_group_w_2"], get["router_expert_w_2"]], axis=2)
    arrays["consts"], arrays["dft"], arrays["decay"] = constants()
    return arrays


def declare(nc, arrays):
    A = {k: nc.dram_tensor(f"in_{k}", v.shape, mybir.dt.from_np(v.dtype), kind="ExternalInput").ap()
         for k, v in arrays.items()}
    return A, nc.dram_tensor("out_0", (1, SEQ, D), mybir.dt.float32, kind="ExternalOutput").ap()


def kernel(**inputs):
    import concourse.bacc as bacc
    from concourse.bass_utils import run_bass_kernel_spmd as run
    nc = bacc.Bacc("TRN2", target_bir_lowering=False, num_devices=1)
    arrays = layout(inputs)
    A, out = declare(nc, arrays)
    build(nc, A, out)
    r = run(nc, [{f"in_{k}": v for k, v in arrays.items()}], core_ids=[0])
    return r.results[0]["out_0"]
```

```python
import math
from contextlib import ExitStack

import numpy as np

import concourse.bass as bass
from concourse import mybir

P = 128
D = 1024
KT = D // P
SEQ = 256
TT = SEQ // P
GRID_W = 64
DEPTH = 2
D_CONV = 512
N_DIFF = 4
DIFF_QK = 64
FF = 4 * D
FOX_HEADS = 16
FOX_DIM = D // FOX_HEADS
RET_HEADS = 4
RET_V_TILES = 4
E = 32
GROUPS = 4
EPG = E // GROUPS
EXPERT_FF = 512
WARM = 8
PAIRS = E // 2
UNIT = 32
SHARES = (UNIT, 2 * UNIT, 3 * UNIT)
SLOTS = P // 2
FURTHER = SEQ // SLOTS - 1
ROUND_KEY = PAIRS * P
ALPHA = (2.0 * DEPTH) ** 0.25
LN_EPS, SUBLN_EPS = 1e-6, 1e-5
LAM_INIT = 0.8 - 0.6 * math.exp(-0.3 * 0)
CHUNK = 256
RING = 4
BANKS = 8
SH1, SC1, G1, SH2, SC2, G2 = (KT * i for i in range(6))

CONSTS = {}
_at = 0
for _name, _n in [("ident", P), ("ones", P), ("mean_d", P), ("mean_v", P), ("mean_gn", P), ("swap", P),
                  ("causal", P), ("before", P), ("iota", P), ("eps", 2), ("fold", 2), ("rope_cos", SEQ), ("rope_sin", SEQ),
                  ("ret_cos", SEQ), ("ret_sin", SEQ)]:
    CONSTS[_name] = (_at, _n)
    _at += _n
N_CONST = _at
N_DFT = 2 * P + 4 * SEQ
N_DECAY = RET_HEADS * (SEQ + P)

VEC1 = {"c": 0, "c_ctx": 8, "ada_b": 16, "gn": 112}
VEC2 = {"ln_g": 0, "ln_b": 32, "mix": 64, "ffn": 80, "final": 96, "subln": 104, "conv": 105}
N_VEC2 = 117
ROW_ROUTER = 256
N_ROW = 256 + DEPTH * (GROUPS + E)
NR = GROUPS + E

IN_ORDER = [("w", 0), ("w", 1), ("r", 0, 0), ("w", 2), ("w", 3), ("r", 0, 1), ("w", 4), ("w", 5), ("f", 0, 0), ("f", 0, 1),
            ("r", 1, 0), ("w", 6), ("w", 7), ("r", 1, 1), ("f", 1, 0), ("f", 1, 1)]
KV_ORDER = []
for _e in IN_ORDER:
    KV_ORDER += [("w", 2 * _e[1]), ("w", 2 * _e[1] + 1)] if _e[0] == "w" else [_e]
ATTN = []
for _s in range(N_DIFF + 2):
    ATTN += [(_s, _n) for _n in range(4) if _s < N_DIFF]
    if 1 <= _s <= N_DIFF:
        ATTN += [(_s - 1, 4), (_s - 1, 5), (_s - 1, 6)]
    if _s >= 2:
        ATTN += [(_s - 2, 7)]
    if 1 <= _s <= N_DIFF:
        ATTN += [("r", _s, 0), ("r", _s, 1), ("f", _s, 0), ("f", _s, 1)]

TILES = {}
_at = 0
for _name, _n in ([("vecs", 2), ("x", 4), ("ctx", 4), ("u", 1), ("ada_0", 4), ("u_var", 1), ("uc", 1), ("ada_1", 4),
                   ("uc_var", 1), ("w_in", 32), ("w_kv", 24), ("rope", 8), ("attn", len(ATTN)), ("mix", 8), ("post1_0", 2), ("mod2_0", 2), ("w1_0", 32), ("w2_0", 8),
                   ("post2_0", 2), ("mod1_1", 2), ("dft_in", 8), ("dft_out", 8), ("fourier", 8), ("post1_1", 2),
                   ("mod2_1", 2), ("w1_1", 32), ("w2_1", 8), ("post2_1", 2),
                   ("fox_norm", 1), ("forget", 1), ("fox_in", 32), ("fox_attn", 40), ("fox_out", 8),
                   ("moe_norm_0", 1), ("router_0", 2), ("hn_0", 4), ("combine_0", 4),
                   ("ret_norm", 1), ("ret_in", 48), ("ret_scores", 4), ("ret_pv", 8), ("gn_mean", 4), ("gn_var", 4),
                   ("ret_out", 8), ("moe_norm_1", 1), ("router_1", 2), ("hn_1", 4), ("combine_1", 4),
                   ("final_norm", 1), ("final", 4)]):
    TILES[_name] = _at
    _at += _n


def build(nc, A, out):
    f32, f32r, i32, u32 = mybir.dt.float32, mybir.dt.float32r, mybir.dt.int32, mybir.dt.uint32
    ALU, ACT, AX = mybir.AluOpType, mybir.ActivationFunctionType, mybir.AxisListType
    ds = bass.ds

    with ExitStack() as ctx:
        start_of = {}

        def sb(name, shape, dt=f32):
            start_of[name] = -(-nc.sbuf_base // 32) * 32
            return ctx.enter_context(nc.sbuf_tensor(name, shape, dt))[tuple(slice(None) for _ in shape)]

        sems = {}

        def S(name):
            if name not in sems:
                sems[name] = ctx.enter_context(nc.semaphore(name))
            return sems[name]

        dense_w = sb("dense_w", [P, RING, KT, CHUNK])
        expert_w = sb("expert_w", [P, 6, KT * 512])
        h = sb("h", [P, KT, SEQ])
        u = sb("u", [P, KT, SEQ])
        work = sb("work", [P, 11776])
        const = sb("const", [P, N_CONST])
        vec = sb("vec", [P, P + N_VEC2])
        mod = sb("mod", [P, DEPTH, 6 * KT, 2])
        cond = work[:, D:D + KT * 32].rearrange("p (k n) -> p k n", k=KT)
        ada_rows = work[:, 0:D].rearrange("p (q n) -> p q n", q=2)
        rowbc = sb("rowbc", [P, N_ROW])
        rows_in = sb("rows_in", [1, N_ROW])
        router_w = sb("router_w", [P, DEPTH, KT, NR])
        forget_w = sb("forget_w", [P, KT, FOX_HEADS])
        forget_b = sb("forget_b", [FOX_HEADS, 1])
        small = sb("small", [P, 136])
        ps = [ctx.enter_context(nc.psum_tensor(f"bank{b}", [P, 512], f32)) for b in range(BANKS)]

        ew = expert_w[:, :, :].rearrange("p s n -> p (s n)")

        def K(name, n=None):
            at, w = CONSTS[name]
            return const[:, at:at + (n or w)]

        def part(t, at, *shape):
            n = int(np.prod(shape))
            v = t[:, at:at + n]
            if len(shape) == 2:
                return v.rearrange("p (a b) -> p a b", a=shape[0])
            if len(shape) == 3:
                return v.rearrange("p (a b c) -> p a b c", a=shape[0], b=shape[1])
            return v

        gate_w = [ew[:, 0:2 * KT * 512], dense_w[:, :, :, :].rearrange("p j k n -> p (j k n)")]
        wk = work[:, :]
        resid = part(wk, 0, KT, SEQ)
        centered = part(wk, 2048, KT, SEQ)
        squares = part(wk, 4096, KT, SEQ)
        pd = part(wk, 6144, TT, 512)
        rstd = part(wk, 7168, SEQ)
        sub_rstd = [part(wk, 7424, SEQ), rstd]
        rope_a = part(wk, 7680, SEQ)
        rope_b = part(wk, 7936, SEQ)
        sq_o = [rope_a, rope_b]
        dft = part(wk, 8192, N_DFT)
        vrow1 = part(wk, 9728, P)
        vrow2 = part(wk, 9856, P)
        x_tok = part(ew, 0, TT, D)
        ctx_tok = part(ew, 2048, TT, D)
        ctxT = part(ew, 4096, KT, SEQ)
        uc = part(ew, 6144, KT, SEQ)
        proj = part(ew, 8192, 16, SEQ)
        kraw = part(ew, 12288, 4, SEQ)
        qrot = [part(ew, 13312, 4, SEQ), part(wk, 10240, 4, SEQ)]
        kall = part(ew, 14336, 4, 512)
        v_all = part(ew, 16384, 4, 512)
        cat = part(ew, 18432, KT, SEQ)
        pdT = part(ew, 20480, 2, 4, SEQ)
        expd = part(ew, 22528, 2, 2, 512)
        dft_mid = part(ew, 16384, KT, TT, 256)
        spectrum = part(ew, 20480, KT, SEQ)
        def parts(name, place, at, shape):
            t = nc.alloc_sbuf_tensor_at(name, [P] + shape, f32r, offset=start_of[place] + 4 * at)
            return t[tuple(slice(None) for _ in range(len(shape) + 1))]
        w_high = parts("w_high", "expert_w", 0, [RING, KT * CHUNK])
        w_low = parts("w_low", "dense_w", 0, [RING, KT, CHUNK])
        hidden = part(ew, 8192, 32, SEQ)
        hidden_low = parts("hidden_low", "expert_w", 8192, [32, SEQ])
        hidden_high = parts("hidden_high", "expert_w", 16384, [32, SEQ])
        u_parts = {"mlp": (parts("u_high_mlp", "work", 4096, [KT, SEQ]), parts("u_low_mlp", "work", 0, [KT, SEQ])),
                   "second": (parts("u_high", "expert_w", 8192, [KT, SEQ]), parts("u_low", "expert_w", 10240, [KT, SEQ]))}
        fq = [part(ew, 12288, 8, SEQ), part(ew, 14336, 8, SEQ)]
        fk = [part(ew, 16384, 8, SEQ), part(ew, 18432, 8, SEQ)]
        PAD = [FOX_DIM, 0]
        fv = part(ew, 20480, TT, D)
        fgate = part(ew, 22528, KT, SEQ)
        fexp = part(wk, 6144, 2, 384)
        fpT = part(wk, 6912, 2, 384)
        cum = part(wk, 8192, SEQ)[0:FOX_HEADS, :]
        ncum = part(wk, 8448, SEQ)[0:FOX_HEADS, :]
        flog = part(wk, 8704, 4, SEQ)[0:FOX_HEADS]
        hn_tok = part(wk, 0, TT, D)
        xg = part(wk, 2048, KT, P)
        xg_more = part(wk, 3072, KT, P)
        sil = part(wk, 4096, 512)
        hid = part(wk, 4608, 512)
        hidT = part(wk, 5120, 4, P)
        y_sb = part(wk, 5632, D)
        pick = part(wk, 6656, TT, P)
        pick_w = part(wk, 6912, TT, P)
        pick_more = part(wk, 7168, TT, P)
        pick_w_more = part(wk, 7424, TT, P)
        pick_wT = part(wk, 7680, TT, P)
        is_first = part(wk, 7936, TT, P)
        is_second = part(wk, 8192, TT, P)
        first_w = part(wk, 8448, TT, P)
        out_tok = part(wk, 8704, TT, D)
        rgate = part(wk, 0, 16, SEQ)
        ro = part(wk, 4096, 16, SEQ)
        rraw = ro
        rtmp = part(wk, 8192, 8, SEQ)
        r_s = part(wk, 8192, RET_HEADS, 384)
        decay = part(wk, 10240, RET_HEADS, 384)
        gn_rstd = part(wk, 10240, RET_HEADS, SEQ)
        rv = part(ew, 16384, TT, 2048)
        rqk = part(ew, 20480, 16, SEQ)
        lg = sb("lg", [P, TT, NR])
        pad8 = sb("pad8", [P, TT, 8])
        top = sb("top", [P, 4, 8])
        topi = sb("topi", [P, 4, 8], u32)
        e_in = sb("e_in", [P, TT, EPG])
        pick_e = part(wk, 10752, 3, TT, E)
        pos = part(wk, 10944, TT, E)
        e_sum = part(wk, 11008, 4, E)
        room = part(wk, 11136, 2, E)
        share = part(wk, 11200, 6, PAIRS)
        of_group = part(wk, 8704, TT * EPG, GROUPS)
        over = part(wk, 8768, 2 * PAIRS, 3)
        key_first = part(wk, 8864, TT, E)
        by_choice = [part(wk, 8928 + 2 * TT * E * b, 2, TT, E) for b in range(3)]
        gone = part(wk, 9312, 2 * TT, FURTHER)
        rounds = part(wk, 9324, 2, TT)
        rt = sb("rt", [P, 40])
        rel = sb("rel", [P, 2, TT])
        rel_more = sb("rel_more", [P, 2, TT])
        more_i = sb("more_i", [P, 3 * PAIRS], i32)
        zrow = sb("zrow", [P, E])
        onehot_g = sb("onehot_g", [P, TT, GROUPS])

        tile_ready = S("tile_ready")
        evacuated = [S(f"evacuated_{b}") for b in range(BANKS)]
        dense_in = [S(f"dense_in_{j}") for j in range(RING)]
        gates_in = [S(f"gates_in_{j}") for j in range(2)]
        expert_in = [S(f"expert_in_{j}") for j in range(4)]
        expert_used = S("expert_used")
        kgroup_used = S("kgroup_used")

        def vcol(at):
            return vec[:, at:at + 1]

        def mcol(l, at, c=0):
            return mod[:, l, at, c:c + 1]

        NORMS = ["u", "uc", "post1_0", "mod2_0", "post2_0", "mod1_1", "post1_1", "mod2_1", "post2_1"]
        ALL_NORMS = NORMS + ["fox_norm", "moe_norm_0", "ret_norm", "moe_norm_1", "final_norm"]

        def norm_affine(name):
            l = int(name[-1])
            if name.startswith("mod"):
                sc, sh = (SC1, SH1) if name[3] == "1" else (SC2, SH2)
                return lambda k: mcol(l, sc + k), lambda k: mcol(l, sh + k)
            at = 16 * l + 8 * (name[4] == "2")
            return lambda k: vcol(P + VEC2["ln_g"] + at + k), lambda k: vcol(P + VEC2["ln_b"] + at + k)

        def bank(t):
            return ps[t % BANKS]

        def wait_tile(eng, t):
            eng.wait_ge(tile_ready, t + 1)

        def wait_evac(eng, t):
            eng.wait_ge(evacuated[t % BANKS], t // BANKS + 1)

        def open_bank(pe, t, i=0):
            if t >= BANKS:
                pe.wait_ge(evacuated[t % BANKS], t // BANKS + i)

        def evac(ins, t):
            return ins.then_inc(evacuated[t % BANKS], 1)

        FIRST = [("ada", r, c) for r in range(2) for c in range(RING)]
        for i in range(3):
            for j in range(RING):
                FIRST += [("w_in", i, j)] + [("ada", 2 + 2 * i + q // RING, q % RING) for q in (2 * j, 2 * j + 1)]
        FIRST += [("ada", r, c) for r in range(8, 6 * DEPTH) for c in range(RING)] + [("mix", 0, j) for j in range(RING)]

        def ada_tiles(r):
            if r < 2:
                return [TILES[f"ada_{r}"] + q for q in range(4)]
            if r < 6:
                return [TILES["w_in"] + 16 * (r // 2 - 1) + IN_ORDER.index((x, r % 2, q)) for x in "rf" for q in range(2)]
            if r < 8:
                return [TILES["w_kv"] + KV_ORDER.index((x, r % 2, q)) for x in "rf" for q in range(2)]
            return [TILES["attn"] + ATTN.index((x, r - 7, q)) for x in "rf" for q in range(2)]

        def in_tile(n):
            return TILES["w_in"] + 16 * (n // 8) + IN_ORDER.index(("w", n % 8))

        def kv_tile(n):
            return TILES["w_kv"] + KV_ORDER.index(("w", n))

        def diff_tile(head, n):
            return ATTN.index((head, n))

        DENSE = []
        n_rot = len(FIRST) // RING - 1
        kg = 0
        for name, w, rot, wide, tile in [
                ("mix", A["w_out_mix"][0], 1, 0, "mix"),
                ("w1_0", A["mlp_w1"][0], 4, 0, "w1_0"), ("w2_0", A["mlp_w2"][0], 4, 1, "w2_0"),
                ("fourier", A["w_out_fourier"][0], 1, 0, "fourier"),
                ("w1_1", A["mlp_w1"][1], 4, 0, "w1_1"), ("w2_1", A["mlp_w2"][1], 4, 1, "w2_1"),
                ("fox_in", A["fox_w_in_2"][0], 4, 0, "fox_in"), ("fox_out", A["fox_w_out_2"][0], 1, 0, "fox_out"),
                ("ret_in", A["ret_w_in_2"][0], 6, 0, "ret_in"), ("ret_out", A["ret_w_out_2"][0], 2, 1, "ret_out")]:
            DENSE.append(dict(name=name, w=w, rot=rot, wide=wide, tile=tile, rot0=n_rot, kg0=kg))
            n_rot += rot
            kg += 4 * (rot - 1) * wide
        DN = {m["name"]: m for m in DENSE}

        split0 = {}
        for m in DENSE:
            if m["name"] in ("w1_0", "w2_0", "w1_1", "w2_1", "fox_in", "ret_in"):
                split0[m["name"]] = 4 * sum(DN[n]["rot"] for n in split0)

        def wait_release(sp, m, i, j):
            last = isinstance(i, int) and i == m["rot"] - 1
            if m["wide"] and not last:
                sp.wait_ge(kgroup_used, m["kg0"] + 4 * i + j + 1)
            elif m["wide"]:
                sp.wait_ge(tile_ready, TILES[m["tile"]] + 2 * j + 2)
            else:
                sp.wait_ge(tile_ready, TILES[m["tile"]] + 8 * i + 2 * j + 2)

        def wait_chunk(pe, m, i, j):
            pe.wait_ge(dense_in[j], 16 * (m["rot0"] + i + 1))

        def split_high(act, name, i, j):
            wait_chunk(act, DN[name], i, j)
            nc.scalar.activation(w_high[:, j, :], dense_w[:, j].rearrange("p k n -> p (k n)"), ACT.Copy).then_inc(
                S("w_high_ready"), 1)

        def split_low(dve, name, i, j):
            dve.wait_ge(S("w_high_ready"), split0[name] + 4 * i + j + 1)
            flat = dense_w[:, j].rearrange("p k n -> p (k n)")
            nc.vector.tensor_tensor(w_low[:, j].rearrange("p k n -> p (k n)"), flat, w_high[:, j, :].bitcast(f32), ALU.subtract).then_inc(
                S("w_split"), 1)

        def ahead(name, after, i, j):
            i, j = i + (j + 2) // RING, (j + 2) % RING
            if isinstance(i, int) and i == DN[name]["rot"]:
                return (after, 0, j) if after else None
            return name, i, j

        def wait_first_release(sp, name, i, j):
            if name == "ada":
                sp.wait_ge(tile_ready, ada_tiles(i)[j // 2] + 1)
            elif i < 2:
                sp.wait_ge(tile_ready, in_tile(8 * i + 2 * j + 1) + 1)
            else:
                sp.wait_ge(tile_ready, kv_tile(4 * j + 3) + 1)

        block = ctx.enter_context(nc.Block())

        @block.sync
        def _(sp):
            def load_chunk(m, i, j):
                w = m["w"]
                if m["wide"]:
                    src = w[ds(i * D, D), j * CHUNK:(j + 1) * CHUNK]
                else:
                    src = w[:, ds(i * RING * CHUNK + j * CHUNK, CHUNK)]
                sp.dma_start(dense_w[:, j], src.rearrange("(k p) n -> p k n", p=P)).then_inc(dense_in[j], 16)

            def first_rotation(n):
                for j in range(RING):
                    if n:
                        wait_release(sp, DENSE[n - 1], DENSE[n - 1]["rot"] - 1, j)
                    load_chunk(DENSE[n], 0, j)

            def other_rotations(n):
                m = DENSE[n]
                if m["rot"] > 1:
                    with sp.Fori(1, m["rot"]) as i:
                        for j in range(RING):
                            wait_release(sp, m, i - 1, j)
                            load_chunk(m, i, j)

            def load_gates(l, pair, place):
                src = A["expert_w_gu_2"][l, ds(2 * pair, 2), :, 0:512].rearrange("a (k p) n -> p (a k) n", p=P)
                sp.dma_start(gate_w[place].rearrange("p (k n) -> p k n", k=2 * KT), src).then_inc(gates_in[place], 16)

            def load_expert(l, pair, slot):
                if slot < 4:
                    src = A["expert_w_gu_2"][l, ds(2 * pair + slot - 2, 1), :, 512:1024].rearrange(
                        "a (k p) n -> p (a k) n", p=P)
                else:
                    src = A["expert_w_down_2"][l, ds(2 * pair, 2), :, (slot - 4) * 512:(slot - 3) * 512].rearrange(
                        "a (k p) n -> p (a k) n", p=P)
                sp.dma_start(expert_w[:, slot].rearrange("p (k n) -> p k n", k=8), src).then_inc(expert_in[slot - 2], 16)

            def next_pair(l, pair, place, gates=True):
                used = 4 * PAIRS * l + 4 * (pair - 1)
                for slot in range(2, 6):
                    sp.wait_ge(expert_used, used + max(2, slot - 1))
                    load_expert(l, pair, slot)
                if gates:
                    sp.wait_ge(expert_used, used + 1)
                    load_gates(l, pair + 1, place)

            sp.dma_start(const[:, :], A["consts"]).then_inc(S("in_const"), 16)
            sp.dma_start(x_tok, A["x"][0].rearrange("(t p) d -> p t d", p=P)).then_inc(S("in_x"), 16)
            sp.dma_start(ctx_tok, A["ctx"][0].rearrange("(t p) d -> p t d", p=P)).then_inc(S("in_ctx"), 16)
            for at, (name, i, j) in enumerate(FIRST):
                w = {"ada": A["ada_w"][i // 6], "w_in": A["w_in"][0], "mix": A["w_out_mix"][0]}[name]
                if at >= RING:
                    wait_first_release(sp, *FIRST[at - RING])
                c0 = (i % 6) * RING * CHUNK + j * CHUNK
                sp.dma_start(dense_w[:, at % RING], w[:, c0:c0 + CHUNK].rearrange("(k p) n -> p k n", p=P)).then_inc(
                    dense_in[at % RING], 16)
            n_of = {m["name"]: n for n, m in enumerate(DENSE)}
            for name in ("w1_0", "w2_0", "fourier", "w1_1", "w2_1"):
                first_rotation(n_of[name])
                other_rotations(n_of[name])
            for name in ("fox_in", "fox_out"):
                first_rotation(n_of[name])
                other_rotations(n_of[name])
            wait_tile(sp, TILES["fox_in"] + 31)
            load_gates(0, 0, 0)
            load_expert(0, 0, 2)
            for l in range(DEPTH):
                wait_tile(sp, TILES["fox_out"] + 7 if l == 0 else TILES["gn_var"] + 3)
                for slot in (3, 4, 5) if l == 0 else (4, 5):
                    load_expert(l, 0, slot)
                m = DN["ret_out" if l else "fox_out"]
                for j in range(RING):
                    wait_release(sp, m, m["rot"] - 1, j)
                load_gates(l, 1, 1)
                sp.wait_ge(expert_used, 4 * PAIRS * l + 1)
                load_gates(l, 2, 0)
                next_pair(l, 1, None, gates=False)
                with sp.Fori(0, PAIRS // 2 - 2) as p:
                    for n in range(2):
                        next_pair(l, 2 * p + 2 + n, 1 - n)
                next_pair(l, PAIRS - 2, 1)
                next_pair(l, PAIRS - 1, None, gates=False)
                if l == 0:
                    sp.wait_ge(expert_used, 4 * PAIRS - 3)
                    first_rotation(n_of["ret_in"])
                    other_rotations(n_of["ret_in"])
                    for q in range(4):
                        wait_evac(sp, TILES["combine_0"] + q)
                    sp.dma_start(decay, A["decay"].rearrange("p (a b) -> p a b", a=RET_HEADS)).then_inc(S("in_decay"), 16)
                    first_rotation(n_of["ret_out"])
                    wait_tile(sp, TILES["ret_in"] + 47)
                    load_gates(1, 0, 0)
                    for slot in (2, 3):
                        load_expert(1, 0, slot)
                    other_rotations(n_of["ret_out"])
            for t in range(TT):
                sp.wait_ge(S("out_act"), t + 1)
                sp.wait_ge(S("out_dve"), t + 1)
                sp.dma_start(out[0, t * P:(t + 1) * P, :], out_tok[:, t]).then_inc(S("out_stored"), 16)
            sp.wait_ge(S("out_stored"), 16 * TT)

        @block.tensor
        def _(pe):
            mm = nc.tensor.matmul
            ident = K("ident")

            def linear(name, tile, rot, rhs, at=0, hook=None, dyn=None):
                m = DN[name]

                def rotation(i):
                    for j in range(RING):
                        wait_chunk(pe, m, at + i, j)
                        for n in range(2):
                            t = tile + 2 * j + n
                            open_bank(pe, t, i)
                            for k in range(KT):
                                if hook is not None:
                                    hook(j, n, k)
                                last = mm(bank(t)[:, 0:SEQ], dense_w[:, j, k, n * P:(n + 1) * P], rhs[:, k, :],
                                          start=k == 0, stop=k == KT - 1)
                            last.then_inc(tile_ready, 1)
                if rot == 1:
                    rotation(0)
                else:
                    if hook is not None:
                        rotation(0)
                        hook = None
                        with pe.Fori(1, rot) as i:
                            rotation(i)
                    else:
                        with pe.Fori(0, rot) as i:
                            rotation(i)

            def token_major(name, tile, rot, at, lhs, tts):
                m = DN[name]

                def rotation(i):
                    for j in range(RING):
                        wait_chunk(pe, m, at + i, j)
                        for tt in range(tts):
                            t = tile + j * tts + tt
                            open_bank(pe, t, i)
                            for k in range(KT):
                                last = mm(bank(t)[:, 0:CHUNK], lhs[:, k, tt * P:(tt + 1) * P], dense_w[:, j, k, :],
                                          start=k == 0, stop=k == KT - 1)
                            last.then_inc(tile_ready, 1)
                if rot == 1:
                    rotation(0)
                else:
                    with pe.Fori(0, rot) as i:
                        rotation(i)

            def three(out, w_part, x_part, hook, start=True, stop=True, tokens_still=False):
                for p, (wp, xp) in enumerate(((0, 0), (1, 0), (0, 1))):
                    for k in range(KT):
                        if hook is not None:
                            hook(p, k)
                        w, x = w_part(wp, k), x_part(xp, k)
                        last = mm(out, x if tokens_still else w, w if tokens_still else x,
                                  start=start and p == 0 and k == 0, stop=stop and p == 2 and k == KT - 1)
                return last

            def w_at(j, k, part, lo, hi):
                return w_low[:, j, k, lo:hi] if part else w_high[:, j, k * CHUNK + lo:k * CHUNK + hi]

            def linear_split(name, tile, rot, x, at=0, norm=None):
                def rotation(i, norm):
                    for j in range(RING):
                        pe.wait_ge(S("w_split"), split0[name] + 4 * (at + i) + j + 1)
                        for n in range(2):
                            t = tile + 2 * j + n
                            open_bank(pe, t, i)

                            def hook(p, k):
                                if norm and j == 0 and n == 0 and p != 1:
                                    pe.wait_ge(S(f"{norm}_low" if p else f"{norm}_high"), k + 1)
                            three(bank(t)[:, 0:SEQ], lambda part, k: w_at(j, k, part, n * P, (n + 1) * P),
                                  lambda part, k: x[part][:, k, :], hook).then_inc(tile_ready, 1)
                if norm:
                    rotation(0, norm)
                    with pe.Fori(1, rot) as i:
                        rotation(i, None)
                elif rot == 1:
                    rotation(0, None)
                else:
                    with pe.Fori(0, rot) as i:
                        rotation(i, None)

            def token_major_split(name, tile, rot, at, x):
                def rotation(i):
                    for j in range(RING):
                        pe.wait_ge(S("w_split"), split0[name] + 4 * (at + i) + j + 1)
                        for tt in range(TT):
                            t = tile + j * TT + tt
                            open_bank(pe, t, i)
                            three(bank(t)[:, 0:CHUNK], lambda part, k: w_at(j, k, part, 0, CHUNK),
                                  lambda part, k: x[part][:, k, tt * P:(tt + 1) * P], None,
                                  tokens_still=True).then_inc(tile_ready, 1)
                if rot == 1:
                    rotation(0)
                else:
                    with pe.Fori(0, rot) as i:
                        rotation(i)

            def wide_split(name, tile, x, groups, ready):
                def group(g, start, stop):
                    for j in range(RING):
                        pe.wait_ge(S("w_split"), split0[name] + 4 * g + j + 1)
                        for n in range(2):
                            t = tile + 2 * j + n
                            if start:
                                open_bank(pe, t)

                            def x_part(part, k):
                                at = g * KT + k
                                if isinstance(at, int):
                                    return x[part][:, at, :]
                                return x[part][:, ds(at, 1), :].rearrange("p a n -> p (a n)")
                            last = three(bank(t)[:, 0:SEQ], lambda part, k: w_at(j, k, part, n * P, (n + 1) * P), x_part,
                                         None, start, stop)
                            if stop:
                                last.then_inc(tile_ready, 1)
                        if not stop:
                            last.then_inc(kgroup_used, 1)
                ready(0)
                group(0, True, False)
                with pe.Fori(1, groups - 1) as g:
                    ready(g)
                    group(g, False, False)
                ready(groups - 1)
                group(groups - 1, False, True)

            def wide(name, tile, rhs, groups, ready):
                m = DN[name]

                def group(g, start, stop):
                    for j in range(RING):
                        wait_chunk(pe, m, g, j)
                        for n in range(2):
                            t = tile + 2 * j + n
                            if start:
                                open_bank(pe, t)
                            for k in range(KT):
                                at = g * KT + k
                                rh = rhs[:, at, :] if isinstance(at, int) else rhs[:, ds(at, 1), :].rearrange("p a n -> p (a n)")
                                last = mm(bank(t)[:, 0:SEQ], dense_w[:, j, k, n * P:(n + 1) * P],
                                          rh, start=start and k == 0, stop=stop and k == KT - 1)
                            if stop:
                                last.then_inc(tile_ready, 1)
                        if not stop:
                            last.then_inc(kgroup_used, 1)
                ready(0)
                group(0, True, False)
                if groups > 2:
                    with pe.Fori(1, groups - 1) as g:
                        ready(g)
                        group(g, False, False)
                ready(groups - 1)
                group(groups - 1, False, True)

            def stat(t, weights, src, tiles, ready):
                open_bank(pe, t)
                for k in range(tiles):
                    ready(k)
                    last = mm(bank(t)[:, 0:SEQ], weights, src[:, k, :], start=k == 0, stop=k == tiles - 1)
                last.then_inc(tile_ready, 1)

            def squares_ready(name):
                def ready(k):
                    if k % 2 == 0:
                        pe.wait_ge(S("squares"), 4 * ALL_NORMS.index(name) + k // 2 + 1)
                return ready

            def keep_warm(t, n):
                open_bank(pe, t)
                for _ in range(n):
                    mm(bank(t)[:, 0:SEQ], ident, K("rope_cos"), start=True, stop=True)

            def layer_norm(name, src, ready, between=None):
                t = TILES[name]
                stat(t, K("mean_d"), src, KT, ready)
                if between is not None:
                    between()
                stat(TILES[f"{name}_var"] if between is not None else t + 1, K("mean_d"), squares, KT, squares_ready(name))
                if between is None:
                    keep_warm(t + 2, WARM)

            def rms_norm(name):
                stat(TILES[name], K("mean_d"), squares, KT, squares_ready(name))
                keep_warm(TILES[name] + 1, WARM)

            def normed(name):
                def hook(j, n, k):
                    if j == 0 and n == 0:
                        pe.wait_ge(S(f"{name}_out"), k + 1)
                return hook

            pe.wait_ge(S("in_const"), 16)
            pe.wait_ge(S("in_small"), 16 * 3)
            t = TILES["vecs"]
            nc.tensor.transpose(bank(t)[:, 0:P], vrow1, ident)
            nc.tensor.transpose(bank(t)[:, P:P + N_VEC2], vrow2[0:N_VEC2, :], ident[0:N_VEC2, 0:N_VEC2]).then_inc(tile_ready, 1)
            mm(bank(t + 1)[:, 0:N_ROW], K("ones")[0:1, :], rows_in[0:1, :], start=True, stop=True).then_inc(tile_ready, 1)
            for src, name in ((x_tok, "x"), (ctx_tok, "ctx")):
                pe.wait_ge(S(f"in_{name}"), 16)
                for q in range(4):
                    t = TILES[name] + q
                    open_bank(pe, t)
                    for k in range(2):
                        for tt in range(TT):
                            last = nc.tensor.transpose(bank(t)[:, k * SEQ + tt * P:k * SEQ + (tt + 1) * P],
                                                       src[:, tt, (2 * q + k) * P:(2 * q + k + 1) * P], ident)
                    last.then_inc(tile_ready, 1)
            def ada_chunk(r, c, i=0):
                at = FIRST.index(("ada", r, c))
                t = ada_tiles(r)[c // 2]
                if c % 2 == 0:
                    open_bank(pe, t, 2 * i)
                pe.wait_ge(dense_in[at % RING], 16 * (at // RING + 1) + 48 * i)
                for k in range(KT):
                    g = 32 * (k % 4)
                    last = mm(bank(t)[g:g + 32, (c % 2) * CHUNK:(c % 2 + 1) * CHUNK], cond[:, k, :], dense_w[:, at % RING, k, :],
                              start=k < 4, stop=k >= 4)
                if c % 2:
                    last.then_inc(tile_ready, 1)

            def ada_fold(r, i=0):
                for q in range(2):
                    rows, t = ada_tiles(r)[q], ada_tiles(r)[2 + q]
                    open_bank(pe, t, 2 * i)
                    pe.wait_ge(evacuated[rows % BANKS], rows // BANKS + 1 + 2 * i)
                    for n in range(4):
                        last = mm(bank(t)[:, 2 * n:2 * n + 2], ada_rows[:, q, n * P:(n + 1) * P], K("fold"),
                                  start=True, stop=True)
                    last.then_inc(tile_ready, 1)

            def ada(r):
                for c in range(RING):
                    ada_chunk(r, c)
                ada_fold(r)

            def x_ready(name):
                def ready(k):
                    if k % 2 == 0:
                        wait_evac(pe, TILES[name] + k // 2)
                return ready
            pe.wait_ge(S("cond_ready"), 1)
            layer_norm("u", h, x_ready("x"), lambda: ada(0))
            layer_norm("uc", ctxT, x_ready("ctx"), lambda: ada(1))
            def beside(r, chunk, i=0):
                for q in (2 * chunk, 2 * chunk + 1):
                    ada_chunk(r + q // RING, q % RING, i)

            keep_warm(in_tile(0), WARM)
            with pe.Fori(0, 2) as i:
                for j in range(RING):
                    at = FIRST.index(("w_in", 0, j))
                    pe.wait_ge(dense_in[at % RING], 16 * (at // RING + 1) + 48 * i)
                    for n in range(2):
                        t = in_tile(2 * j + n)
                        open_bank(pe, t, 2 * i)
                        for k in range(KT):
                            normed("u")(j, n, k)
                            last = mm(bank(t)[:, 0:SEQ], dense_w[:, at % RING, k, n * P:(n + 1) * P], u[:, k, :],
                                      start=k == 0, stop=k == KT - 1)
                        last.then_inc(tile_ready, 1)
                    if j == 2:
                        ada_fold(2, i)
                    beside(2, j, i)
                ada_fold(3, i)
            pe.wait_ge(S("uc_out"), KT)
            for j in range(RING):
                at = FIRST.index(("w_in", 2, j))
                pe.wait_ge(dense_in[at % RING], 16 * (at // RING + 1))
                for x in range(4):
                    t = kv_tile(4 * j + x)
                    open_bank(pe, t)
                    for k in range(KT):
                        if j < 2:
                            n, src = x // 2, (u, uc)[x % 2]
                            last = mm(bank(t)[:, 0:SEQ], dense_w[:, at % RING, k, n * P:(n + 1) * P], src[:, k, :],
                                      start=k == 0, stop=k == KT - 1)
                        else:
                            src, tt = (u, uc)[x // 2], x % 2
                            last = mm(bank(t)[:, 0:CHUNK], src[:, k, tt * P:(tt + 1) * P], dense_w[:, at % RING, k, :],
                                      start=k == 0, stop=k == KT - 1)
                    last.then_inc(tile_ready, 1)
                if j == 2:
                    ada_fold(6)
                beside(6, j)
            ada_fold(7)
            for n in range(8):
                t = TILES["rope"] + n
                if n < 4:
                    wait_evac(pe, in_tile(12 + n))
                else:
                    wait_evac(pe, kv_tile(2 * (n - 4)))
                open_bank(pe, t)
                src = proj[:, 12 + n, :] if n < 4 else kraw[:, n - 4, :]
                mm(bank(t)[:, 0:SEQ], K("swap"), src, start=True, stop=True).then_inc(tile_ready, 1)
            for n in range(8):
                wait_evac(pe, kv_tile(8 + n))
            T0 = TILES["attn"]
            pe.wait_ge(S("q_zero"), 2)
            keep_warm(T0 + diff_tile(0, 0), WARM)
            for step in range(N_DIFF + 2):
                if step < N_DIFF:
                    pe.wait_ge(S("rope_out"), step + 1)
                    pe.wait_ge(S("rope_out"), N_DIFF + step + 1)
                    for qt in range(TT):
                        for c in range(2):
                            t = T0 + diff_tile(step, 2 * qt + c)
                            open_bank(pe, t)
                            mm(bank(t)[:, :], qrot[c][:, step, qt * P:(qt + 1) * P], kall[:, step, :],
                               start=True, stop=True).then_inc(tile_ready, 1)
                if 1 <= step <= N_DIFF:
                    g = step - 1
                    for qt in range(TT):
                        t = T0 + diff_tile(g, 4 + qt)
                        pe.wait_ge(S("pd_ready"), 2 * g + qt + 1)
                        open_bank(pe, t)
                        for kt in range(4):
                            last = nc.tensor.transpose(bank(t)[:, kt * P:(kt + 1) * P], pd[:, qt, kt * P:(kt + 1) * P], ident)
                        last.then_inc(tile_ready, 1)
                    t = T0 + diff_tile(g, 6)
                    for qt in range(TT):
                        wait_evac(pe, T0 + diff_tile(g, 4 + qt))
                    open_bank(pe, t)
                    for kt in range(4):
                        last = mm(bank(t)[:, 0:SEQ], v_all[:, kt, g * P:(g + 1) * P], pdT[:, g % 2, kt, :],
                                  start=kt == 0, stop=kt == 3)
                    last.then_inc(tile_ready, 1)
                if step >= 2:
                    g = step - 2
                    t = T0 + diff_tile(g, 7)
                    pe.wait_ge(S("sub_squares"), g + 1)
                    open_bank(pe, t)
                    mm(bank(t)[:, 0:SEQ], K("mean_v"), sq_o[g % 2], start=True, stop=True).then_inc(tile_ready, 1)
                if 1 <= step <= N_DIFF:
                    ada(7 + step)
            pe.wait_ge(S("conv_out"), 4)
            pe.wait_ge(S("sub_out"), N_DIFF)
            linear("mix", TILES["mix"], 1, cat)

            def mlp(l):
                layer_norm(f"post1_{l}", resid, lambda k: wait_evac(pe, TILES["mix" if l == 0 else "fourier"] + k))
                layer_norm(f"mod2_{l}", h, lambda k: pe.wait_ge(S(f"post1_{l}_out"), k + 1))
                linear_split(f"w1_{l}", TILES[f"w1_{l}"], 4, u_parts["mlp"], norm=f"mod2_{l}")
                wide_split(f"w2_{l}", TILES[f"w2_{l}"], (hidden_high, hidden_low), 4,
                           lambda g: pe.wait_ge(S("hidden_ready"), 16 * l + 4 * g + 4))
                layer_norm(f"post2_{l}", resid, lambda k: wait_evac(pe, TILES[f"w2_{l}"] + k))

            mlp(0)
            layer_norm("mod1_1", h, lambda k: pe.wait_ge(S("post2_0_out"), k + 1))
            pe.wait_ge(S("in_dft"), 16)
            for g in range(KT):
                t = TILES["dft_in"] + g
                pe.wait_ge(S("mod1_1_out"), g + 1)
                open_bank(pe, t)
                for tt in range(TT):
                    last = mm(bank(t)[:, tt * 256:(tt + 1) * 256], u[:, g, tt * P:(tt + 1) * P], dft[:, 0:2 * P],
                              start=True, stop=True)
                last.then_inc(tile_ready, 1)
            for g in range(KT):
                t = TILES["dft_out"] + g
                wait_evac(pe, TILES["dft_in"] + g)
                open_bank(pe, t)
                for tt in range(TT):
                    for cs in range(2):
                        at = 2 * P + (2 * cs + tt) * SEQ
                        last = mm(bank(t)[:, 0:SEQ], dft_mid[:, g, tt, cs * P:(cs + 1) * P], dft[:, at:at + SEQ],
                                  start=tt == 0 and cs == 0, stop=tt == 1 and cs == 1)
                last.then_inc(tile_ready, 1)
            linear("fourier", TILES["fourier"], 1, spectrum,
                   hook=lambda j, n, k: wait_evac(pe, TILES["dft_out"] + k) if j == 0 and n == 0 else None)
            mlp(1)

            keep_warm(TILES["fox_norm"], 2 * WARM)
            rms_norm("fox_norm")
            t = TILES["forget"]
            open_bank(pe, t)
            pe.wait_ge(S("in_forget"), 32)
            for k in range(KT):
                pe.wait_ge(S("fox_norm_out"), k + 1)
                last = mm(bank(t)[0:FOX_HEADS, 0:SEQ], forget_w[:, k, :], u[:, k, :], start=k == 0, stop=k == KT - 1)
            last.then_inc(tile_ready, 1)
            F = TILES["fox_in"]
            linear_split("fox_in", F, 2, u_parts["second"], norm="fox_norm")
            token_major_split("fox_in", F + 16, 1, 2, u_parts["second"])
            linear_split("fox_in", F + 24, 1, u_parts["second"], at=3)
            T1 = TILES["fox_attn"]
            pe.wait_ge(S("fox_bias_rows"), 16 * 4)
            for n in range(16):
                wait_evac(pe, F + n)
            for n in range(8):
                wait_evac(pe, F + 16 + n)
            for step in range(FOX_HEADS // 2 + 1):
                if step < FOX_HEADS // 2:
                    for a in range(2):
                        t = T1 + fox_tile(step, a)
                        open_bank(pe, t)
                        for qt, (c0, nk) in enumerate(((0, P), (P, SEQ))):
                            mm(bank(t)[:, c0:c0 + nk], fq[a][:, step, qt * P:(qt + 1) * P], fk[a][:, step, 0:nk],
                               start=True, stop=False)
                            last = mm(bank(t)[:, c0 + nk - P:c0 + nk], ident, K("causal"), start=False, stop=True)
                        last.then_inc(tile_ready, 1)
                if step >= 1:
                    g = step - 1
                    for a in range(2):
                        t = T1 + fox_tile(g, 2 + a)
                        pe.wait_ge(S("fox_probs"), 2 * g + a + 1)
                        open_bank(pe, t)
                        for n in range(3):
                            last = nc.tensor.transpose(bank(t)[:, n * P:(n + 1) * P], fexp[:, a, n * P:(n + 1) * P], ident)
                        last.then_inc(tile_ready, 1)
                    t = T1 + fox_tile(g, 4)
                    open_bank(pe, t)
                    for a in range(2):
                        wait_evac(pe, T1 + fox_tile(g, 2 + a))
                    for kt, q0 in ((0, 0), (1, P)):
                        for a in range(2):
                            lo = a * FOX_DIM
                            c0 = (2 * g + a) * FOX_DIM
                            rows = fpT[:, a, 0:SEQ] if kt == 0 else fpT[:, a, SEQ:SEQ + P]
                            last = mm(bank(t)[lo:lo + FOX_DIM, q0:SEQ], fv[:, kt, c0:c0 + FOX_DIM], rows,
                                      start=kt == 0, stop=kt == 1)
                    last.then_inc(tile_ready, 1)
            linear("fox_out", TILES["fox_out"], 1, fgate,
                   hook=lambda j, n, k: wait_evac(pe, T1 + fox_tile(k, 4)) if j == 0 and n == 0 else None)

            def experts(l):
                rms_norm(f"moe_norm_{l}")
                t = TILES[f"router_{l}"]
                open_bank(pe, t)
                pe.wait_ge(S("in_router"), 16 * DEPTH)
                pe.wait_ge(S(f"moe_norm_{l}_out"), KT)
                for tt in range(TT):
                    for k in range(KT):
                        last = mm(bank(t)[:, tt * NR:(tt + 1) * NR], u[:, k, tt * P:(tt + 1) * P], router_w[:, l, k, :],
                                  start=k == 0, stop=k == KT - 1)
                last.then_inc(tile_ready, 1)
                for q in range(4):
                    t = TILES[f"hn_{l}"] + q
                    open_bank(pe, t)
                    for n in range(4):
                        k = (q % 2) * 4 + n
                        last = nc.tensor.transpose(bank(t)[:, n * P:(n + 1) * P],
                                                   u[:, k, (q // 2) * P:(q // 2 + 1) * P], ident)
                    last.then_inc(tile_ready, 1)
                t = TILES[f"router_{l}"] + 1
                open_bank(pe, t)
                pe.wait_ge(S("choices"), l + 1)
                mm(bank(t)[:, 0:E], K("before"), pick_e[:, 2, 0, :], start=True, stop=True)
                mm(bank(t)[:, E:2 * E], K("ones"), pick_e[:, 2, 0, :], start=True, stop=False)
                mm(bank(t)[:, E:2 * E], K("before"), pick_e[:, 2, 1, :], start=False, stop=True)
                mm(bank(t)[:, 2 * E:3 * E], K("ones"), pick_e[:, 2, 0, :], start=True, stop=False)
                mm(bank(t)[:, 2 * E:3 * E], K("ones"), pick_e[:, 2, 1, :], start=False, stop=True).then_inc(tile_ready, 1)
                A0 = TILES[f"combine_{l}"]
                total, free = [bank(A0 + q) for q in range(4)], [bank(A0 + 4 + q) for q in range(4)]
                for q in range(4):
                    open_bank(pe, A0 + q)
                    mm(total[q][:, :], ident, h[:, 2 * q:2 * q + 2, :].rearrange("p k n -> p (k n)"), start=True, stop=False)
                for q in range(4):
                    wait_evac(pe, TILES[f"hn_{l}"] + q)
                wait_evac(pe, TILES[f"router_{l}"] + 1)
                for b in range(BANKS):
                    pe.wait_ge(evacuated[b], (A0 - b + BANKS - 1) // BANKS)

                def gather(half, source):
                    for k in range(4 * half, 4 * half + 4):
                        for tt in range(TT):
                            last = mm(free[k // 4][:, (k % 4) * P:(k % 4 + 1) * P], hn_tok[:, tt, k * P:(k + 1) * P],
                                      source[:, tt, :], start=tt == 0, stop=tt == TT - 1)
                    return last

                def tiles_of(first):
                    if first == SLOTS:
                        return [(slice(0, SLOTS), 0), (slice(SLOTS, P), 1)]
                    return [(slice(at, at + UNIT), int(at >= first)) for at in range(0, P, UNIT)]

                def project(half, rows, gates=None, first=SLOTS):
                    for k in range(KT):
                        for cols, a in tiles_of(first):
                            w = expert_w[:, 2 + a, k * 512:(k + 1) * 512] if half else gates[:, (a * KT + k) * 512:(a * KT + k + 1) * 512]
                            last = mm(free[half][cols, :], rows[:, k, cols], w,
                                      start=k == 0, stop=k == KT - 1)
                    return last

                def turn_pick(source, done):
                    for tt in range(TT):
                        last = nc.tensor.transpose(free[3][:, tt * P:(tt + 1) * P], source[:, tt, :], ident)
                    last.then_inc(done, 1)

                def turn_hidden(done):
                    for f in range(4):
                        last = nc.tensor.transpose(free[2][:, f * P:(f + 1) * P], hid[:, f * P:(f + 1) * P], ident)
                    last.then_inc(done, 1)

                def down(half, loaded, first=SLOTS):
                    pe.wait_ge(expert_in[2 + half], loaded)
                    for f in range(4):
                        for cols, a in tiles_of(first):
                            at = (4 * a + f) * 512
                            last = mm(free[2 + half][cols, :], hidT[:, f, cols], expert_w[:, 4 + half, at:at + 512],
                                      start=f == 0, stop=f == 3)
                    return last

                def add_up(half):
                    for k in range(4 * half, 4 * half + 4):
                        last = mm(total[k // 2][:, (k % 2) * SEQ:(k % 2 + 1) * SEQ], y_sb[:, k * P:(k + 1) * P],
                                  pick_wT.rearrange("p t n -> p (t n)"), start=False, stop=False)
                    return last

                for _ in range(WARM):
                    mm(free[3][:, 0:SEQ], ident, K("rope_cos"), start=True, stop=True)
                pe.wait_ge(S("pick_ready"), (PAIRS + 1) * l + 1)
                for half in range(2):
                    gather(half, pick).then_inc(S("gathered"), 1)
                pe.wait_ge(S(f"more_known_{l}"), 1)

                def one_pair(i, place, gates_loaded):
                    n = PAIRS * l + i
                    gates = gate_w[place]

                    def tokens_there():
                        pe.wait_ge(S("xg_act"), (PAIRS + 1) * l + i + 1)
                        pe.wait_ge(S("xg_dve"), (PAIRS + 1) * l + i + 1)
                    n_more = pe.value_load(more_i[0:1, ds(i, 1)], min_val=0, max_val=FURTHER)
                    first_rows = pe.value_load(more_i[0:1, ds(i + 2 * PAIRS, 1)], min_val=UNIT, max_val=P - UNIT)
                    with pe.If(n_more > 0):
                        before = pe.value_load(more_i[0:1, ds(i + PAIRS, 1)], min_val=0, max_val=2 * SEQ // SLOTS)
                        with pe.Fori(0, FURTHER) as r:
                            with pe.If(r < n_more):
                                c = before + r
                                tokens_there()
                                pe.wait_ge(S(f"more_pick_ready_{l}"), c + 1)
                                gather(0, pick_more)
                                gather(1, pick_more).then_inc(S(f"more_gathered_{l}"), 1)
                                pe.wait_ge(S(f"more_xg_act_{l}"), c + 1)
                                pe.wait_ge(S(f"more_xg_dve_{l}"), c + 1)
                                pe.wait_ge(gates_in[place], gates_loaded)
                                project(0, xg_more, gates).then_inc(S(f"more_gate_{l}"), 1)
                                for a in range(2):
                                    pe.wait_ge(expert_in[a], 16 * (n + 1))
                                project(1, xg_more).then_inc(S(f"more_up_{l}"), 1)
                                turn_pick(pick_w_more, S(f"more_pick_turned_{l}"))
                                pe.wait_ge(S(f"more_hidden_{l}"), c + 1)
                                turn_hidden(S(f"more_hidden_turned_{l}"))
                                pe.wait_ge(S(f"more_hidT_{l}"), c + 1)
                                pe.wait_ge(S(f"more_pick_wT_{l}"), c + 1)
                                down(0, 16 * (n + 1))
                                down(1, 16 * (n + 1)).then_inc(S(f"more_down_{l}"), 1)
                                pe.wait_ge(S(f"more_y_act_{l}"), c + 1)
                                pe.wait_ge(S(f"more_y_dve_{l}"), c + 1)
                                add_up(0)
                                add_up(1).then_inc(S(f"more_added_{l}"), 1)
                    for first in SHARES:
                        with pe.If(first_rows == first):
                            tokens_there()
                            pe.wait_ge(gates_in[place], gates_loaded)
                            project(0, xg, gates, first).then_inc(expert_used, 1)
                            for a in range(2):
                                pe.wait_ge(expert_in[a], 16 * (n + 1))
                            project(1, xg, first=first).then_inc(expert_used, 1)
                    pe.wait_ge(S("pick_ready"), (PAIRS + 1) * l + i + 2)
                    pe.wait_ge(S("silu_e"), n + 1)
                    gather(0, pick).then_inc(S("gathered"), 1)
                    pe.wait_ge(S("pick_w_ready"), (PAIRS + 1) * l + i + 1)
                    turn_pick(pick_w, S("pick_turned"))
                    pe.wait_ge(S("hidden_e"), n + 1)
                    turn_hidden(S("hidden_turned"))
                    gather(1, pick).then_inc(S("gathered"), 1)
                    pe.wait_ge(S("hidT_ready"), n + 1)
                    pe.wait_ge(S("pick_wT_ready"), n + 1)
                    for first in SHARES:
                        with pe.If(first_rows == first):
                            for half in range(2):
                                down(half, 16 * (n + 1), first).then_inc(expert_used, 1)
                    pe.wait_ge(S("y_act"), n + 1)
                    add_up(0)
                    pe.wait_ge(S("y_dve"), n + 1)
                    add_up(1).then_inc(S("added"), 1)
                with pe.Fori(0, PAIRS // 2) as p:
                    for place in range(2):
                        one_pair(2 * p + place, place, 16 * (PAIRS // 2 * l + p + 1))
                for q in range(4):
                    mm(total[q][:, 0:2], ident, zrow[:, 0:2], start=False, stop=True).then_inc(tile_ready, 1)
                pe.wait_ge(S("xg_act"), (PAIRS + 1) * (l + 1))
                pe.wait_ge(S("xg_dve"), (PAIRS + 1) * (l + 1))
            experts(0)
            rms_norm("ret_norm")
            R = TILES["ret_in"]
            linear_split("ret_in", R, 2, u_parts["second"], norm="ret_norm")
            token_major_split("ret_in", R + 16, 2, 2, u_parts["second"])
            linear_split("ret_in", R + 32, 2, u_parts["second"], at=4)
            pe.wait_ge(S("rotated"), 2)
            for hd in range(RET_HEADS):
                t = TILES["ret_scores"] + hd
                open_bank(pe, t)
                for jt, (c0, i0, n) in enumerate(((0, 0, SEQ), (SEQ, P, P))):
                    for s in range(2):
                        last = mm(bank(t)[:, c0:c0 + n], rqk[:, 8 + 2 * hd + s, jt * P:(jt + 1) * P],
                                  rqk[:, 2 * hd + s, i0:i0 + n], start=s == 0, stop=s == 1)
                last.then_inc(tile_ready, 1)
            for n in range(16):
                wait_evac(pe, R + 16 + n)
            for n in range(8):
                t = TILES["ret_pv"] + n
                hd = n // 2
                open_bank(pe, t)
                wait_evac(pe, TILES["ret_scores"] + hd)
                for s in range(2):
                    c0 = (2 * n + s) * P
                    mm(bank(t)[:, s * SEQ:(s + 1) * SEQ], rv[:, 0, c0:c0 + P], r_s[:, hd, 0:SEQ], start=True, stop=False)
                    last = mm(bank(t)[:, s * SEQ + P:(s + 1) * SEQ], rv[:, 1, c0:c0 + P], r_s[:, hd, SEQ:SEQ + P],
                              start=False, stop=True)
                last.then_inc(tile_ready, 1)
            for hd in range(RET_HEADS):
                stat(TILES["gn_mean"] + hd, K("mean_gn"), ro[:, 4 * hd:4 * hd + 4, :], 4,
                     lambda k: wait_evac(pe, TILES["ret_pv"] + 2 * hd + k // 2))
            for hd in range(RET_HEADS):
                stat(TILES["gn_var"] + hd, K("mean_gn"), rqk[:, 4 * hd:4 * hd + 4, :], 4,
                     lambda k: pe.wait_ge(S("gn_squares"), hd + 1))
            keep_warm(TILES["ret_out"], 2 * WARM)
            wide("ret_out", TILES["ret_out"], rgate, 2, lambda g: pe.wait_ge(S("ret_gated"), 8 * g + 8))
            experts(1)
            rms_norm("final_norm")
            pe.wait_ge(S("final_norm_out"), KT)
            for q in range(4):
                t = TILES["final"] + q
                open_bank(pe, t)
                for n in range(4):
                    k = (q % 2) * 4 + n
                    last = nc.tensor.transpose(bank(t)[:, n * P:(n + 1) * P], u[:, k, (q // 2) * P:(q // 2 + 1) * P], ident)
                last.then_inc(tile_ready, 1)

        @block.scalar
        def _(act):
            fn = nc.scalar.activation

            def copy_out(t, dst, src, func=None, scale=1.0):
                wait_tile(act, t)
                return evac(fn(dst, src, func or ACT.Copy, scale=scale), t)

            def square(name, src, wait_piece):
                for p in range(4):
                    wait_piece(p)
                    fn(squares[:, 2 * p:2 * p + 2, :], src[:, 2 * p:2 * p + 2, :], ACT.Square).then_inc(S("squares"), 1)

            def deviation(dst, t, eps=0):
                wait_tile(act, t)
                at = CONSTS["eps"][0] + eps
                evac(fn(dst, bank(t)[:, 0:SEQ], ACT.Sqrt, bias=const[:, at:at + 1]), t)

            def ln_squares(name, between=None):
                square(name, centered, lambda p: act.wait_ge(S("centered"), 4 * NORMS.index(name) + p + 1))
                if between is not None:
                    between()
                deviation(rstd, TILES[f"{name}_var"] if between is not None else TILES[name] + 1)

            def take_ada(r, q, i=0):
                t = ada_tiles(r)[q]
                act.wait_ge(tile_ready, t + 1 + 16 * i)
                evac(fn(ada_rows[:, q, :], bank(t)[:, :], ACT.Copy), t)

            def ln_out(name, dst, done):
                scale, shift = norm_affine(name)
                for k in range(KT):
                    act.wait_ge(S("standardized"), KT * NORMS.index(name) + k + 1)
                    fn(dst[:, k, :], centered[:, k, :], ACT.Identity, scale=scale(k), bias=shift(k)).then_inc(S(done), 1)

            def layer_norm(name, dst, done=None):
                ln_squares(name)
                ln_out(name, dst, done or f"{name}_out")

            def rms_squares(name, wait_piece):
                square(name, h, wait_piece)
                deviation(rstd, TILES[name])

            def added(name):
                return lambda p: [wait_evac(act, TILES[name] + n) for n in (2 * p, 2 * p + 1)]

            def high_of_u(name, where):
                for k in range(KT):
                    act.wait_ge(S(f"{name}_out"), k + 1)
                    fn(u_parts[where][0][:, k, :], u[:, k, :], ACT.Copy).then_inc(S(f"{name}_high"), 1)

            def split_ahead(name, after, i, j):
                a = ahead(name, after, i, j)
                if a:
                    split_high(act, *a)

            act.dma_start(vrow1, A["vec1"]).then_inc(S("in_small"), 16)
            act.dma_start(vrow2[0:N_VEC2, :], A["vec2"]).then_inc(S("in_small"), 16)
            act.dma_start(rows_in[:, :], A["rows"]).then_inc(S("in_small"), 16)
            act.dma_start(dft, A["dft"]).then_inc(S("in_dft"), 16)
            for l in range(DEPTH):
                act.dma_start(router_w[:, l], A["router_w"][l].rearrange("(k p) n -> p k n", p=P)).then_inc(S("in_router"), 16)
            act.dma_start(forget_w[:, :, :], A["fox_w_in_2"][0, :, 4 * D:4 * D + FOX_HEADS].rearrange(
                "(k p) n -> p k n", p=P)).then_inc(S("in_forget"), 16)
            act.dma_start(forget_b[:, :], A["fox_b_f_2"].rearrange("a n -> n a")).then_inc(S("in_forget"), 16)

            wait_evac(act, TILES["vecs"])
            act.wait_ge(S("cond_zero"), 1)
            fn(cond[:, :, 0:2], vec[:, 0:16].rearrange("p (a k) -> p k a", a=2), ACT.Silu).then_inc(S("cond_ready"), 1)
            for q in range(4):
                copy_out(TILES["ctx"] + q, ctxT[:, 2 * q:2 * q + 2, :],
                         bank(TILES["ctx"] + q)[:, :].rearrange("p (k n) -> p k n", k=2))
            ln_squares("u", lambda: [take_ada(0, q) for q in range(2)])
            ln_squares("uc", lambda: [take_ada(1, q) for q in range(2)])
            with act.Fori(0, 2) as i:
                for e in IN_ORDER:
                    if e[0] == "w":
                        t = in_tile(e[1])
                        act.wait_ge(tile_ready, t + 16 * i + 1)
                        evac(fn(proj[:, ds(8 * i + e[1], 1), :].rearrange("p a n -> p (a n)"), bank(t)[:, 0:SEQ], ACT.Copy), t)
                    elif e[0] == "r":
                        take_ada(2 + e[1], e[2], i)
            for e in KV_ORDER:
                if e[0] == "w":
                    n, t = e[1], kv_tile(e[1])
                    if n >= 8:
                        m = n - 8
                        copy_out(t, v_all[:, m % 4, (m // 4) * CHUNK:(m // 4 + 1) * CHUNK], bank(t)[:, 0:CHUNK])
                    elif n % 2:
                        copy_out(t, kall[:, n // 2, SEQ:2 * SEQ], bank(t)[:, 0:SEQ])
                    else:
                        copy_out(t, kraw[:, n // 2, :], bank(t)[:, 0:SEQ])
                elif e[0] == "r":
                    take_ada(6 + e[1], e[2])
            act.wait_ge(S("lam_sums"), 2)
            fn(small[:, 4:6], small[:, 0:2], ACT.Exp).then_inc(S("lam_exps"), 1)
            T0 = TILES["attn"]
            for step in range(N_DIFF + 2):
                if step < N_DIFF:
                    for n in range(4):
                        t = T0 + diff_tile(step, n)
                        qt, c = n // 2, n % 2
                        act.wait_ge(S("diff_max"), 4 * step + n + 1)
                        if step:
                            act.wait_ge(S("pd_ready"), 2 * (step - 1) + qt + 1)
                        evac(fn(expd[:, qt, c, :], bank(t)[:, :], ACT.Exp, bias=small[:, 16 + n:17 + n],
                                accum_out=small[:, 24 + n:25 + n]), t)
                if 1 <= step <= N_DIFF:
                    g = step - 1
                    for qt in range(TT):
                        t = T0 + diff_tile(g, 4 + qt)
                        copy_out(t, pdT[:, g % 2, :, qt * P:(qt + 1) * P],
                                 bank(t)[:, :].rearrange("p (k n) -> p k n", k=4))
                    t = T0 + diff_tile(g, 6)
                    wait_tile(act, t)
                    if g >= 2:
                        wait_tile(act, T0 + diff_tile(g - 2, 7))
                    fn(sq_o[g % 2], bank(t)[:, 0:SEQ], ACT.Square).then_inc(S("sub_squares"), 1)
                    evac(fn(cat[:, 4 + g, :], bank(t)[:, 0:SEQ], ACT.Copy), t)
                if step >= 2:
                    g = step - 2
                    if g >= 2:
                        act.wait_ge(S("sub_out"), g - 1)
                    deviation(sub_rstd[g % 2], T0 + diff_tile(g, 7), 1)
                if 1 <= step <= N_DIFF:
                    for q in range(2):
                        take_ada(7 + step, q)

            def mlp(l):
                w1, w2 = f"w1_{l}", f"w2_{l}"
                for j in range(2):
                    split_high(act, w1, 0, j)
                layer_norm(f"post1_{l}", h)
                layer_norm(f"mod2_{l}", u_parts["mlp"][0], f"mod2_{l}_high")

                def rotation(i):
                    for j in range(RING):
                        split_ahead(w1, w2, i, j)
                        for n in (2 * j, 2 * j + 1):
                            t = TILES[w1] + n
                            act.wait_ge(tile_ready, t + 8 * i + 1)
                            evac(fn(hidden[:, ds(8 * i + n, 1), :].rearrange("p a n -> p (a n)"), bank(t)[:, 0:SEQ], ACT.Relu), t)
                        act.wait_ge(S("hidden_done"), 16 * l + 4 * i + j + 1)
                        at = ds(8 * i + 2 * j, 2)
                        fn(hidden_high[:, at, :], hidden[:, at, :], ACT.Copy).then_inc(S("hidden_high"), 1)
                with act.Fori(0, 3) as i:
                    rotation(i)
                rotation(3)
                for j in (2, 3):
                    split_high(act, w2, 0, j)
                with act.Fori(1, 4) as i:
                    for j in range(RING):
                        split_high(act, w2, i, j)
                layer_norm(f"post2_{l}", h)

            mlp(0)
            layer_norm("mod1_1", u)
            for g in range(KT):
                t = TILES["dft_in"] + g
                copy_out(t, dft_mid[:, g], bank(t)[:, :].rearrange("p (t n) -> p t n", t=TT))
            mlp(1)

            for j in range(2):
                split_high(act, "fox_in", 0, j)
            rms_squares("fox_norm", lambda p: act.wait_ge(S("post2_1_out"), 2 * p + 2))
            high_of_u("fox_norm", "second")
            for j in (2, 3):
                split_high(act, "fox_in", 0, j)
            t = TILES["forget"]
            act.wait_ge(S("forget_abs"), 1)
            fn(flog[:, 1, :], flog[:, 0, :], ACT.Exp, scale=-1.0).then_inc(S("forget_exp"), 1)
            act.wait_ge(S("forget_one"), 1)
            fn(flog[:, 1, :], flog[:, 1, :], ACT.Ln).then_inc(S("forget_ln"), 1)
            F = TILES["fox_in"]
            for i in range(4):
                for j in range(RING):
                    if (i, j) >= (0, 2):
                        split_ahead("fox_in", None, i, j)
                    for n in (2 * j, 2 * j + 1):
                        t = F + 8 * i + n
                        if i < 2:
                            wait_tile(act, t)
                            for a in range(2):
                                rows = slice(a * FOX_DIM, (a + 1) * FOX_DIM)
                                last = fn((fq, fk)[i][a][rows, n, :], bank(t)[rows, 0:SEQ], ACT.Copy,
                                          scale=1.0 if i else FOX_DIM ** -0.5)
                            evac(last, t)
                        elif i == 2:
                            copy_out(t, fv[:, n % 2, j * CHUNK:(j + 1) * CHUNK], bank(t)[:, 0:CHUNK])
                        else:
                            copy_out(t, fgate[:, n, :], bank(t)[:, 0:SEQ], ACT.Sigmoid)
            T1 = TILES["fox_attn"]
            for step in range(FOX_HEADS // 2 + 1):
                if step < FOX_HEADS // 2:
                    for a in range(2):
                        t = T1 + fox_tile(step, a)
                        act.wait_ge(S("fox_max"), 2 * (2 * step + a) + 2)
                        if step:
                            wait_tile(act, T1 + fox_tile(step - 1, 2 + a))
                        for qt, (c0, nk) in enumerate(((0, P), (P, SEQ))):
                            last = fn(fexp[:, a, c0:c0 + nk], bank(t)[:, c0:c0 + nk], ACT.Exp,
                                      bias=small[:, 32 + 2 * a + qt:33 + 2 * a + qt],
                                      accum_out=small[:, 36 + 2 * a + qt:37 + 2 * a + qt])
                        evac(last, t)
                if step >= 1:
                    g = step - 1
                    for a in range(2):
                        t = T1 + fox_tile(g, 2 + a)
                        if g:
                            wait_tile(act, T1 + fox_tile(g - 1, 4))
                        copy_out(t, fpT[:, a, :], bank(t)[:, 0:384])

            def experts(l):
                rms_squares(f"moe_norm_{l}", added("ret_out" if l else "fox_out"))
                act.wait_ge(S("group_max"), l + 1)
                for tt in range(TT):
                    fn(rt[:, 0 + 4 * tt:4 + 4 * tt], lg[:, tt, 0:GROUPS], ACT.Exp, bias=rt[:, 8 + tt:9 + tt],
                       accum_out=rt[:, 10 + tt:11 + tt]).then_inc(S("group_exp"), 1)
                act.wait_ge(S("second_gap"), l + 1)
                fn(rt[:, 14:16], rt[:, 12:14], ACT.Exp).then_inc(S("second_exp"), 1)
                for q in (0, 2):
                    t = TILES[f"hn_{l}"] + q
                    copy_out(t, hn_tok[:, q // 2, 0:512], bank(t)[:, :])

                free = [bank(TILES[f"combine_{l}"] + 4 + q) for q in range(4)]

                def silu(done):
                    fn(sil, free[0][:, :], ACT.Silu).then_inc(done, 1)

                def take_xg(rows, done):
                    fn(rows[:, 0:4, :], free[0][:, :].rearrange("p (k n) -> p k n", k=4), ACT.Copy).then_inc(done, 1)

                def take_hidT(done):
                    fn(hidT, free[2][:, :].rearrange("p (f n) -> p f n", f=4), ACT.Copy).then_inc(done, 1)

                def take_y(done):
                    fn(y_sb[:, 0:512], free[2][:, :], ACT.Copy).then_inc(done, 1)

                act.wait_ge(S("gathered"), 2 * (PAIRS + 1) * l + 1)
                take_xg(xg, S("xg_act"))
                act.wait_ge(S(f"more_known_{l}"), 1)
                with act.Fori(0, PAIRS) as i:
                    n = PAIRS * l + i
                    n_more = act.value_load(more_i[0:1, ds(i, 1)], min_val=0, max_val=FURTHER)
                    with act.If(n_more > 0):
                        before = act.value_load(more_i[0:1, ds(i + PAIRS, 1)], min_val=0, max_val=2 * SEQ // SLOTS)
                        with act.Fori(0, FURTHER) as r:
                            with act.If(r < n_more):
                                c = before + r
                                act.wait_ge(S(f"more_gathered_{l}"), c + 1)
                                take_xg(xg_more, S(f"more_xg_act_{l}"))
                                act.wait_ge(S(f"more_gate_{l}"), c + 1)
                                silu(S(f"more_silu_{l}"))
                                act.wait_ge(S(f"more_hidden_turned_{l}"), c + 1)
                                take_hidT(S(f"more_hidT_{l}"))
                                act.wait_ge(S(f"more_down_{l}"), c + 1)
                                take_y(S(f"more_y_act_{l}"))
                    act.wait_ge(expert_used, 4 * n + 1)
                    silu(S("silu_e"))
                    act.wait_ge(S("gathered"), 2 * ((PAIRS + 1) * l + i + 1) + 1)
                    take_xg(xg, S("xg_act"))
                    act.wait_ge(S("hidden_turned"), n + 1)
                    take_hidT(S("hidT_ready"))
                    act.wait_ge(expert_used, 4 * n + 3)
                    take_y(S("y_act"))
                for q in (0, 2):
                    t = TILES[f"combine_{l}"] + q
                    wait_tile(act, t)
                    evac(fn(h[:, 2 * q:2 * q + 2, :], bank(t)[:, :].rearrange("p (k n) -> p k n", k=2), ACT.Copy), t)

            experts(0)
            split_high(act, "ret_in", 0, 0)
            rms_squares("ret_norm", lambda p: wait_evac(act, TILES["combine_0"] + p))
            split_high(act, "ret_in", 0, 1)
            high_of_u("ret_norm", "second")
            R = TILES["ret_in"]
            for i in range(6):
                for j in range(RING):
                    split_ahead("ret_in", None, i, j)
                    for n in (2 * j, 2 * j + 1):
                        t = R + 8 * i + n
                        if i < 2:
                            copy_out(t, rraw[:, 8 * i + n, :], bank(t)[:, 0:SEQ], scale=(D // RET_HEADS) ** -0.5 if i else 1.0)
                        elif i < 4:
                            c0 = (4 * (i - 2) + j) * CHUNK
                            copy_out(t, rv[:, n % 2, c0:c0 + CHUNK], bank(t)[:, 0:CHUNK])
                        else:
                            copy_out(t, rgate[:, 8 * (i - 4) + n, :], bank(t)[:, 0:SEQ], ACT.Silu)
            for n in range(8):
                t = TILES["ret_pv"] + n
                copy_out(t, ro[:, 2 * n:2 * n + 2, :], bank(t)[:, :].rearrange("p (k n) -> p k n", k=2))
            for hd in range(RET_HEADS):
                wait_evac(act, TILES["gn_mean"] + hd)
                fn(rqk[:, 4 * hd:4 * hd + 4, :], ro[:, 4 * hd:4 * hd + 4, :], ACT.Square).then_inc(S("gn_squares"), 1)
            for hd in range(RET_HEADS):
                deviation(gn_rstd[:, hd, :], TILES["gn_var"] + hd)
            experts(1)
            rms_squares("final_norm", lambda p: wait_evac(act, TILES["combine_1"] + p))
            for q in (0, 2):
                t = TILES["final"] + q
                wait_tile(act, t)
                fn(out_tok[:, q // 2, 0:512], bank(t)[:, :], ACT.Copy).then_inc(S("out_act"), 1)

        @block.vector
        def _(dve):
            V = nc.vector
            chain = S("dve_chain")
            n_chain = [0]

            def link(ins):
                n_chain[0] += 1
                ins.then_inc(chain, 1)
                dve.wait_ge(chain, n_chain[0])

            def over_tiles(v, n):
                return v.unsqueeze(1).broadcast_to([P, n, SEQ])

            def inv_std(dst, t):
                wait_evac(dve, t)
                link(V.reciprocal(dst, dst))

            def low_of_u(name, where):
                high, low = u_parts[where]
                for k in range(KT):
                    dve.wait_ge(S(f"{name}_out"), k + 1)
                    dve.wait_ge(S(f"{name}_high"), k + 1)
                    V.tensor_tensor(low[:, k, :], u[:, k, :], high[:, k, :].bitcast(f32), ALU.subtract).then_inc(S(f"{name}_low"), 1)

            def split_ahead(name, after, i, j):
                a = ahead(name, after, i, j)
                if a:
                    split_low(dve, *a)

            def standardize(name, src, dst, between=None, idle=None):
                t = TILES[name]
                wait_tile(dve, t)
                if NORMS.index(name):
                    dve.wait_ge(S("standardized"), KT * NORMS.index(name))
                for p in range(4):
                    two = slice(2 * p, 2 * p + 2)
                    last = V.tensor_tensor(centered[:, two, :], src[:, two, :], over_tiles(bank(t)[:, 0:SEQ], 2), ALU.subtract)
                    last.then_inc(S("centered"), 1)
                dve.wait_ge(S("centered"), 4 * NORMS.index(name) + 4)
                dve.sem_inc(evacuated[t % BANKS], 1)
                if between is not None:
                    between()
                if idle is not None:
                    idle()
                inv_std(rstd, TILES[f"{name}_var"] if between is not None else t + 1)
                for k in range(KT):
                    V.tensor_tensor(dst[:, k, :], centered[:, k, :], rstd, ALU.mult).then_inc(S("standardized"), 1)

            def scale_shift(name, src, dst, scale, shift):
                dve.wait_ge(S("standardized"), KT * NORMS.index(name) + KT)
                for k in range(KT):
                    V.tensor_scalar(dst[:, k, :], src[:, k, :], scale(k), shift(k), ALU.mult, ALU.add).then_inc(S(f"{name}_out"), 1)

            def layer_norm(name, src, idle=None):
                standardize(name, src, centered, idle=idle)

            def take_ada(r, i=0):
                tiles = ada_tiles(r)[2:]
                for q, t in enumerate(tiles):
                    dve.wait_ge(tile_ready, t + 1 + 16 * i)
                    at = 8 * r + 4 * q + 16 * i
                    evac(V.tensor_tensor(mod_all[:, ds(at, 4), :], bank(t)[:, 0:8].rearrange("p (m a) -> p m a", a=2),
                                         vec[:, ds(at + VEC1["ada_b"], 4)].unsqueeze(2).broadcast_to([P, 4, 2]), ALU.add), t)
                for t in tiles:
                    dve.wait_ge(evacuated[t % BANKS], t // BANKS + 1 + 2 * i)

            mod_all = mod[:, :, :, :].rearrange("p l m a -> p (l m) a")

            def rms_norm(name, gain):
                inv_std(rstd, TILES[name])
                for k in range(KT):
                    V.scalar_tensor_tensor(u[:, k, :], h[:, k, :], gain(k), rstd, ALU.mult, ALU.mult).then_inc(S(f"{name}_out"), 1)


            V.memset(cond[:, :, :], 0.0).then_inc(S("cond_zero"), 1)
            t = TILES["vecs"]
            wait_tile(dve, t)
            evac(V.tensor_copy(vec[:, :], bank(t)[:, 0:P + N_VEC2]), t)
            wait_tile(dve, t + 1)
            evac(V.tensor_copy(rowbc[:, :], bank(t + 1)[:, 0:N_ROW]), t + 1)
            wait_evac(dve, t)
            wait_evac(dve, t + 1)
            for n in range(2):
                V.tensor_tensor_reduce(out=small[:, 64:128], in0=rowbc[:, 128 * n:128 * n + 64],
                                       in1=rowbc[:, 128 * n + 64:128 * n + 128], scale=1.0, scalar=0.0,
                                       op0=ALU.mult, op1=ALU.add, accum_out=small[:, n:n + 1]).then_inc(S("lam_sums"), 1)
                dve.wait_ge(S("lam_sums"), n + 1)
            for q in range(4):
                t = TILES["x"] + q
                wait_tile(dve, t)
                evac(V.tensor_copy(h[:, 2 * q:2 * q + 2, :], bank(t)[:, :].rearrange("p (k n) -> p k n", k=2)), t)
            for q in range(4):
                wait_evac(dve, TILES["x"] + q)
            standardize("u", h, u, lambda: take_ada(0))
            for q in range(4):
                wait_evac(dve, TILES["ctx"] + q)
            standardize("uc", ctxT, uc, lambda: take_ada(1))
            link(V.tensor_scalar(mod[:, 0, SC1:SC1 + KT, :], mod[:, 0, SC1:SC1 + KT, :], 1.0, None, ALU.add))
            scale_shift("u", u, u, lambda k: mcol(0, SC1 + k), lambda k: mcol(0, SH1 + k))
            scale_shift("uc", uc, uc, lambda k: mcol(0, SC1 + k, 1), lambda k: mcol(0, SH1 + k, 1))
            with dve.Fori(0, 2) as i:
                for s in range(2):
                    take_ada(2 + s, i)
            for n in range(4):
                for b in range(3):
                    wait_evac(dve, in_tile(4 * b + n))
                gb, gc, cv = (proj[:, 4 * b + n, :] for b in range(3))
                w0 = P + VEC2["conv"]
                link(V.tensor_tensor(gc, gc, cv, ALU.mult))
                link(V.tensor_scalar(cv, gc, vcol(w0 + 4 + n), None, ALU.mult))
                link(V.scalar_tensor_tensor(cv[:, 1:SEQ], gc[:, 0:SEQ - 1], vcol(w0 + n), cv[:, 1:SEQ], ALU.mult, ALU.add))
                link(V.scalar_tensor_tensor(cv[:, 0:SEQ - 1], gc[:, 1:SEQ], vcol(w0 + 8 + n), cv[:, 0:SEQ - 1], ALU.mult, ALU.add))
                V.tensor_tensor(cat[:, n, :], gb, cv, ALU.mult).then_inc(S("conv_out"), 1)
            for r in (6, 7):
                take_ada(r)
            for n in range(8):
                t = TILES["rope"] + n
                raw = proj[:, 12 + n, :] if n < 4 else kraw[:, n - 4, :]
                scale = DIFF_QK ** -0.5 if n < 4 else 1.0
                wait_tile(dve, t)
                V.scalar_tensor_tensor(rope_b, raw, scale, K("rope_cos"), ALU.mult, ALU.mult).then_inc(S("rope_cos_part"), 1)
                evac(V.scalar_tensor_tensor(rope_a, bank(t)[:, 0:SEQ], scale, K("rope_sin"), ALU.mult, ALU.mult), t)
                dve.wait_ge(S("rope_cos_part"), n + 1)
                wait_evac(dve, t)
                if n < 4:
                    for c in range(2):
                        rows = slice(c * DIFF_QK, (c + 1) * DIFF_QK)
                        last = V.tensor_tensor(qrot[c][rows, n, :], rope_a[rows, :], rope_b[rows, :], ALU.add)
                else:
                    last = V.tensor_tensor(kall[:, n - 4, 0:SEQ], rope_a, rope_b, ALU.add)
                last.then_inc(S("rope_out"), 1)
                dve.wait_ge(S("rope_out"), n + 1)
            dve.wait_ge(S("lam_exps"), 1)
            link(V.tensor_tensor(small[:, 6:7], small[:, 5:6], small[:, 4:5], ALU.subtract))
            link(V.tensor_scalar(small[:, 7:8], small[:, 6:7], LAM_INIT, None, ALU.subtract))
            link(V.tensor_scalar(small[:, 8:9], vcol(P + VEC2["subln"]), 1.0 - LAM_INIT, None, ALU.mult))
            T0 = TILES["attn"]
            for step in range(N_DIFF + 2):
                if step < N_DIFF:
                    for n in range(4):
                        t = T0 + diff_tile(step, n)
                        wait_tile(dve, t)
                        V.tensor_reduce(small[:, 16 + n:17 + n], bank(t)[:, :], AX.X, ALU.max, negate=True).then_inc(S("diff_max"), 1)
                    for qt in range(TT):
                        for c in range(2):
                            wait_evac(dve, T0 + diff_tile(step, 2 * qt + c))
                        link(V.reciprocal(small[:, 128 + 2 * qt:130 + 2 * qt], small[:, 24 + 2 * qt:26 + 2 * qt]))
                        link(V.tensor_scalar(small[:, 129 + 2 * qt:130 + 2 * qt], small[:, 129 + 2 * qt:130 + 2 * qt],
                                             small[:, 7:8], None, ALU.mult))
                        link(V.tensor_scalar(expd[:, qt, 0, :], expd[:, qt, 0, :], small[:, 128 + 2 * qt:129 + 2 * qt], None, ALU.mult))
                        if step:
                            wait_tile(dve, T0 + diff_tile(step - 1, 4 + qt))
                        V.scalar_tensor_tensor(pd[:, qt, :], expd[:, qt, 1, :], small[:, 129 + 2 * qt:130 + 2 * qt],
                                               expd[:, qt, 0, :], ALU.mult, ALU.add).then_inc(S("pd_ready"), 1)
                if step >= 2:
                    g = step - 2
                    inv_std(sub_rstd[g % 2], T0 + diff_tile(g, 7))
                    wait_evac(dve, T0 + diff_tile(g, 6))
                    V.scalar_tensor_tensor(cat[:, 4 + g, :], cat[:, 4 + g, :], small[:, 8:9], sub_rstd[g % 2],
                                           ALU.mult, ALU.mult).then_inc(S("sub_out"), 1)
                if 1 <= step <= N_DIFF:
                    take_ada(7 + step)
            for l, at in ((0, SC2), (1, SC1), (1, SC2)):
                link(V.tensor_scalar(mod[:, l, at:at + KT, :], mod[:, l, at:at + KT, :], 1.0, None, ALU.add))

            def residual(name, l, gate):
                link(V.tensor_scalar(resid, h[:, :, :], ALPHA, None, ALU.mult))
                for k in range(KT):
                    t = TILES[name] + k
                    wait_tile(dve, t)
                    evac(V.scalar_tensor_tensor(resid[:, k, :], bank(t)[:, 0:SEQ], mcol(l, gate + k), resid[:, k, :],
                                                ALU.mult, ALU.add), t)

            def mlp(l):
                name = "mix" if l == 0 else "fourier"
                residual(name, l, G1)
                w1, w2 = f"w1_{l}", f"w2_{l}"
                layer_norm(f"post1_{l}", resid, idle=lambda: [split_low(dve, w1, 0, j) for j in range(2)])
                dve.wait_ge(S(f"post1_{l}_out"), KT)
                layer_norm(f"mod2_{l}", h)
                low_of_u(f"mod2_{l}", "mlp")

                def rotation(i):
                    for j in range(RING):
                        split_ahead(w1, w2, i, j)
                        for n in (2 * j, 2 * j + 1):
                            t = TILES[w1] + n
                            dve.wait_ge(evacuated[t % BANKS], t // BANKS + 1 + i)
                        v = hidden[:, ds(8 * i + 2 * j, 2), :]
                        V.tensor_tensor(v, v, v, ALU.mult).then_inc(S("hidden_done"), 1)
                        dve.wait_ge(S("hidden_high"), 16 * l + 4 * i + j + 1)
                        at = ds(8 * i + 2 * j, 2)
                        V.tensor_tensor(hidden_low[:, at, :], hidden[:, at, :], hidden_high[:, at, :].bitcast(f32),
                                        ALU.subtract).then_inc(S("hidden_ready"), 1)
                with dve.Fori(0, 3) as i:
                    rotation(i)
                rotation(3)
                for j in (2, 3):
                    split_low(dve, w2, 0, j)
                with dve.Fori(1, 4) as i:
                    for j in range(RING):
                        split_low(dve, w2, i, j)
                residual(f"w2_{l}", l, G2)
                layer_norm(f"post2_{l}", resid)
                dve.wait_ge(S(f"post2_{l}_out"), KT)

            mlp(0)
            layer_norm("mod1_1", h)
            for g in range(KT):
                t = TILES["dft_out"] + g
                wait_tile(dve, t)
                evac(V.tensor_copy(spectrum[:, g, :], bank(t)[:, 0:SEQ]), t)
            mlp(1)

            for j in range(2):
                split_low(dve, "fox_in", 0, j)
            rms_norm("fox_norm", lambda k: vcol(P + VEC2["mix"] + k))
            low_of_u("fox_norm", "second")
            for j in (2, 3):
                split_low(dve, "fox_in", 0, j)
            t = TILES["forget"]
            dve.wait_ge(S("in_forget"), 32)
            wait_tile(dve, t)
            evac(V.tensor_scalar(flog[:, 2, :], bank(t)[0:FOX_HEADS, 0:SEQ], forget_b[:, 0:1], None, ALU.add), t)
            wait_evac(dve, t)
            V.scalar_tensor_tensor(flog[:, 0, :], flog[:, 2, :], -1.0, flog[:, 2, :], ALU.mult, ALU.max).then_inc(S("forget_abs"), 1)
            dve.wait_ge(S("forget_abs"), 1)
            link(V.tensor_scalar(flog[:, 2, :], flog[:, 2, :], 0.0, None, ALU.min))
            link(V.memset(flog[:, 3, :], 1.0))
            dve.wait_ge(S("forget_exp"), 1)
            V.tensor_scalar(flog[:, 1, :], flog[:, 1, :], 1.0, None, ALU.add).then_inc(S("forget_one"), 1)
            dve.wait_ge(S("forget_ln"), 1)
            link(V.tensor_tensor(flog[:, 2, :], flog[:, 2, :], flog[:, 1, :], ALU.subtract))
            V.tensor_tensor_scan(cum, flog[:, 3, :], flog[:, 2, :], 0.0, ALU.mult, ALU.add).then_inc(S("cum_ready"), 1)
            dve.wait_ge(S("cum_ready"), 1)
            V.tensor_scalar(ncum, cum, -1.0, None, ALU.mult).then_inc(S("cum_ready"), 1)
            for i in range(1, 4):
                for j in range(RING):
                    split_low(dve, "fox_in", i, j)
            F, T1 = TILES["fox_in"], TILES["fox_attn"]
            for step in range(FOX_HEADS // 2 + 1):
                if step < FOX_HEADS // 2:
                    for a in range(2):
                        t = T1 + fox_tile(step, a)
                        wait_tile(dve, t)
                        for qt, (c0, nk) in enumerate(((0, P), (P, SEQ))):
                            V.tensor_reduce(small[:, 32 + 2 * a + qt:33 + 2 * a + qt], bank(t)[:, c0:c0 + nk], AX.X, ALU.max,
                                            negate=True).then_inc(S("fox_max"), 1)
                    for a in range(2):
                        wait_evac(dve, T1 + fox_tile(step, a))
                        link(V.reciprocal(small[:, 40 + 2 * a:42 + 2 * a], small[:, 36 + 2 * a:38 + 2 * a]))
                        link(V.tensor_scalar(fexp[:, a, 0:P], fexp[:, a, 0:P], small[:, 40 + 2 * a:41 + 2 * a], None, ALU.mult))
                        V.tensor_scalar(fexp[:, a, P:384], fexp[:, a, P:384], small[:, 41 + 2 * a:42 + 2 * a], None,
                                        ALU.mult).then_inc(S("fox_probs"), 1)
                if step >= 1:
                    g = step - 1
                    t = T1 + fox_tile(g, 4)
                    wait_tile(dve, t)
                    wait_evac(dve, F + 24 + g)
                    evac(V.tensor_tensor(fgate[:, g, :], fgate[:, g, :], bank(t)[:, 0:SEQ], ALU.mult), t)

            def add_to_h(name):
                for k in range(KT):
                    t = TILES[name] + k
                    wait_tile(dve, t)
                    evac(V.tensor_tensor(h[:, k, :], h[:, k, :], bank(t)[:, 0:SEQ], ALU.add), t)

            add_to_h("fox_out")

            def experts(l):
                rms_norm(f"moe_norm_{l}", lambda k: vcol(P + VEC2["ffn"] + 8 * l + k))
                if l == 0:
                    link(V.memset(zrow[:, :], 0.0))
                link(V.memset(pad8[:, :, :], -3.0e38))
                iota = K("iota")
                bias = rowbc[:, ROW_ROUTER + NR * l:ROW_ROUTER + NR * (l + 1)]
                t = TILES[f"router_{l}"]
                wait_tile(dve, t)
                logits = bank(t)[:, 0:TT * NR].rearrange("p (t n) -> p t n", t=TT)
                V.tensor_tensor(pad8[:, :, 0:GROUPS], logits[:, :, 0:GROUPS],
                                bias[:, 0:GROUPS].unsqueeze(1).broadcast_to([P, TT, GROUPS]), ALU.add)
                evac(V.tensor_tensor(lg[:, :, :], logits, bias.unsqueeze(1).broadcast_to([P, TT, NR]), ALU.add), t)
                wait_evac(dve, t)
                for tt in range(TT):
                    last = V.max(top[:, tt, :], pad8[:, tt, :])
                link(last)
                for tt in range(TT):
                    V.max_index(topi[:, tt, :], top[:, tt, :], pad8[:, tt, :])
                link(V.tensor_scalar(rt[:, 8:10], top[:, 0:TT, 0], -1.0, None, ALU.mult))
                link(V.tensor_copy(rt[:, 16:18], topi[:, 0:TT, 0]))
                V.tensor_copy(rt[:, 8:10], rt[:, 8:10]).then_inc(S("group_max"), 1)
                link(V.tensor_tensor(onehot_g, iota[:, 0:GROUPS].unsqueeze(1).broadcast_to([P, TT, GROUPS]),
                                     rt[:, 16:18].unsqueeze(2).broadcast_to([P, TT, GROUPS]), ALU.is_equal))
                for tt in range(TT):
                    last = V.tensor_tensor(of_group[:, EPG * tt:EPG * (tt + 1), :],
                                           lg[:, tt, GROUPS:NR].rearrange("p (g e) -> p e g", g=GROUPS),
                                           onehot_g[:, tt, :].unsqueeze(1).broadcast_to([P, EPG, GROUPS]), ALU.mult)
                link(last)
                link(V.tensor_reduce(e_in[:, :, :].rearrange("p t e -> p (t e)"), of_group, AX.X, ALU.add))
                for tt in range(TT):
                    last = V.max(top[:, 2 + tt, :], e_in[:, tt, :])
                link(last)
                for tt in range(TT):
                    V.max_index(topi[:, 2 + tt, :], top[:, 2 + tt, :], e_in[:, tt, :])
                link(V.tensor_tensor(rt[:, 12:14], top[:, 2:4, 1], top[:, 2:4, 0], ALU.subtract))
                index, number = (rt[:, b:b + 4].rearrange("p (t c) -> p t c", t=TT) for b in (18, 22))
                link(V.tensor_copy(index, topi[:, 2:4, 0:2]))
                link(V.scalar_tensor_tensor(number, rt[:, 16:18].unsqueeze(2).broadcast_to([P, TT, 2]), float(EPG), index,
                                            ALU.mult, ALU.add))
                for c in range(2):
                    last = V.tensor_tensor(pick_e[:, c, :, :], iota[:, 0:E].unsqueeze(1).broadcast_to([P, TT, E]),
                                           number[:, :, c:c + 1].broadcast_to([P, TT, E]), ALU.is_equal)
                link(last)
                V.tensor_tensor(pick_e[:, 2, :, :], pick_e[:, 0, :, :], pick_e[:, 1, :, :], ALU.add).then_inc(S("choices"), 1)
                V.tensor_copy(rt[:, 12:14], rt[:, 12:14]).then_inc(S("second_gap"), 1)
                for q in (1, 3):
                    t = TILES[f"hn_{l}"] + q
                    wait_tile(dve, t)
                    evac(V.tensor_copy(hn_tok[:, q // 2, 512:1024], bank(t)[:, :]), t)
                t = TILES[f"router_{l}"] + 1
                wait_tile(dve, t)
                link(V.tensor_copy(pos[:, :, :], bank(t)[:, 0:TT * E].rearrange("p (t n) -> p t n", t=TT)))
                evac(V.tensor_copy(e_sum[:, 0, :], bank(t)[:, 2 * E:3 * E]), t)
                wait_evac(dve, t)
                counts = e_sum[:, 0, :].rearrange("p (i a) -> p a i", a=2)
                place, held = (rt[:, b:b + 4].rearrange("p (c t) -> p c t", c=2) for b in (26, 30))

                def both(v):
                    return v.unsqueeze(1).broadcast_to([P, 2, TT, E])
                need, spare = share[:, 0, :], share[:, 1, :]
                fit, first_units, more, upto = (share[:, b, :] for b in (2, 3, 4, 5))
                units = iota[:, UNIT:P:UNIT].unsqueeze(1).broadcast_to([P, PAIRS, 3])
                for a, test in ((0, ALU.is_gt), (1, ALU.is_le)):
                    last = V.tensor_tensor(over[:, PAIRS * a:PAIRS * (a + 1), :], counts[:, a, :].unsqueeze(2).broadcast_to([P, PAIRS, 3]),
                                           units, test)
                link(last)
                V.tensor_reduce(share[:, 0:2, :].rearrange("p a i -> p (a i)"), over, AX.X, ALU.add)
                link(V.tensor_tensor(by_choice[0], pick_e[:, 0:2, :, :], both(pos), ALU.mult))
                V.tensor_reduce(place, by_choice[0], AX.X, ALU.add)
                link(V.scalar_tensor_tensor(fit, need, 1.0, spare, ALU.add, ALU.is_le))
                link(V.scalar_tensor_tensor(first_units, need, -1.0, fit, ALU.add, ALU.mult))
                link(V.tensor_scalar(first_units, first_units, float(UNIT), float(SLOTS), ALU.mult, ALU.add))
                rows_of, first_key = (room[:, b, :].rearrange("p (i a) -> p a i", a=2) for b in range(2))
                V.tensor_copy(rows_of[:, 0, :], first_units)
                V.tensor_scalar(rows_of[:, 1, :], first_units, -1.0, float(P), ALU.mult, ALU.add)
                V.tensor_scalar(first_key[:, 0, :], iota[:, 0:PAIRS], float(P), None, ALU.mult)
                link(V.scalar_tensor_tensor(first_key[:, 1, :], iota[:, 0:PAIRS], float(P), first_units, ALU.mult, ALU.add))
                V.tensor_tensor(by_choice[1], pick_e[:, 0:2, :, :], both(room[:, 0:1, :].broadcast_to([P, TT, E])), ALU.mult)
                link(V.tensor_tensor(key_first, pos, room[:, 1:2, :].broadcast_to([P, TT, E]), ALU.add))
                V.tensor_tensor(by_choice[2], pick_e[:, 0:2, :, :], both(key_first), ALU.mult)
                link(V.tensor_reduce(held, by_choice[1], AX.X, ALU.add))
                V.tensor_reduce(rel[:, :, :], by_choice[2], AX.X, ALU.add)
                for n in range(1, FURTHER + 1):
                    last = V.scalar_tensor_tensor(gone[:, :, n - 1], rt[:, 30:34], float(n), rt[:, 26:30], ALU.mult, ALU.is_le)
                link(last)
                link(V.tensor_reduce(rounds.rearrange("p c t -> p (c t)"), gone, AX.X, ALU.add))
                link(V.scalar_tensor_tensor(rel_more[:, :, :], held, -float(ROUND_KEY), rounds, ALU.add, ALU.mult))
                link(V.tensor_tensor(rel[:, :, :], rel[:, :, :], rel_more[:, :, :], ALU.subtract))

                def build_pick(keys, plain, weighted, linked, plain_done, weighted_done):
                    for tt in range(TT):
                        V.tensor_scalar(is_first[:, tt, :], iota, keys[:, 0, tt:tt + 1], None, ALU.is_equal)
                        last = V.tensor_scalar(is_second[:, tt, :], iota, keys[:, 1, tt:tt + 1], None, ALU.is_equal)
                    linked(last)
                    V.tensor_tensor(plain, is_first, is_second, ALU.add).then_inc(plain_done, 1)
                    weigh(weighted, linked, weighted_done) if weighted is not None else None

                def weigh(weighted, linked, weighted_done):
                    for tt in range(TT):
                        last = V.tensor_scalar(first_w[:, tt, :], is_first[:, tt, :], rt[:, 36 + tt:37 + tt], None, ALU.mult)
                    linked(last)
                    for tt in range(TT):
                        last = V.scalar_tensor_tensor(weighted[:, tt, :], is_second[:, tt, :], rt[:, 38 + tt:39 + tt],
                                                      first_w[:, tt, :], ALU.mult, ALU.add)
                    last.then_inc(weighted_done, 1)

                build_pick(rel, pick, None, link, S("pick_ready"), None)
                link(V.tensor_scalar(rel[:, :, :], rel[:, :, :], float(-P), None, ALU.add))
                dve.wait_ge(S("group_exp"), TT * (l + 1))
                dve.wait_ge(S("second_exp"), l + 1)
                link(V.tensor_scalar(rt[:, 34:36], rt[:, 14:16], 1.0, None, ALU.add))
                link(V.tensor_tensor(rt[:, 34:36], rt[:, 34:36], rt[:, 10:12], ALU.mult))
                link(V.reciprocal(rt[:, 36:38], rt[:, 34:36]))
                link(V.tensor_tensor(rt[:, 38:40], rt[:, 36:38], rt[:, 14:16], ALU.mult))
                weigh(pick_w, link, S("pick_w_ready"))
                crowd = e_sum[:, 1, 0:PAIRS]
                link(V.tensor_tensor(crowd, counts[:, 0, :], counts[:, 1, :], ALU.max))
                link(V.tensor_scalar(more, crowd, float(SLOTS), None, ALU.is_gt))
                for n in range(2, FURTHER + 1):
                    link(V.scalar_tensor_tensor(more, crowd, float(n * SLOTS), more, ALU.is_gt, ALU.add))
                link(V.tensor_scalar(fit, fit, -1.0, 1.0, ALU.mult, ALU.add))
                link(V.tensor_tensor(more, more, fit, ALU.mult))
                link(V.tensor_tensor_scan(upto, more, zrow[:, 0:PAIRS], 0.0, ALU.add, ALU.add))
                link(V.tensor_tensor(upto, upto, more, ALU.subtract))
                V.tensor_copy(more_i[:, 0:PAIRS], more)
                V.tensor_copy(more_i[:, PAIRS:2 * PAIRS], upto)
                V.tensor_copy(more_i[:, 2 * PAIRS:3 * PAIRS], first_units).then_inc(S(f"more_known_{l}"), 1)
                dve.wait_ge(S(f"more_known_{l}"), 1)
                free = [bank(TILES[f"combine_{l}"] + 4 + q) for q in range(4)]

                def make_hidden(done):
                    V.tensor_tensor(hid, sil, free[1][:, :], ALU.mult).then_inc(done, 1)

                def take_xg(rows, done):
                    V.tensor_copy(rows[:, 4:8, :], free[1][:, :].rearrange("p (k n) -> p k n", k=4)).then_inc(done, 1)

                def take_pick_wT(done):
                    V.tensor_copy(pick_wT, free[3][:, 0:SEQ].rearrange("p (t n) -> p t n", t=TT)).then_inc(done, 1)

                def take_y(done):
                    V.tensor_copy(y_sb[:, 512:1024], free[3][:, :]).then_inc(done, 1)

                dve.wait_ge(S("gathered"), 2 * (PAIRS + 1) * l + 2)
                take_xg(xg, S("xg_dve"))
                loop_chain, more_chain = S(f"pick_chain_{l}"), S(f"more_chain_{l}")
                with dve.Fori(0, PAIRS) as i:
                    n = PAIRS * l + i
                    at = [0]

                    def linked(ins):
                        at[0] += 1
                        ins.then_inc(loop_chain, 1)
                        dve.wait_ge(loop_chain, 4 * i + at[0])
                    n_more = dve.value_load(more_i[0:1, ds(i, 1)], min_val=0, max_val=FURTHER)
                    V.tensor_scalar(rel_more[:, :, :], rel[:, :, :], float(P - ROUND_KEY), None, ALU.add).then_inc(loop_chain, 1)
                    at[0] += 1
                    with dve.If(n_more > 0):
                        before = dve.value_load(more_i[0:1, ds(i + PAIRS, 1)], min_val=0, max_val=2 * SEQ // SLOTS)
                        with dve.Fori(0, FURTHER) as r:
                            with dve.If(r < n_more):
                                c = before + r
                                more_at = [0]

                                def linked_more(ins):
                                    more_at[0] += 1
                                    ins.then_inc(more_chain, 1)
                                    dve.wait_ge(more_chain, 3 * c + more_at[0])
                                dve.wait_ge(loop_chain, 4 * i + 1)
                                dve.wait_ge(S("pick_w_ready"), (PAIRS + 1) * l + i + 1)
                                build_pick(rel_more, pick_more, pick_w_more, linked_more, S(f"more_pick_ready_{l}"),
                                           S(f"more_pick_w_ready_{l}"))
                                linked_more(V.tensor_scalar(rel_more[:, :, :], rel_more[:, :, :], float(-ROUND_KEY), None, ALU.add))
                                dve.wait_ge(S(f"more_gathered_{l}"), c + 1)
                                take_xg(xg_more, S(f"more_xg_dve_{l}"))
                                dve.wait_ge(S(f"more_up_{l}"), c + 1)
                                dve.wait_ge(S(f"more_silu_{l}"), c + 1)
                                make_hidden(S(f"more_hidden_{l}"))
                                dve.wait_ge(S(f"more_pick_turned_{l}"), c + 1)
                                take_pick_wT(S(f"more_pick_wT_{l}"))
                                dve.wait_ge(S(f"more_down_{l}"), c + 1)
                                take_y(S(f"more_y_dve_{l}"))
                    dve.wait_ge(S("pick_w_ready"), (PAIRS + 1) * l + i + 1)
                    build_pick(rel, pick, None, linked, S("pick_ready"), None)
                    linked(V.tensor_scalar(rel[:, :, :], rel[:, :, :], float(-P), None, ALU.add))
                    dve.wait_ge(S("silu_e"), n + 1)
                    dve.wait_ge(expert_used, 4 * n + 2)
                    make_hidden(S("hidden_e"))
                    dve.wait_ge(S("pick_turned"), n + 1)
                    take_pick_wT(S("pick_wT_ready"))
                    dve.wait_ge(S("gathered"), 2 * ((PAIRS + 1) * l + i + 1) + 2)
                    take_xg(xg, S("xg_dve"))
                    weigh(pick_w, linked, S("pick_w_ready"))
                    dve.wait_ge(expert_used, 4 * n + 4)
                    take_y(S("y_dve"))
                for q in (1, 3):
                    t = TILES[f"combine_{l}"] + q
                    wait_tile(dve, t)
                    evac(V.tensor_copy(h[:, 2 * q:2 * q + 2, :], bank(t)[:, :].rearrange("p (k n) -> p k n", k=2)), t)
                for q in range(4):
                    wait_evac(dve, TILES[f"combine_{l}"] + q)

            for n in range(8):
                wait_evac(dve, TILES["fox_out"] + n)
            experts(0)
            split_low(dve, "ret_in", 0, 0)
            rms_norm("ret_norm", lambda k: vcol(P + VEC2["mix"] + 8 + k))
            low_of_u("ret_norm", "second")
            for j in (1, 2, 3):
                split_low(dve, "ret_in", 0, j)
            for j in range(RING):
                split_low(dve, "ret_in", 1, j)
            R = TILES["ret_in"]
            for qk in range(2):
                for n in range(8):
                    wait_evac(dve, R + 8 * qk + n)
                raw = rraw[:, 8 * qk:8 * qk + 8, :].rearrange("p (a s) n -> p a s n", s=2)
                dst = rqk[:, 8 * qk:8 * qk + 8, :].rearrange("p (a s) n -> p a s n", s=2)
                cos, sin = over_tiles(K("ret_cos"), 4), over_tiles(K("ret_sin"), 4)
                tmp = rtmp[:, 0:4, :]
                link(V.tensor_tensor(dst[:, :, 0, :], raw[:, :, 0, :], cos, ALU.mult))
                link(V.tensor_tensor(tmp, raw[:, :, 1, :], sin, ALU.mult))
                link(V.tensor_tensor(dst[:, :, 0, :], dst[:, :, 0, :], tmp, ALU.subtract))
                link(V.tensor_tensor(dst[:, :, 1, :], raw[:, :, 1, :], cos, ALU.mult))
                link(V.tensor_tensor(tmp, raw[:, :, 0, :], sin, ALU.mult))
                V.tensor_tensor(dst[:, :, 1, :], dst[:, :, 1, :], tmp, ALU.add).then_inc(S("rotated"), 1)
                dve.wait_ge(S("rotated"), qk + 1)
                for i in ((2,), (3, 4, 5))[qk]:
                    for j in range(RING):
                        split_low(dve, "ret_in", i, j)
            dve.wait_ge(S("in_decay"), 16)
            for hd in range(RET_HEADS):
                t = TILES["ret_scores"] + hd
                wait_tile(dve, t)
                evac(V.tensor_tensor(r_s[:, hd, :], bank(t)[:, 0:384], decay[:, hd, :], ALU.mult), t)
            for hd in range(RET_HEADS):
                t = TILES["gn_mean"] + hd
                wait_tile(dve, t)
                o = ro[:, 4 * hd:4 * hd + 4, :]
                evac(V.tensor_tensor(o, o, over_tiles(bank(t)[:, 0:SEQ], 4), ALU.subtract), t)
            for hd in range(RET_HEADS):
                wait_evac(dve, TILES["ret_scores"] + hd)
                wait_evac(dve, TILES["gn_mean"] + hd)
                inv_std(gn_rstd[:, hd, :], TILES["gn_var"] + hd)
                o = ro[:, 4 * hd:4 * hd + 4, :]
                link(V.tensor_tensor(o, o, over_tiles(gn_rstd[:, hd, :], 4), ALU.mult))
                for n in range(4 * hd, 4 * hd + 4):
                    wait_evac(dve, R + 32 + n)
                    V.scalar_tensor_tensor(rgate[:, n, :], ro[:, n, :], vcol(VEC1["gn"] + n), rgate[:, n, :],
                                           ALU.mult, ALU.mult).then_inc(S("ret_gated"), 1)
            add_to_h("ret_out")
            for n in range(8):
                wait_evac(dve, TILES["ret_out"] + n)
            experts(1)
            rms_norm("final_norm", lambda k: vcol(P + VEC2["final"] + k))
            for q in (1, 3):
                t = TILES["final"] + q
                wait_tile(dve, t)
                V.tensor_copy(out_tok[:, q // 2, 512:1024], bank(t)[:, :]).then_inc(S("out_dve"), 1)


        @block.gpsimd
        def _(pool):
            for c in range(2):
                other = slice((1 - c) * DIFF_QK, (2 - c) * DIFF_QK)
                nc.gpsimd.memset(qrot[c][other, :, :], 0.0).then_inc(S("q_zero"), 1)
            for l in range(DEPTH):
                name = f"mod2_{l}"
                scale, shift = norm_affine(name)
                for k in range(KT):
                    pool.wait_ge(S("standardized"), KT * NORMS.index(name) + k + 1)
                    nc.gpsimd.tensor_scalar(u[:, k, :], centered[:, k, :], scale(k), shift(k), ALU.mult, ALU.add).then_inc(
                        S(f"{name}_out"), 1)
            wait_tile(pool, TILES["w2_1"] + 7)
            for a in range(2):
                for x in (fq[a], fk[a]):
                    nc.gpsimd.memset(x[PAD[a]:PAD[a] + FOX_DIM, :, :], 0.0).then_inc(S("fox_pads"), 1)
            pool.wait_ge(S("fox_pads"), 4)
            for a in range(2):
                ones_k, ones_q = PAD[a], PAD[a] + 32
                nc.gpsimd.memset(fk[a][ones_k:ones_k + 1, :, :], 1.0).then_inc(S("fox_pads"), 1)
                nc.gpsimd.memset(fq[a][ones_q:ones_q + 1, :, :], 1.0).then_inc(S("fox_pads"), 1)
            pool.wait_ge(S("fox_pads"), 8)
            pool.wait_ge(S("cum_ready"), 2)
            for a in range(2):
                for dst, src in ((fq[a][PAD[a]:PAD[a] + 1], cum), (fk[a][PAD[a] + 32:PAD[a] + 33], ncum)):
                    pool.dma_start(dst, src[a:FOX_HEADS:2, :]).then_inc(S("fox_bias_rows"), 16)


def fox_tile(pair, n):
    if n < 2:
        return (0 if pair == 0 else 2 + 5 * (pair - 1)) + n
    return (2 + 5 * pair) + (2 if pair + 1 < FOX_HEADS // 2 else 0) + n - 2


def constants():
    f = np.float32
    c = np.zeros((P, N_CONST), f)

    def put(name, v):
        at, n = CONSTS[name]
        c[:, at:at + n] = v
    p = np.arange(P)
    put("ident", np.eye(P))
    put("ones", 1.0)
    put("mean_d", 1.0 / D)
    put("mean_v", 1.0 / P)
    put("mean_gn", 1.0 / (RET_V_TILES * P))
    swap = np.zeros((P, P), f)
    for m in range(P):
        if m % 32 < 16:
            swap[m + 16, m] = -1.0
        else:
            swap[m - 16, m] = 1.0
    put("swap", swap)
    put("causal", np.where(p[None, :] <= p[:, None], 0.0, -1e30))
    put("before", (p[:, None] < p[None, :]).astype(f))
    put("iota", np.broadcast_to(p.astype(f), (P, P)))
    put("fold", np.tile(np.eye(32, 2), (4, 1)))
    put("eps", np.array([[LN_EPS, SUBLN_EPS]], f))
    n = np.arange(SEQ)
    inv = (f(10000.0) ** (-np.arange(16, dtype=f) / f(16))).astype(f)
    where = np.where((p % 64 < 32)[:, None], (n // GRID_W)[None, :], (n % GRID_W)[None, :]).astype(f)
    ang = where * inv[p % 16][:, None]
    put("rope_cos", np.cos(ang))
    put("rope_sin", np.sin(ang))
    inv = (f(1.0) / (f(10000.0) ** np.linspace(0.0, 1.0, P, dtype=f))).astype(f)
    ang = n[None, :].astype(f) * inv[:, None]
    put("ret_cos", np.cos(ang))
    put("ret_sin", np.sin(ang))
    d = np.zeros((P, N_DFT), np.float64)
    th = 2 * np.pi * np.outer(p, p) / P
    d[:, 0:P], d[:, P:2 * P] = np.cos(th), np.sin(th)
    norm = 1.0 / math.sqrt(SEQ * P)
    for tt in range(TT):
        th = 2 * np.pi * (np.outer(p + tt * P, n) % SEQ) / SEQ
        d[:, 2 * P + tt * SEQ:2 * P + (tt + 1) * SEQ] = norm * np.cos(th)
        d[:, 2 * P + (2 + tt) * SEQ:2 * P + (3 + tt) * SEQ] = -norm * np.sin(th)
    g = np.zeros((P, RET_HEADS, SEQ + P), np.float64)
    for hd in range(RET_HEADS):
        log_g = math.log(1.0 - 2.0 ** (-5.0 - hd))
        r = n[None, :] - p[:, None]
        g[:, hd, 0:SEQ] = np.where(r >= 0, np.exp(log_g * np.maximum(r, 0)), 0.0)
        r = p[None, :] - p[:, None]
        g[:, hd, SEQ:] = np.where(r >= 0, np.exp(log_g * np.maximum(r, 0)), 0.0)
    return c, d.astype(f), g.reshape(P, N_DECAY).astype(f)


_DIRECT = ["x", "ctx", "ada_w", "mlp_w1", "mlp_w2", "w_in", "w_out_mix", "w_out_fourier", "fox_w_in_2", "fox_b_f_2",
           "fox_w_out_2", "ret_w_in_2", "ret_w_out_2", "expert_w_gu_2", "expert_w_down_2"]


def layout(inputs):
    get = {k: np.asarray(v) for k, v in inputs.items()}
    arrays = {k: np.ascontiguousarray(get[k]) for k in _DIRECT}
    arrays["vec1"] = np.concatenate([get[k].reshape(-1, P) for k in ("c", "c_ctx", "ada_b", "ret_gn_gain_2")])
    arrays["vec2"] = np.concatenate([get[k].reshape(-1, P) for k in
                                     ("ln_g", "ln_b", "norm_mix_2", "norm_ffn_2", "norm_final_2", "subln_g", "conv_w")])
    arrays["rows"] = np.concatenate([get["lambda_qk"].reshape(1, -1)] + [
        get[k][l].reshape(1, -1) for l in range(DEPTH) for k in ("router_group_b_2", "router_expert_b_2")], axis=1)
    arrays["router_w"] = np.concatenate([get["router_group_w_2"], get["router_expert_w_2"]], axis=2)
    arrays["consts"], arrays["dft"], arrays["decay"] = constants()
    return arrays


def declare(nc, arrays):
    A = {k: nc.dram_tensor(f"in_{k}", v.shape, mybir.dt.from_np(v.dtype), kind="ExternalInput").ap()
         for k, v in arrays.items()}
    return A, nc.dram_tensor("out_0", (1, SEQ, D), mybir.dt.float32, kind="ExternalOutput").ap()


def kernel(**inputs):
    import concourse.bacc as bacc
    from concourse.bass_utils import run_bass_kernel_spmd as run
    nc = bacc.Bacc("TRN2", target_bir_lowering=False, num_devices=1)
    arrays = layout(inputs)
    A, out = declare(nc, arrays)
    build(nc, A, out)
    r = run(nc, [{f"in_{k}": v for k, v in arrays.items()}], core_ids=[0])
    return r.results[0]["out_0"]
```
